# Optimizing a Trainium2 kernel written in Bass

```python
import math
import jax
import jax.numpy as jnp
from jax import lax
import numpy as np

D_MODEL = 1024
BATCH = 1
SEQ = 512
DEPTH = 2

GRID_W = 64
CTX_LEN = 256
NORM_EPS = 1e-6
ROPE_BASE = 10000.0
RET_HEADS = D_MODEL // 256
RET_DK = 64
RET_DV = 2 * RET_DK
RET_CHUNK = 128
DIFF_HEADS = D_MODEL // 256
DIFF_DH = 64
DIFF_DV = 2 * DIFF_DH
Q_BLOCK = 128
POOL_WINDOWS = (2, 4, 8, 16)
POOL_GROUP = D_MODEL // len(POOL_WINDOWS)
N_EXPERTS = 16
N_EXPERT_GROUPS = 4
EXPERTS_PER_GROUP = N_EXPERTS // N_EXPERT_GROUPS
TOP_K = 2
D_EXPERT = 512
RET_Q_W = RET_HEADS * RET_DK
DIFF_Q_W = DIFF_HEADS * 2 * DIFF_DH
RET_G_W = RET_HEADS * RET_DV
RET_K_W = RET_HEADS * RET_DK
RET_V_W = RET_HEADS * RET_DV
DIFF_K_W = DIFF_HEADS * 2 * DIFF_DH
DIFF_V_W = DIFF_HEADS * DIFF_DV
QG_W = RET_Q_W + DIFF_Q_W + RET_G_W
KV_W = RET_K_W + RET_V_W + DIFF_K_W + DIFF_V_W
IN_W = QG_W + KV_W
QG_SPLITS = (RET_Q_W, RET_Q_W + DIFF_Q_W)
KV_SPLITS = (RET_K_W, RET_K_W + RET_V_W, RET_K_W + RET_V_W + DIFF_K_W)
MIX_W = RET_HEADS * RET_DV + DIFF_HEADS * DIFF_DV
N_EVEN = (DEPTH + 1) // 2
N_ODD = DEPTH // 2

kernel_name = 'hybrid_retention_diffattn_pool_moe_dit'

def rms_norm(x, w):
    xf = x.astype(jnp.float32)
    y = xf * lax.rsqrt(jnp.mean(xf * xf, axis=-1, keepdims=True) + NORM_EPS)
    return (y * w.astype(jnp.float32)).astype(x.dtype)

def head_rms(o):
    of = o.astype(jnp.float32)
    return of * lax.rsqrt(jnp.mean(of * of, axis=-1, keepdims=True) + NORM_EPS)

def modulate(h, shift, scale):
    return h * (1 + scale) + shift

def rope_1d(x, pos):
    half = x.shape[-1] // 2
    inv = ROPE_BASE ** (-jnp.arange(half, dtype=jnp.float32) / half)
    ang = pos.astype(jnp.float32)[:, None] * inv[None, :]
    cos = jnp.cos(ang).astype(x.dtype)
    sin = jnp.sin(ang).astype(x.dtype)
    x1, x2 = x[..., :half], x[..., half:]
    return jnp.concatenate([x1 * cos - x2 * sin, x1 * sin + x2 * cos], axis=-1)

def rope_2d(x, row, col):
    h = x.shape[-1] // 2
    return jnp.concatenate([rope_1d(x[..., :h], row), rope_1d(x[..., h:], col)], axis=-1)

def to_heads(a, n_heads):
    b, t, _ = a.shape
    return a.reshape(b, t, n_heads, -1).transpose(0, 2, 1, 3)

def to_pair_heads(a):
    b, t, _ = a.shape
    return a.reshape(b, t, DIFF_HEADS, 2, DIFF_DH).transpose(0, 2, 3, 1, 4)

def from_heads(o):
    b, h, t, d = o.shape
    return o.transpose(0, 2, 1, 3).reshape(b, t, h * d)

def retention_chunked(q, k, v, log_g, s0):
    b, h, t, dk = q.shape
    dv = v.shape[-1]
    n = t // RET_CHUNK
    qc = q.reshape(b, h, n, RET_CHUNK, dk)
    kc = k.reshape(b, h, n, RET_CHUNK, dk)
    vc = v.reshape(b, h, n, RET_CHUNK, dv)
    pos = jnp.arange(RET_CHUNK, dtype=jnp.float32)
    lg = log_g[:, None]
    gap = pos[:, None] - pos[None, :]
    mask = jnp.where(gap >= 0, jnp.exp(lg[:, :, None] * jnp.maximum(gap, 0.0)[None]), 0.0)
    scores = jnp.einsum('bhnid,bhnjd->bhnij', qc, kc) * mask[None, :, None]
    o_intra = jnp.einsum('bhnij,bhnje->bhnie', scores, vc)
    k_dec = jnp.exp(lg * (RET_CHUNK - 1 - pos))
    q_dec = jnp.exp(lg * (pos + 1))
    c_dec = jnp.exp(log_g * RET_CHUNK)
    kv = jnp.einsum('bhnjd,bhnje->nbhde', kc * k_dec[None, :, None, :, None], vc)

    def step(s, kv_i):
        return c_dec[None, :, None, None] * s + kv_i, s

    s_final, s_in = lax.scan(step, s0, kv)
    o_cross = jnp.einsum('bhnid,nbhde->bhnie', qc * q_dec[None, :, None, :, None], s_in)
    return (o_intra + o_cross).reshape(b, h, t, dv), s_final

def retention_state(k, v, log_g):
    t = k.shape[2]
    dec = jnp.exp(log_g[:, None] * (t - 1 - jnp.arange(t, dtype=jnp.float32)))
    return jnp.einsum('bhtd,bhte->bhde', k * dec[None, :, :, None], v)

def bidir_retention(q, k, v, log_decay, s0_f, s0_b):
    o_f, s_f = retention_chunked(q, k, v, log_decay[0], s0_f)
    o_b, s_b = retention_chunked(jnp.flip(q, 2), jnp.flip(k, 2), jnp.flip(v, 2), log_decay[1], s0_b)
    return o_f + jnp.flip(o_b, 2), s_f, s_b

def diff_softmax_pair(q, k, v, lam):
    s = jnp.einsum('bhcqd,bhckd->bhcqk', q, k).astype(jnp.float32) * (DIFF_DH ** -0.5)
    p = jax.nn.softmax(s, axis=-1)
    a = p[:, :, 0] - lam * p[:, :, 1]
    return jnp.einsum('bhqk,bhkd->bhqd', a.astype(v.dtype), v)

def diff_attention_blocked(q, k_all, v_all, lam):
    b, h, _, t, dh = q.shape
    nb = t // Q_BLOCK
    qb = q.reshape(b, h, 2, nb, Q_BLOCK, dh).transpose(3, 0, 1, 2, 4, 5)
    ob = lax.map(lambda blk: diff_softmax_pair(blk, k_all, v_all, lam), qb)
    return ob.transpose(1, 2, 0, 3, 4).reshape(b, h, t, -1)

def even_mixer(hx, hc, w_in, w_out, log_decay, lam_vec, subln_w, layer_idx, row, col, ctx_out):
    b = hx.shape[0]
    f32 = jnp.float32
    lam_init = 0.8 - 0.6 * math.exp(-0.3 * layer_idx)
    lv = lam_vec.astype(f32)
    lam = jnp.exp(jnp.sum(lv[0] * lv[1])) - jnp.exp(jnp.sum(lv[2] * lv[3])) + lam_init
    ld = log_decay.astype(f32)
    k_scale = RET_DK ** -0.5

    xq, xdq, xg = jnp.split(hx @ w_in[:, :QG_W], QG_SPLITS, axis=-1)
    xk, xv, xdk, xdv = jnp.split(hx @ w_in[:, QG_W:], KV_SPLITS, axis=-1)
    ck, cv, cdk, cdv = jnp.split(hc @ w_in[:, QG_W:], KV_SPLITS, axis=-1)

    rq = rope_2d(to_heads(xq, RET_HEADS), row, col).astype(f32)
    rk = (rope_2d(to_heads(xk, RET_HEADS), row, col) * k_scale).astype(f32)
    rv = to_heads(xv, RET_HEADS).astype(f32)
    crk = (to_heads(ck, RET_HEADS) * k_scale).astype(f32)
    crv = to_heads(cv, RET_HEADS).astype(f32)
    if ctx_out:
        zeros = jnp.zeros((b, RET_HEADS, RET_DK, RET_DV), f32)
        cq, cdq, cg = jnp.split(hc @ w_in[:, :QG_W], QG_SPLITS, axis=-1)
        c_ret, s_f, s_b = bidir_retention(to_heads(cq, RET_HEADS).astype(f32), crk, crv, ld, zeros, zeros)
    else:
        s_f = retention_state(crk, crv, ld[0])
        s_b = retention_state(jnp.flip(crk, 2), jnp.flip(crv, 2), ld[1])
    x_ret, _, _ = bidir_retention(rq, rk, rv, ld, s_f, s_b)

    dq = rope_2d(to_pair_heads(xdq), row, col)
    dk = rope_2d(to_pair_heads(xdk), row, col)
    dv = to_heads(xdv, DIFF_HEADS)
    cdk_h = to_pair_heads(cdk)
    cdv_h = to_heads(cdv, DIFF_HEADS)
    k_all = jnp.concatenate([cdk_h, dk], axis=3)
    v_all = jnp.concatenate([cdv_h, dv], axis=2)
    x_diff = diff_attention_blocked(dq, k_all, v_all, lam)

    def merge(o_ret, gate, o_diff):
        ret = from_heads(head_rms(o_ret)).astype(gate.dtype) * jax.nn.silu(gate)
        dif = from_heads(head_rms(o_diff) * subln_w.astype(f32) * (1.0 - lam_init)).astype(gate.dtype)
        return jnp.concatenate([ret, dif], axis=-1) @ w_out

    out_x = merge(x_ret, xg, x_diff)
    out_c = None
    if ctx_out:
        c_diff = diff_softmax_pair(to_pair_heads(cdq), cdk_h, cdv_h, lam)
        out_c = merge(c_ret, cg, c_diff)
    return out_x, out_c

def pool_mixer(h, pool_w, pool_scale):
    b, t, d = h.shape
    hf = h.astype(jnp.float32)
    cs = jnp.concatenate([jnp.zeros((b, 1, d), jnp.float32), jnp.cumsum(hf, axis=1)], axis=1)
    pos = jnp.arange(t)
    groups = []
    for gi, w in enumerate(POOL_WINDOWS):
        left = w // 2
        right = w - 1 - left
        lo = jnp.clip(pos - left, 0, t)
        hi = jnp.clip(pos + right + 1, 0, t)
        sl = cs[:, :, gi * POOL_GROUP:(gi + 1) * POOL_GROUP]
        mean = (sl[:, hi] - sl[:, lo]) / (hi - lo).astype(jnp.float32)[None, :, None]
        groups.append(mean - hf[:, :, gi * POOL_GROUP:(gi + 1) * POOL_GROUP])
    pooled = jnp.stack(groups, axis=2).astype(h.dtype)
    mixed = jnp.einsum('btgc,gcd->btgd', pooled, pool_w).reshape(b, t, d)
    return mixed * pool_scale

def moe_route(flat, router_w, router_b):
    n = flat.shape[0]
    s = jax.nn.sigmoid((flat @ router_w).astype(jnp.float32))
    biased = s + router_b.astype(jnp.float32)
    grp_score = jnp.sum(lax.top_k(biased.reshape(n, N_EXPERT_GROUPS, EXPERTS_PER_GROUP), TOP_K)[0], axis=-1)
    g_sel = jnp.argmax(grp_score, axis=-1)
    in_group = (jnp.arange(N_EXPERTS) // EXPERTS_PER_GROUP)[None, :] == g_sel[:, None]
    _, idx = lax.top_k(jnp.where(in_group, biased, -jnp.inf), TOP_K)
    w = jnp.take_along_axis(s, idx, axis=-1)
    w = w / jnp.sum(w, axis=-1, keepdims=True)
    return jnp.sum(jax.nn.one_hot(idx, N_EXPERTS, dtype=jnp.float32) * w[..., None], axis=1)

def moe_ffn(h, router_w, router_b, w_gate, w_up, w_down):
    b, t, d = h.shape
    flat = h.reshape(-1, d)
    combine = moe_route(flat, router_w, router_b)
    out = jnp.zeros(flat.shape, jnp.float32)
    for e in range(N_EXPERTS):
        hid = jax.nn.silu(flat @ w_gate[e]) * (flat @ w_up[e])
        out = out + combine[:, e:e + 1] * (hid @ w_down[e]).astype(jnp.float32)
    return out.astype(h.dtype).reshape(b, t, d)

def setup_inputs(seed: int = 0) -> dict:
    key = jax.random.key(seed)
    ks = jax.random.split(key, 21)
    f32 = jnp.float32

    def nrm(k, shape, scale):
        return jax.random.normal(k, shape, f32) * scale

    base_decay = jnp.log1p(-(2.0 ** (-5.0 - jnp.arange(RET_HEADS, dtype=f32))))
    return {
        'x': nrm(ks[0], (BATCH, SEQ, D_MODEL), 1.0),
        'c': nrm(ks[1], (BATCH, D_MODEL), 1.0),
        'ctx': nrm(ks[2], (BATCH, CTX_LEN, D_MODEL), 1.0),
        'c_ctx': nrm(ks[3], (D_MODEL,), 1.0),
        'ada_w': nrm(ks[4], (DEPTH, D_MODEL, 6 * D_MODEL), 0.5 * D_MODEL ** -0.5),
        'ada_b': nrm(ks[5], (DEPTH, 6 * D_MODEL), 0.02),
        'norm_mix_w': 1.0 + nrm(ks[6], (DEPTH, D_MODEL), 0.01),
        'norm_ffn_w': 1.0 + nrm(ks[7], (DEPTH, D_MODEL), 0.01),
        'w_in': nrm(ks[8], (N_EVEN, D_MODEL, IN_W), D_MODEL ** -0.5),
        'w_out': nrm(ks[9], (N_EVEN, MIX_W, D_MODEL), MIX_W ** -0.5),
        'ret_log_decay': base_decay[None, None, :] * (1.0 + nrm(ks[10], (N_EVEN, 2, RET_HEADS), 0.05)),
        'diff_lambda': nrm(ks[11], (N_EVEN, 4, DIFF_DH), 0.1),
        'diff_subln_w': 1.0 + nrm(ks[12], (N_EVEN, DIFF_DV), 0.01),
        'pool_w': nrm(ks[13], (N_ODD, len(POOL_WINDOWS), POOL_GROUP, POOL_GROUP), POOL_GROUP ** -0.5),
        'pool_scale': 1.0 + nrm(ks[14], (N_ODD, D_MODEL), 0.1),
        'router_w': nrm(ks[15], (D_MODEL, N_EXPERTS), D_MODEL ** -0.5),
        'router_b': nrm(ks[16], (N_EXPERTS,), 0.01),
        'moe_w_gate': nrm(ks[17], (DEPTH, N_EXPERTS, D_MODEL, D_EXPERT), D_MODEL ** -0.5),
        'moe_w_up': nrm(ks[18], (DEPTH, N_EXPERTS, D_MODEL, D_EXPERT), D_MODEL ** -0.5),
        'moe_w_down': nrm(ks[19], (DEPTH, N_EXPERTS, D_EXPERT, D_MODEL), D_EXPERT ** -0.5),
        'final_norm_w': 1.0 + nrm(ks[20], (D_MODEL,), 0.01),
    }

def reference(x, c, ctx, c_ctx, ada_w, ada_b, norm_mix_w, norm_ffn_w, w_in, w_out, ret_log_decay,
              diff_lambda, diff_subln_w, pool_w, pool_scale, router_w, router_b, moe_w_gate, moe_w_up,
              moe_w_down, final_norm_w):
    t = x.shape[1]
    rows = t // GRID_W
    row = jnp.repeat(jnp.arange(rows), GRID_W)
    col = jnp.tile(jnp.arange(GRID_W), rows)
    silu_c = jax.nn.silu(c)
    silu_cc = jax.nn.silu(c_ctx)
    cx = ctx
    for l in range(DEPTH):
        even = l % 2 == 0
        li = l // 2
        ctx_after = any(j % 2 == 0 for j in range(l + 1, DEPTH))
        ctx_in = even or ctx_after
        mod = (silu_c @ ada_w[l] + ada_b[l])[:, None, :]
        sh1, sc1, g1, sh2, sc2, g2 = jnp.split(mod, 6, axis=-1)
        hx = modulate(rms_norm(x, norm_mix_w[l]), sh1, sc1)
        hc = None
        if ctx_in:
            cmod = (silu_cc @ ada_w[l] + ada_b[l])[None, None, :]
            csh1, csc1, cg1, csh2, csc2, cg2 = jnp.split(cmod, 6, axis=-1)
            hc = modulate(rms_norm(cx, norm_mix_w[l]), csh1, csc1)
        if even:
            mx, mc = even_mixer(hx, hc, w_in[li], w_out[li], ret_log_decay[li], diff_lambda[li],
                                diff_subln_w[li], l, row, col, ctx_after)
        else:
            mx = pool_mixer(hx, pool_w[li], pool_scale[li])
            mc = pool_mixer(hc, pool_w[li], pool_scale[li]) if ctx_after else None
        x = x + g1 * mx
        x = x + g2 * moe_ffn(modulate(rms_norm(x, norm_ffn_w[l]), sh2, sc2), router_w, router_b,
                             moe_w_gate[l], moe_w_up[l], moe_w_down[l])
        if ctx_after:
            cx = cx + cg1 * mc
            cx = cx + cg2 * moe_ffn(modulate(rms_norm(cx, norm_ffn_w[l]), csh2, csc2), router_w, router_b,
                                    moe_w_gate[l], moe_w_up[l], moe_w_down[l])
    return rms_norm(x, final_norm_w)


_drawn_inputs = setup_inputs


def setup_inputs(seed=0):
    import zlib

    import numpy as np

    out = dict(_drawn_inputs(seed))
    spreads = {}
    factors = {'norm_mix_w': 2.716, 'diff_subln_w': 80.713, 'final_norm_w': 200.0, 'norm_ffn_w': 6.876}
    for name, (base, spread) in spreads.items():
        noise = np.random.default_rng([zlib.crc32(name.encode()), seed]).standard_normal(out[name].shape)
        drawn = base * np.exp(spread * noise) if base else spread * noise
        out[name] = jnp.asarray(drawn.astype(out[name].dtype))
    for name, factor in factors.items():
        out[name] = (out[name] * factor).astype(out[name].dtype)
    return out
```

```python
from contextlib import ExitStack
import math

import numpy as np

import concourse.bass as bass
from concourse import mybir

ALU = mybir.AluOpType
ACT = mybir.ActivationFunctionType
AX = mybir.AxisListType
F32 = mybir.dt.float32
I32 = mybir.dt.int32
U32 = mybir.dt.uint32
I16 = mybir.dt.int16

P = 128
D, SEQ, CTX, DEPTH = 1024, 512, 256, 2
KD = D // P
NT, NC = SEQ // P, CTX // P
NK = NT + NC
HEADS, DK, DV = 4, 64, 128
NE, NG, DE = 16, 4, 512
KE = DE // P
HALF = 512
EPS = 1e-6
LAM_INIT = 0.8 - 0.6 * math.exp(-0.3 * 0)
WINDOWS = (2, 4, 8, 16)
GRID_W = 64
SLOT_W = 4096
GAP_W = SEQ + 7 * P
GAP_0 = 5 * P
LIST_N = NE * SEQ

SH1, SC1, G1, SH2, SC2, G2 = (KD * i for i in range(6))
C_ROW, CC_ROW, NM_ROW, NF_ROW, PS_ROW, SMALL_ROWS = 0, KD, 2 * KD, 4 * KD, 6 * KD, 7 * KD


def constants():
    half = DK // 4
    inv = 10000.0 ** (-np.arange(half, dtype=np.float32) / np.float32(half))
    pos = np.arange(SEQ)
    tables = []
    for p in (pos // GRID_W, pos % GRID_W):
        ang = p.astype(np.float32)[:, None] * inv.astype(np.float32)[None, :]
        tables.append((np.cos(ang), np.sin(ang)))
    rope_cos = np.concatenate([tables[0][0], tables[0][0], tables[1][0], tables[1][0]], 1)
    rope_sin = np.concatenate([-tables[0][1], tables[0][1], -tables[1][1], tables[1][1]], 1)
    gap = (np.arange(GAP_W) - GAP_0)[None, :] - np.arange(P)[:, None]
    before = np.triu(np.ones((P, P), np.float32), 1)
    bands = np.zeros((P, len(WINDOWS), 5, P), np.float32)
    for g, w in enumerate(WINDOWS):
        left, right = w // 2, w - 1 - w // 2
        full = np.zeros((SEQ, SEQ), np.float64)
        for t in range(SEQ):
            lo, hi = max(t - left, 0), min(t + right + 1, SEQ)
            full[lo:hi, t] = 1.0 / (hi - lo)
            full[t, t] -= 1.0
        for b, (a, t) in enumerate([(0, 0), (1, 1), (NT - 1, NT - 1), (0, 1), (2, 1)]):
            bands[:, g, b] = full[a * P:(a + 1) * P, t * P:(t + 1) * P]
    rows = np.zeros((2, NE), np.float32)
    rows[0] = np.arange(NE)
    rows[1] = np.arange(NE) // (NE // NG)
    token = np.arange(SEQ, dtype=np.int32).reshape(NT, P).T
    return {
        "k_ident": np.eye(P, dtype=np.float32), "k_cos": rope_cos.astype(np.float32),
        "k_sin": rope_sin.astype(np.float32), "k_gap": gap.astype(np.int16), "k_before": before,
        "k_bands": bands.reshape(P, -1), "k_rows": rows, "k_token": np.ascontiguousarray(token),
        "k_zero": np.zeros((P, LIST_N // P), np.int32),
    }


def build_program(nc, a, out):
    ctx = ExitStack()
    with ctx, nc.allow_non_contiguous_dma(reason="short rows of small tables"):
        def sb(name, shape, dt=F32):
            return ctx.enter_context(nc.sbuf_tensor(name, shape, dt))

        held = []

        def sem(name):
            held.append(nc.alloc_semaphore(name=name))
            return held[-1]

        def stage_over():
            nc.clear_and_free_semaphores(list(held))
            held.clear()
            nc.all_engine_barrier()

        xh_dram = nc.dram_tensor("xh_scratch", [SEQ, D], F32).ap()
        list_dram = nc.dram_tensor("list_scratch", [LIST_N, 1], I32).ap()
        y_dram = nc.dram_tensor("y_scratch", [LIST_N, D], F32).ap()

        bank = ctx.enter_context(nc.psum_tensor("bank", [P, 8, HALF], F32))

        x = sb("x_res", [P, NT, D])
        ident = sb("ident", [P, P])
        ones = sb("ones", [P, P])
        small = sb("small", [P, SMALL_ROWS])
        bias_cols = sb("bias_cols", [P, DEPTH * 6 * KD])
        silu_c = sb("silu_c", [P, 2, KD])
        mod = sb("mod", [P, DEPTH, 6 * KD, 2])
        norm_a = sb("norm_a", [P, 5, KD])
        gate1_b = sb("gate1_b", [P, D])
        gate2_b = sb("gate2_b", [P, D])
        stats = sb("stats", [P, 8])
        rstd = sb("rstd", [P, 8])
        minus_half = sb("minus_half", [P, NT])
        ring = sb("ring", [P, 4, SLOT_W])
        ARENA = 28928
        arena = sb("arena", [P, ARENA])

        def carve(start, *dims):
            n = int(np.prod(dims))
            assert start + n <= ARENA, (start, n)
            v = arena[:, start:start + n]
            if len(dims) > 1:
                names = " ".join(f"d{i}" for i in range(len(dims)))
                v = v.rearrange(f"p ({names}) -> p {names}", **{f"d{i}": d for i, d in enumerate(dims)})
            return v, start + n

        def linker(eng, s):
            n = [0]

            def link(ins):
                n[0] += 1
                ins.then_inc(s, 1)
                eng.wait_ge(s, n[0])
            return link

        def cols(ap, width):
            return ap.unsqueeze(2).to_broadcast([P, ap.shape[1], width])

        qT, at = carve(0, 6, SEQ)
        kT, at = carve(at, 6, NK * P)
        v_tok, at = carve(at, NK, 2 * HEADS * DV)
        gate, late = carve(at, NT, HEADS * DV)
        hT, at = carve(late, KD, SEQ)
        hcT, at = carve(at, KD, CTX)
        xhat2, at = carve(at, 2, D)
        ctx_raw, at = carve(at, NC, D)
        rope_x, at = carve(at, HALF)
        rope_y, at = carve(at, HALF)
        roped, at = carve(at, 2, HALF)
        cos_t, at = carve(at, NT, DK)
        sin_t, at = carve(at, NT, DK)
        decay, at = carve(late, 2, GAP_W)
        retp, at = carve(at, 4, SEQ)
        decay_c, at = carve(at, NC, SEQ)
        prob, at = carve(at, 2, 2, NK * P)
        diffp, at = carve(at, NK * P)
        diffT, at = carve(at, NK, P)
        dif_out, at = carve(at, NT, HEADS * DV)
        squares, at = carve(at, NT, DV)
        mixT = kT.rearrange("p a b -> p (a b)")[:, 0:KD * SEQ].rearrange("p (k t) -> p k t", k=KD)

        gap = gate1_b[:, 0:GAP_W // 2].bitcast(I16)
        gap_pos = sb("gap_pos", [P, P])
        gap_neg = sb("gap_neg", [P, P])
        decay_arg = sb("decay_arg", [P, P])
        ld = sb("ld", [P, 2 * HEADS])
        ld_neg = sb("ld_neg", [P, 2 * HEADS])
        lam_in = sb("lam_in", [P, 4 * DK])
        lam_pr = sb("lam_pr", [P, 2, DK])
        lam_s = sb("lam_s", [P, 2])
        lam_e = sb("lam_e", [P, 2])
        lam_v = sb("lam_v", [P, 2])
        subln = sb("subln", [P, DV])
        hstat = sb("hstat", [P, 2 * HEADS, NT])
        hrstd = sb("hrstd", [P, 2 * HEADS, NT])
        smax = sb("smax", [P, 2, 2])
        sden = sb("sden", [P, 2, 2])
        srec = sb("srec", [P, 2, 2])

        w_in, w_out, ada_w = a["w_in"], a["w_out"], a["ada_w"]

        def slab(w, c0):
            return w[:, c0:c0 + HALF].rearrange("(k p) c -> p k c", p=P)

        stream = [("ada", 0, j) for j in range(4)] + [("win", 0, j) for j in range(6)]
        stream += [("ada", 0, j) for j in range(4, 12)] + [("wout", 0, j) for j in range(2)]
        stream += [("ada", 1, j) for j in range(12)]

        units = [(j, t) for j in range(6) for t in range(NK if j >= 2 else NT)]

        def parts(j, t):
            p = {0: [(0, 256, "q", 0), (256, 256, "q", 2)], 1: [(0, 256, "q", 4), (256, 256, "g", 0)],
                 2: [(0, 256, "g", 256), (256, 256, "k", 0)], 3: [(0, 512, "v", 0)],
                 4: [(0, 512, "k", 2)], 5: [(0, 512, "v", 512)]}[j]
            return [q for q in p if t < NT or q[2] not in "qg"]

        roped_units = [u for u, (j, t) in enumerate(units) if any(q[2] in "qk" for q in parts(j, t))]
        gate_units = [u for u, (j, t) in enumerate(units) if any(q[2] == "g" for q in parts(j, t))]
        v_units = [u for u, (j, t) in enumerate(units) if any(q[2] == "v" for q in parts(j, t))]

        m_ld = {n: sem(f"m_ld_{n}") for n in ("ident", "smallA", "smallB", "rope", "row", "gap", "zero")}
        m_x = [sem(f"m_x{t}") for t in range(NK)]
        m_small = sem("m_small_transposed")
        m_cols = sem("m_small_cols")
        m_silu = sem("m_silu_c")
        m_slot = [sem(f"m_slot{i}_loaded") for i in range(4)]
        m_ada = sem("m_adaln_slab_done")
        m_modc = sem("m_mod_copied")
        m_na = sem("m_norm_a_ready")
        m_sq = sem("m_square_sum")
        m_rs = sem("m_rstd")
        m_xh = sem("m_xhat")
        m_xt = sem("m_xhat_transposed")
        m_hta = sem("m_hT_by_act")
        m_htd = sem("m_hT_by_dve")
        m_proj = sem("m_projected")
        m_rope = sem("m_roped")
        m_gv = sem("m_gate_or_v_copied")
        m_qkt = sem("m_qk_transposed")
        m_qkc = sem("m_qk_copied")
        m_dchain = sem("m_dve_chain")
        m_pchain = sem("m_pool_chain")
        m_achain = sem("m_act_chain")
        m_lam = sem("m_lambda_sums")
        m_lame = sem("m_lambda_exps")
        m_gapc = sem("m_decay_args")
        m_dk_arg = sem("m_decay_arg")
        m_dk = sem("m_decay_exp")
        m_dkd = sem("m_decay_ready")
        m_rs_s = sem("m_ret_scores")
        m_rs_p = sem("m_ret_masked")
        m_rs_v = sem("m_ret_values_done")
        m_o = sem("m_head_out")
        m_osq = sem("m_head_squares")
        m_ost = sem("m_head_stat")
        m_orr = sem("m_head_rstd")
        m_on = sem("m_head_normed")
        m_ds = sem("m_diff_scores")
        m_dm = sem("m_diff_max")
        m_de = sem("m_diff_exp")
        m_dp = sem("m_diff_combined")
        m_dt = sem("m_diff_transposed")
        m_dc = sem("m_diff_copied")
        m_dg = sem("m_diag")
        m_gr = sem("m_gate_rows")
        m_grc = sem("m_gate_rows_copied")
        m_mt = sem("m_mix_transposed")
        m_mtc = sem("m_mix_copied")
        m_op = sem("m_out_projected")
        m_xr = sem("m_x_updated")
        m_mset = sem("m_memsets")

        RU = HEADS * NK
        DU = HEADS * NT

        def pair(c):
            return bank[:, 2 * c:2 * c + 2, :].rearrange("p b c -> p (b c)")[:, 0:NK * P]

        tr_diff = bank[:, 4:6, :].rearrange("p b c -> p (b c)")[:, 0:NK * P]

        diag1 = qT.rearrange("p a b -> p (a b)")[:, 0:KD * P].rearrange("p (k n) -> p k n", k=KD)
        upd = qT.rearrange("p a b -> p (a b)")[:, KD * P:KD * P + HALF]

        with nc.Block() as block:

            @block.sync
            def _(sp):
                for n, (kind, l, j) in enumerate(stream):
                    if n >= 4:
                        was, l0, j0 = stream[n - 4]
                        if was == "ada":
                            sp.wait_ge(m_ada, 12 * l0 + j0 + 1)
                        elif was == "win":
                            sp.wait_ge(m_proj, max(u for u, (s, _) in enumerate(units) if s == j0) + 1)
                        else:
                            sp.wait_ge(m_op, NT * (j0 + 1))
                    w = {"ada": ada_w[l], "win": w_in[0], "wout": w_out[0]}[kind]
                    sp.dma_start(ring[:, n % 4, :].rearrange("p (k c) -> p k c", k=KD),
                                 slab(w, j * HALF)).then_inc(m_slot[n % 4], 16)

            @block.scalar
            def _(act):
                link = linker(act, m_achain)
                act.dma_start(ident[:], a["k_ident"]).then_inc(m_ld["ident"], 16)
                for r0, src in ((C_ROW, a["c"][0]), (CC_ROW, a["c_ctx"]), (NM_ROW, a["norm_mix_w"][0]),
                                (NM_ROW + KD, a["norm_mix_w"][1]), (NF_ROW, a["norm_ffn_w"][0]),
                                (NF_ROW + KD, a["norm_ffn_w"][1]), (PS_ROW, a["pool_scale"][0])):
                    act.dma_start(arena[r0:r0 + KD, 0:P], src.rearrange("(r c) -> r c", c=P)).then_inc(m_ld["smallA"], 16)
                act.dma_start(arena[0:DEPTH * 6 * KD, P:2 * P],
                              a["ada_b"].rearrange("l (r c) -> (l r) c", c=P)).then_inc(m_ld["smallB"], 16)
                for t in range(NK):
                    if t < NT:
                        act.dma_start(x[:, t, :], a["x"][0, t * P:(t + 1) * P, :]).then_inc(m_x[t], 16)
                    else:
                        act.dma_start(ctx_raw[:, t - NT, :],
                                      a["ctx"][0, (t - NT) * P:(t - NT + 1) * P, :]).then_inc(m_x[t], 16)
                act.dma_start(cos_t, a["k_cos"].rearrange("(t p) c -> p t c", p=P)).then_inc(m_ld["rope"], 16)
                act.dma_start(sin_t, a["k_sin"].rearrange("(t p) c -> p t c", p=P)).then_inc(m_ld["rope"], 16)
                act.dma_start(gap, a["k_gap"]).then_inc(m_ld["gap"], 16)
                act.dma_start(list_dram.rearrange("(p c) o -> p (c o)", p=P), a["k_zero"]).then_inc(m_ld["zero"], 16)
                act.dma_start(ld[:], a["ret_log_decay"].rearrange("n d h -> n (d h)").partition_broadcast(P)
                              .rearrange("p n c -> p (n c)")).then_inc(m_ld["row"], 16)
                act.dma_start(lam_in[:], a["diff_lambda"].rearrange("n d h -> n (d h)").partition_broadcast(P)
                              .rearrange("p n c -> p (n c)")).then_inc(m_ld["row"], 16)
                act.dma_start(subln[:], a["diff_subln_w"].partition_broadcast(P)
                              .rearrange("p n c -> p (n c)")).then_inc(m_ld["row"], 16)
                act.wait_ge(m_cols, 1)
                nc.scalar.activation(silu_c[:].rearrange("p v k -> p (v k)"), small[:, C_ROW:C_ROW + 2 * KD],
                                     ACT.Silu).then_inc(m_silu, 1)

                def squares_of(t):
                    act.wait_ge(m_x[t], 16)
                    if t >= 2:
                        act.wait_ge(m_xt, t - 1)
                    src = x[:, t, :] if t < NT else ctx_raw[:, t - NT, :]
                    nc.scalar.activation(xhat2[:, t % 2, :], src, ACT.Square,
                                         accum_out=stats[:, t:t + 1]).then_inc(m_sq, 1)

                def hT_of(t):
                    act.wait_ge(m_xt, t + 1)
                    act.wait_ge(m_na, 1)
                    v, na = (0, 0) if t < NT else (1, 1)
                    for k in range(KD // 2):
                        dst = hT[:, k, t * P:(t + 1) * P] if t < NT else hcT[:, k, (t - NT) * P:(t - NT + 1) * P]
                        last = nc.scalar.activation(dst, bank[:, (t % 2) * 2 + k // 4, (k % 4) * P:(k % 4 + 1) * P],
                                                    ACT.Identity, scale=norm_a[:, na, k:k + 1],
                                                    bias=mod[:, 0, SH1 + k, v:v + 1])
                    last.then_inc(m_hta, 1)

                squares_of(0)
                squares_of(1)
                for t in range(NK):
                    hT_of(t)
                    if t + 2 < NK:
                        squares_of(t + 2)

                def copy_qk(r):
                    j, t = units[roped_units[r]]
                    act.wait_ge(m_qkt, r + 1)
                    for c0, w, kind, b0 in parts(j, t):
                        if kind in "qk":
                            dst = (qT if kind == "q" else kT)[:, b0:b0 + w // P, t * P:(t + 1) * P]
                            last = nc.scalar.copy(dst, bank[:, 4 + r % 2, c0:c0 + w].rearrange("p (b c) -> p b c", c=P))
                    last.then_inc(m_qkc, 1)

                r = 0
                for u, (j, t) in enumerate(units):
                    for c0, w, kind, b0 in parts(j, t):
                        if kind not in "gv":
                            continue
                        act.wait_ge(m_proj, u + 1)
                        if u in roped_units:
                            act.wait_ge(m_rope, roped_units.index(u) + 1)
                        ps = bank[:, u % 3, c0:c0 + w]
                        if kind == "g":
                            nc.scalar.activation(gate[:, t, b0:b0 + w], ps, ACT.Silu).then_inc(m_gv, 1)
                        else:
                            nc.scalar.copy(v_tok[:, t, b0:b0 + w], ps).then_inc(m_gv, 1)
                    while r < len(roped_units) and roped_units[r] <= u - 1:
                        copy_qk(r)
                        r += 1
                while r < len(roped_units):
                    copy_qk(r)
                    r += 1

                act.wait_ge(m_lam, 1)
                nc.scalar.activation(lam_e[:], lam_s[:], ACT.Exp).then_inc(m_lame, 1)

                def decay_of(h):
                    act.wait_ge(m_proj, len(units))
                    if h >= 2:
                        act.wait_ge(m_rs_p, NK * (h - 1))
                    d = decay[:, h % 2, :]
                    nc.scalar.activation(d[:, GAP_0 + P:], gap[:, GAP_0 + P:], ACT.Exp, scale=ld[:, h:h + 1])
                    nc.scalar.activation(d[:, 0:GAP_0], gap[:, 0:GAP_0], ACT.Exp,
                                         scale=ld_neg[:, HEADS + h:HEADS + h + 1]).then_inc(m_dk, 1)
                    act.wait_ge(m_dk_arg, h + 1)
                    nc.scalar.activation(d[:, GAP_0:GAP_0 + P], decay_arg[:], ACT.Exp).then_inc(m_dk, 1)

                def head_squares(n):
                    if n < HEADS:
                        act.wait_ge(m_rs_v, NK * (n + 1))
                    else:
                        act.wait_ge(m_o, n - HEADS + 1)
                    if n >= 1:
                        act.wait_ge(m_ost, n)
                    nc.scalar.activation(squares, bank[:, 6 + n % 2, :].rearrange("p (t c) -> p t c", c=DV),
                                         ACT.Square).then_inc(m_osq, 1)

                act.wait_ge(m_gapc, 1)
                decay_of(0)
                decay_of(1)
                for h in range(HEADS):
                    head_squares(h)
                    if h + 2 < HEADS:
                        decay_of(h + 2)

                def exps(u):
                    act.wait_ge(m_dm, u + 1)
                    if u >= 2:
                        act.wait_ge(m_dp, u - 1)
                    for c in range(2):
                        nc.scalar.activation(prob[:, u % 2, c, :], pair(c), ACT.Exp, scale=DK ** -0.5,
                                             bias=smax[:, u % 2, c:c + 1],
                                             accum_out=sden[:, u % 2, c:c + 1]).then_inc(m_de, 1)

                def copy_T(u):
                    act.wait_ge(m_dt, u + 1)
                    nc.scalar.copy(diffT.rearrange("p t c -> p (t c)"), tr_diff).then_inc(m_dc, 1)

                for u in range(DU):
                    exps(u)
                    if u >= 1:
                        copy_T(u - 1)
                    if u >= 3 and (u - 3) % NT == NT - 1:
                        head_squares(HEADS + (u - 3) // NT)
                copy_T(DU - 1)
                for h in range((DU - 3) // NT, HEADS):
                    head_squares(HEADS + h)
                act.wait_ge(m_gr, 1)
                nc.scalar.copy(gate1_b[:], bank[:, 4:6, :].rearrange("p b c -> p (b c)")).then_inc(m_grc, 1)
                for hh in range(2 * HEADS):
                    act.wait_ge(m_mt, hh + 1)
                    nc.scalar.copy(mixT[:, hh, :], bank[:, hh % 4, :]).then_inc(m_mtc, 1)

            @block.gpsimd
            def _(pool):
                link = linker(pool, m_pchain)
                link(nc.gpsimd.memset(minus_half[:], -0.5))
                for t in range(NK):
                    pool.wait_ge(m_sq, t + 1)
                    link(nc.gpsimd.tensor_scalar(rstd[:, t:t + 1], stats[:, t:t + 1], 1.0 / D, EPS, ALU.mult, ALU.add))
                    nc.gpsimd.tensor_tensor(rstd[:, t:t + 1], rstd[:, t:t + 1], minus_half[:, 0:1],
                                            ALU.pow).then_inc(m_rs, 1)
                for n in range(2 * HEADS):
                    pool.wait_ge(m_ost, n + 1)
                    link(nc.gpsimd.tensor_scalar(hrstd[:, n, :], hstat[:, n, :], 1.0 / DV, EPS, ALU.mult, ALU.add))
                    nc.gpsimd.tensor_tensor(hrstd[:, n, :], hrstd[:, n, :], minus_half[:], ALU.pow).then_inc(m_orr, 1)

            @block.vector
            def _(dve):
                link = linker(dve, m_dchain)
                nc.vector.memset(ones[:], 1.0).then_inc(m_mset, 1)
                dve.wait_ge(m_small, 1)
                nc.vector.tensor_copy(small[:], bank[:, 6, 0:SMALL_ROWS]).then_inc(m_cols, 1)
                nc.vector.tensor_copy(bias_cols[:], bank[:, 6, P:P + DEPTH * 6 * KD]).then_inc(m_cols, 1)

                def mod_copy(l, j0, j1):
                    w = HALF // P
                    src = bank[:, 7, 2 * 6 * KD * l + 2 * w * j0:2 * 6 * KD * l + 2 * w * j1]
                    return nc.vector.tensor_tensor(
                        mod[:, l, w * j0:w * j1, :], src.rearrange("p (j v) -> p j v", v=2),
                        cols(bias_cols[:, 6 * KD * l + w * j0:6 * KD * l + w * j1], 2), ALU.add)

                def norm_scale(n, l, sc, v, row):
                    return nc.vector.scalar_tensor_tensor(norm_a[:, n, :], mod[:, l, sc:sc + KD, v], 1.0,
                                                          small[:, row:row + KD], ALU.add, ALU.mult)

                def xhat_of(t):
                    dve.wait_ge(m_rs, t + 1)
                    src = x[:, t, :] if t < NT else ctx_raw[:, t - NT, :]
                    nc.vector.tensor_scalar(xhat2[:, t % 2, :], src, rstd[:, t:t + 1], None, ALU.mult).then_inc(m_xh, 1)

                def hT_of(t):
                    dve.wait_ge(m_xt, t + 1)
                    v, na = (0, 0) if t < NT else (1, 1)
                    for k in range(KD // 2, KD):
                        dst = hT[:, k, t * P:(t + 1) * P] if t < NT else hcT[:, k, (t - NT) * P:(t - NT + 1) * P]
                        last = nc.vector.tensor_scalar(dst, bank[:, (t % 2) * 2 + k // 4, (k % 4) * P:(k % 4 + 1) * P],
                                                       norm_a[:, na, k:k + 1], mod[:, 0, SH1 + k, v:v + 1],
                                                       ALU.mult, ALU.add)
                    last.then_inc(m_htd, 1)

                xhat_of(0)
                xhat_of(1)
                dve.wait_ge(m_ada, 4)
                dve.wait_ge(m_cols, 2)
                link(mod_copy(0, 0, 4))
                nc.vector.scalar_tensor_tensor(norm_a[:, 0, :], mod[:, 0, SC1:SC1 + KD, 0], 1.0,
                                               small[:, NM_ROW:NM_ROW + KD], ALU.add, ALU.mult)
                ins = norm_scale(1, 0, SC1, 1, NM_ROW)
                ins.then_inc(m_na, 1)
                dve.wait_ge(m_na, 1)
                for t in range(NK):
                    hT_of(t)
                    if t + 2 < NK:
                        xhat_of(t + 2)

                dve.wait_ge(m_ld["rope"], 32)
                for r, u in enumerate(roped_units):
                    j, t = units[u]
                    dve.wait_ge(m_proj, u + 1)
                    if r >= 2:
                        dve.wait_ge(m_qkt, r - 1)
                    if r >= 1:
                        dve.wait_ge(m_rope, r)
                    ps = bank[:, u % 3, :]
                    got = [q for q in parts(j, t) if q[2] in "qk"]
                    c0, w = got[0][0], sum(q[1] for q in got)
                    dst = roped[:, r % 2, c0:c0 + w]
                    if t >= NT:
                        nc.vector.tensor_copy(dst, ps[:, c0:c0 + w]).then_inc(m_rope, 1)
                        continue
                    n = w // DK
                    nc.vector.tensor_tensor(
                        rope_x[:, 0:w].rearrange("p (h c) -> p h c", c=DK),
                        ps[:, c0:c0 + w].rearrange("p (h c) -> p h c", c=DK),
                        cos_t[:, t, :].unsqueeze(1).to_broadcast([P, n, DK]), ALU.mult)
                    swap = ps[:, c0:c0 + w].rearrange("p (h g s c) -> p h g s c", g=2, s=2, c=DK // 4)
                    turned = rope_y[:, 0:w].rearrange("p (h g s c) -> p h g s c", g=2, s=2, c=DK // 4)
                    sine = sin_t[:, t, :].rearrange("p (g s c) -> p g s c", g=2, s=2)
                    for s in range(2):
                        ins = nc.vector.tensor_tensor(
                            turned[:, :, :, s, :], swap[:, :, :, 1 - s, :],
                            sine[:, :, s, :].unsqueeze(1).to_broadcast([P, n, 2, DK // 4]), ALU.mult)
                    link(ins)
                    nc.vector.tensor_tensor(dst, rope_x[:, 0:w], rope_y[:, 0:w], ALU.add).then_inc(m_rope, 1)

                dve.wait_ge(m_ada, 12)
                link(mod_copy(0, 4, 12))
                link(norm_scale(2, 0, SC2, 0, NF_ROW))

                dve.wait_ge(m_ld["row"], 48)
                lv = lam_in[:].rearrange("p (a b c) -> p a b c", a=2, b=2)
                link(nc.vector.tensor_tensor(lam_pr[:], lv[:, :, 0, :], lv[:, :, 1, :], ALU.mult))
                nc.vector.tensor_reduce(lam_s[:], lam_pr[:], AX.X, ALU.add).then_inc(m_lam, 1)
                nc.vector.tensor_scalar(subln[:], subln[:], 1.0 - LAM_INIT, None, ALU.mult)
                nc.vector.tensor_scalar(ld_neg[:], ld[:], -1.0, None, ALU.mult)
                dve.wait_ge(m_ld["gap"], 16)
                nc.vector.tensor_scalar(gap_pos[:], gap[:, GAP_0:GAP_0 + P], 0.0, None, ALU.max)
                nc.vector.tensor_scalar(gap_neg[:], gap[:, GAP_0:GAP_0 + P], 0.0, None, ALU.min).then_inc(m_gapc, 1)
                dve.wait_ge(m_gapc, 1)
                nc.vector.memset(lam_v[:, 0:1], 1.0)
                dve.wait_ge(m_lame, 1)
                link(nc.vector.tensor_tensor(lam_v[:, 1:2], lam_e[:, 1:2], lam_e[:, 0:1], ALU.subtract))
                link(nc.vector.tensor_scalar(lam_v[:, 1:2], lam_v[:, 1:2], -LAM_INIT, None, ALU.add))

                def decay_arg_of(h):
                    if h >= 1:
                        dve.wait_ge(m_dk, 2 * h)
                    link(nc.vector.tensor_scalar(decay_arg[:], gap_pos[:], ld[:, h:h + 1], None, ALU.mult))
                    nc.vector.scalar_tensor_tensor(decay_arg[:], gap_neg[:], ld_neg[:, HEADS + h:HEADS + h + 1],
                                                   decay_arg[:], ALU.mult, ALU.add).then_inc(m_dk_arg, 1)

                def decay_finish(h):
                    dve.wait_ge(m_dk, 2 * h + 2)
                    d = decay[:, h % 2, :]
                    ins = nc.vector.tensor_tensor(d[:, GAP_0:GAP_0 + P], d[:, GAP_0:GAP_0 + P], ident[:], ALU.add)
                    for cp in range(NC):
                        f0, b0 = GAP_0 - P * (cp - NC), GAP_0 - P * (NT + cp)
                        ins = nc.vector.tensor_tensor(decay_c[:, cp, :], d[:, f0:f0 + SEQ], d[:, b0:b0 + SEQ], ALU.add)
                    link(ins)

                def head_stat(n):
                    dve.wait_ge(m_osq, n + 1)
                    nc.vector.tensor_reduce(hstat[:, n, :], squares, AX.X, ALU.add).then_inc(m_ost, 1)

                def head_norm(n):
                    dve.wait_ge(m_orr, n + 1)
                    o = bank[:, 6 + n % 2, :].rearrange("p (t c) -> p t c", c=DV)
                    for t in range(NT):
                        if n < HEADS:
                            dst = gate[:, t, n * DV:(n + 1) * DV]
                            with_ = dst
                        else:
                            dst = dif_out[:, t, (n - HEADS) * DV:(n - HEADS + 1) * DV]
                            with_ = subln[:]
                        ins = nc.vector.scalar_tensor_tensor(dst, o[:, t, :], hrstd[:, n, t:t + 1], with_,
                                                             ALU.mult, ALU.mult)
                    ins.then_inc(m_on, 1)

                decay_arg_of(0)
                decay_arg_of(1)
                for h in range(HEADS):
                    decay_finish(h)
                    for m in range(NK):
                        u = h * NK + m
                        dve.wait_ge(m_rs_s, u + 1)
                        if u >= 4:
                            dve.wait_ge(m_rs_v, u - 3)
                        win = (decay[:, h % 2, GAP_0 - P * m:GAP_0 - P * m + SEQ] if m < NT
                               else decay_c[:, m - NT, :])
                        nc.vector.tensor_tensor(retp[:, u % 4, :], bank[:, u % 4, :], win, ALU.mult).then_inc(m_rs_p, 1)
                        if m == 2 and h >= 1:
                            head_stat(h - 1)
                        if m == 4 and h >= 1:
                            head_norm(h - 1)
                    if h + 2 < HEADS:
                        decay_arg_of(h + 2)
                    dve.wait_ge(m_rs_p, NK * (h + 1))
                head_stat(HEADS - 1)
                head_norm(HEADS - 1)

                def combine(u):
                    b = u % 2
                    dve.wait_ge(m_de, 2 * u + 2)
                    link(nc.vector.reciprocal(srec[:, b, :], sden[:, b, :]))
                    link(nc.vector.tensor_tensor(srec[:, b, :], srec[:, b, :], lam_v[:], ALU.mult))
                    if u >= 1:
                        dve.wait_ge(m_dt, u)
                    link(nc.vector.tensor_scalar(diffp, prob[:, b, 0, :], srec[:, b, 0:1], None, ALU.mult))
                    nc.vector.scalar_tensor_tensor(diffp, prob[:, b, 1, :], srec[:, b, 1:2], diffp,
                                                   ALU.mult, ALU.add).then_inc(m_dp, 1)

                for u in range(DU):
                    dve.wait_ge(m_ds, u + 1)
                    both = bank[:, 0:4, :].rearrange("p (c b) n -> p c (b n)", c=2)[:, :, 0:NK * P]
                    link(nc.vector.tensor_reduce(smax[:, u % 2, :], both, AX.X, ALU.max))
                    nc.vector.tensor_scalar(smax[:, u % 2, :], smax[:, u % 2, :], -(DK ** -0.5), None,
                                            ALU.mult).then_inc(m_dm, 1)
                    if u >= 1:
                        combine(u - 1)
                    if u >= 4 and (u - 4) % NT == NT - 1:
                        head_stat(HEADS + (u - 4) // NT)
                        head_norm(HEADS + (u - 4) // NT)
                combine(DU - 1)
                for h in range((DU - 4) // NT, HEADS):
                    head_stat(HEADS + h)
                    head_norm(HEADS + h)

                for k in range(KD):
                    ins = nc.vector.tensor_scalar(diag1[:, k, :], ident[:], mod[:, 0, G1 + k, 0:1], None, ALU.mult)
                ins.then_inc(m_dg, 1)
                dve.wait_ge(m_grc, 1)
                for n in range(2 * NT):
                    hf, t = n // NT, n % NT
                    dve.wait_ge(m_op, n + 1)
                    if n >= 1:
                        dve.wait_ge(m_xr, n)
                    link(nc.vector.tensor_tensor(upd, bank[:, 4 + n % 2, :], gate1_b[:, hf * HALF:(hf + 1) * HALF],
                                                 ALU.mult))
                    xs = x[:, t, hf * HALF:(hf + 1) * HALF]
                    nc.vector.tensor_tensor(xs, xs, upd, ALU.add).then_inc(m_xr, 1)
                dve.wait_ge(m_ada, 24)
                link(mod_copy(1, 0, 12))
                norm_scale(3, 1, SC1, 0, NM_ROW + KD)
                norm_scale(4, 1, SC2, 0, NF_ROW + KD)
                nc.vector.tensor_tensor(mod[:, 1, G1:G1 + KD, 0], mod[:, 1, G1:G1 + KD, 0],
                                        small[:, PS_ROW:PS_ROW + KD], ALU.mult)

            @block.tensor
            def _(pe):
                pe.wait_ge(m_ld["ident"], 16)
                pe.wait_ge(m_ld["smallA"], 7 * 16)
                pe.wait_ge(m_ld["smallB"], 16)
                pe.transpose(bank[:, 6, 0:SMALL_ROWS], arena[0:SMALL_ROWS, 0:P], ident[0:SMALL_ROWS, 0:SMALL_ROWS])
                nb = DEPTH * 6 * KD
                pe.transpose(bank[:, 6, P:P + nb], arena[0:nb, P:2 * P], ident[0:nb, 0:nb]).then_inc(m_small, 1)

                seen = [0]

                def slot():
                    n = seen[0]
                    seen[0] += 1
                    pe.wait_ge(m_slot[n % 4], 16 * (n // 4 + 1))
                    return n, ring[:, n % 4, :].rearrange("p (k c) -> p k c", k=KD)

                def adaln(l, j):
                    n, w = slot()
                    for b in range(HALF // P):
                        col = 2 * (6 * KD * l + j * (HALF // P) + b)
                        for k in range(KD):
                            last = pe.matmul(bank[:, 7, col:col + 2], w[:, k, b * P:(b + 1) * P], silu_c[:, :, k],
                                             start=(k == 0), stop=(k == KD - 1))
                    last.then_inc(m_ada, 1)
                    return last

                pe.wait_ge(m_silu, 1)
                for j in range(4):
                    last = adaln(0, j)

                for t in range(NK):
                    pe.wait_ge(m_xh, t + 1)
                    if t >= 2:
                        pe.wait_ge(m_hta, t - 1)
                        pe.wait_ge(m_htd, t - 1)
                    for k in range(KD):
                        last = pe.transpose(bank[:, (t % 2) * 2 + k // 4, (k % 4) * P:(k % 4 + 1) * P],
                                            xhat2[:, t % 2, k * P:(k + 1) * P], ident[:])
                    last.then_inc(m_xt, 1)
                pe.wait_ge(m_hta, NK)
                pe.wait_ge(m_htd, NK)

                def unit_read(u):
                    if u in rope_at:
                        pe.wait_ge(m_rope, rope_at[u] + 1)
                    if u in gv_at:
                        pe.wait_ge(m_gv, gv_at[u] + 1)

                rope_at = {u: i for i, u in enumerate(roped_units)}
                gv_at = {u: i for i, u in enumerate(sorted(gate_units + v_units))}

                def transpose_unit(u):
                    if u not in rope_at:
                        return
                    r = rope_at[u]
                    pe.wait_ge(m_rope, r + 1)
                    if r >= 2:
                        pe.wait_ge(m_qkc, r - 1)
                    for c0, w, kind, b0 in parts(*units[u]):
                        if kind in "qk":
                            for c in range(c0, c0 + w, P):
                                last = pe.transpose(bank[:, 4 + r % 2, c:c + P], roped[:, r % 2, c:c + P], ident[:])
                    last.then_inc(m_qkt, 1)

                at_slab = {}
                for u, (j, t) in enumerate(units):
                    if j not in at_slab:
                        at_slab[j] = slot()
                    n, w = at_slab[j]
                    if u >= 3:
                        unit_read(u - 3)
                    got = parts(j, t)
                    c0, c1 = got[0][0], got[-1][0] + got[-1][1]
                    for k in range(KD):
                        h = hT[:, k, t * P:(t + 1) * P] if t < NT else hcT[:, k, (t - NT) * P:(t - NT + 1) * P]
                        last = pe.matmul(bank[:, u % 3, c0:c1], h, w[:, k, c0:c1], start=(k == 0), stop=(k == KD - 1))
                    last.then_inc(m_proj, 1)
                    if u >= 1:
                        transpose_unit(u - 1)
                transpose_unit(len(units) - 1)
                for u in range(len(units) - 3, len(units)):
                    unit_read(u)

                for j in range(4, 12):
                    last = adaln(0, j)

                pe.wait_ge(m_qkc, len(roped_units))

                def ret_scores(u):
                    h, m = divmod(u, NK)
                    if u >= 4:
                        pe.wait_ge(m_rs_p, u - 3)
                    lo = DK * (h % 2)
                    pe.matmul(bank[:, u % 4, :], kT[lo:lo + DK, h // 2, m * P:(m + 1) * P], qT[lo:lo + DK, h // 2, :],
                              start=True, stop=True).then_inc(m_rs_s, 1)

                def ret_values(u):
                    h, m = divmod(u, NK)
                    if m == 0 and h >= 2:
                        pe.wait_ge(m_on, h - 1)
                    pe.wait_ge(m_rs_p, u + 1)
                    for t in range(NT):
                        last = pe.matmul(bank[:, 6 + h % 2, t * DV:(t + 1) * DV], retp[:, u % 4, t * P:(t + 1) * P],
                                         v_tok[:, m, h * DV:(h + 1) * DV], start=(m == 0 and t == 0),
                                         stop=(m == NK - 1 and t == NT - 1), skip_group_check=True)
                    last.then_inc(m_rs_v, 1)

                for u in range(RU + 2):
                    if u < RU:
                        ret_scores(u)
                    if u >= 2:
                        ret_values(u - 2)

                def diff_scores(u):
                    h, t = divmod(u, NT)
                    if u == 0:
                        pe.wait_ge(m_rs_p, RU)
                    else:
                        pe.wait_ge(m_de, 2 * u)
                    for c in range(2):
                        for b, (k0, k1) in enumerate(((0, HALF), (HALF, NK * P))):
                            last = pe.matmul(bank[:, 2 * c + b, 0:k1 - k0], qT[c * DK:(c + 1) * DK, 2 + h, t * P:(t + 1) * P],
                                             kT[c * DK:(c + 1) * DK, 2 + h, k0:k1], start=True, stop=True)
                    last.then_inc(m_ds, 1)

                def diff_transpose(u):
                    pe.wait_ge(m_dp, u + 1)
                    if u >= 1:
                        pe.wait_ge(m_dc, u)
                    for m in range(NK):
                        last = pe.transpose(tr_diff[:, m * P:(m + 1) * P], diffp[:, m * P:(m + 1) * P], ident[:])
                    last.then_inc(m_dt, 1)

                def diff_values(u):
                    h, t = divmod(u, NT)
                    n = HEADS + h
                    if t == 0:
                        pe.wait_ge(m_on, n - 1)
                    pe.wait_ge(m_dc, u + 1)
                    for m in range(NK):
                        last = pe.matmul(bank[:, 6 + n % 2, t * DV:(t + 1) * DV], diffT[:, m, :],
                                         v_tok[:, m, n * DV:(n + 1) * DV], start=(m == 0), stop=(m == NK - 1))
                    if t == NT - 1:
                        last.then_inc(m_o, 1)

                for u in range(DU + 2):
                    if u < DU:
                        diff_scores(u)
                    if u >= 2:
                        diff_values(u - 2)
                    if 1 <= u <= DU:
                        diff_transpose(u - 1)

                pe.wait_ge(m_mset, 1)
                pe.wait_ge(m_dg, 1)
                for k in range(KD):
                    last = pe.matmul(bank[:, 4 + k // 4, (k % 4) * P:(k % 4 + 1) * P], ones[:], diag1[:, k, :],
                                     start=True, stop=True)
                last.then_inc(m_gr, 1)

                for hh in range(2 * HEADS):
                    pe.wait_ge(m_on, 2 * HEADS)
                    if hh >= 4:
                        pe.wait_ge(m_mtc, hh - 3)
                    src = gate if hh < HEADS else dif_out
                    c0 = (hh % HEADS) * DV
                    for t in range(NT):
                        last = pe.transpose(bank[:, hh % 4, t * P:(t + 1) * P], src[:, t, c0:c0 + DV], ident[:])
                    last.then_inc(m_mt, 1)
                pe.wait_ge(m_grc, 1)
                pe.wait_ge(m_mtc, 2 * HEADS)
                for hf in range(2):
                    n, w = slot()
                    for t in range(NT):
                        i = hf * NT + t
                        if i >= 2:
                            pe.wait_ge(m_xr, i - 1)
                        for k in range(KD):
                            last = pe.matmul(bank[:, 4 + i % 2, :], mixT[:, k, t * P:(t + 1) * P], w[:, k, :],
                                             start=(k == 0), stop=(k == KD - 1))
                        last.then_inc(m_op, 1)
                for j in range(12):
                    last = adaln(1, j)

        stage_over()

        ring6, at = carve(0, 2, SLOT_W)
        moe0 = at
        at_small = [22000]

        def small_tile(name, shape, dt=F32):
            v, at_small[0] = carve(at_small[0], *shape[1:])
            return v if dt == F32 else v.bitcast(dt)

        router_w = small_tile("router_w_sb", [P, KD, NE])
        router_b = small_tile("router_b_sb", [P, NE])
        krows = small_tile("krows", [P, 2, NE])
        token = small_tile("token", [P, NT], I32)
        before = small_tile("before", [P, P])
        score = small_tile("score", [P, NT, NE])
        biased = small_tile("biased", [P, NT, NE])
        g_hi = small_tile("g_hi", [P, NT * NG, 2])
        g_lo = small_tile("g_lo", [P, NT * NG, 2])
        g_t = small_tile("g_t", [P, 3, NT * NG])
        g_pad = small_tile("g_pad", [P, NT, 8])
        top8 = small_tile("top8", [P, NT, 8])
        top8i = small_tile("top8i", [P, NT, 8], U32)
        g_sel = small_tile("g_sel", [P, NT])
        in_grp = small_tile("in_grp", [P, NT, NE])
        masked = small_tile("masked", [P, NT, NE])
        e_sel = small_tile("e_sel", [P, 2, NT])
        pick = small_tile("pick", [P, 2, NT, NE])
        e_mask = small_tile("e_mask", [P, NT, NE])
        r_tmp = small_tile("r_tmp", [P, 2, NT, NE])
        weight = small_tile("weight", [P, 2, NT])
        w_sum = small_tile("w_sum", [P, NT])
        row_tmp = small_tile("row_tmp", [P, 2, 2, NT])
        place = small_tile("place", [P, 2, NT])
        row_of = small_tile("row_of", [P, 2, NT], U32)
        entry_of = small_tile("entry_of", [P, 2, NT], U32)
        max_count = small_tile("max_count", [P, 1], I32)
        lists = small_tile("lists", [P, NE], I32)
        idx = small_tile("idx", [P, 2], U32)

        def moe(l):
            m_const = sem(f"moe{l}_tables_loaded")
            e_ = lambda s: sem(f"moe{l}_{s}")
            na = 2 if l == 0 else 4
            wg, wu, wd = a["moe_w_gate"][l], a["moe_w_up"][l], a["moe_w_down"][l]
            xhat, at = carve(moe0, NT, D)
            hT, at = carve(at, KD, SEQ)
            diag, at = carve(at, KD, P)
            xg, at = carve(moe0, 2, D)
            xgT, at = carve(at, 2, KD, P)
            act_g, at = carve(at, DE)
            hid, at = carve(at, DE)
            hidT, at = carve(at, KE, P)
            y_sb, at = carve(at, 2, D)

            def slot(i):
                return ring[:, i, :] if i < 4 else ring6[:, i - 4, :]

            def put(eng, w, e, i, k):
                src = w[bass.ds(e, 1)].rearrange("a (k p) c -> p (a k) c", p=P)
                return eng.dma_start(slot(i).rearrange("p (k c) -> p k c", k=k), src)

            s_sq, s_rs, s_xh, s_xst, s_xt = e_("square_sum"), e_("rstd"), e_("xhat"), e_("xhat_stored"), e_("xhat_T")
            s_hta, s_htd = e_("hT_by_act"), e_("hT_by_dve")
            s_lg, s_sc, s_mask, s_pos = e_("logits"), e_("scores"), e_("mask"), e_("places")
            s_rows, s_cnt = e_("rows_ready"), e_("count_ready")
            s_put, s_list = e_("lists_written"), e_("lists_loaded")
            s_dg, s_gr, s_grc = e_("diag"), e_("gate_rows"), e_("gate_rows_copied")
            s_load = [e_(f"slot{i}_loaded") for i in range(6)]
            s_idx = e_("idx_ready")
            s_xg = [e_(f"rows_gathered{u}") for u in range(2)]
            s_gt, s_gtc = e_("rows_T"), e_("rows_T_copied")
            s_gate, s_up, s_silu, s_hid = e_("gate_done"), e_("up_done"), e_("silu_done"), e_("hid_ready")
            s_ht2, s_ht2c, s_dn, s_y = e_("hid_T"), e_("hid_T_copied"), e_("down_done"), e_("y_ready")
            s_yst = [e_(f"y_stored{u}") for u in range(2)]
            s_dc, s_pc = e_("dve_chain"), e_("pool_chain")

            with nc.Block() as block:

                @block.sync
                def _(sp):
                    if l == 0:
                        sp.dma_start(router_w[:], a["router_w"].rearrange("(k p) e -> p k e", p=P)).then_inc(m_const, 16)
                        sp.dma_start(router_b[:], a["router_b"].partition_broadcast(P)).then_inc(m_const, 16)
                        sp.dma_start(krows[:], a["k_rows"].partition_broadcast(P)).then_inc(m_const, 16)
                        sp.dma_start(token[:], a["k_token"]).then_inc(m_const, 16)
                        sp.dma_start(before[:], a["k_before"]).then_inc(m_const, 16)
                    for u in range(2):
                        put(sp, wg, u, 3 * u, KD).then_inc(s_load[3 * u], 16)
                        put(sp, wu, u, 3 * u + 1, KD).then_inc(s_load[3 * u + 1], 16)
                        put(sp, wd, u, 3 * u + 2, KE).then_inc(s_load[3 * u + 2], 16)
                    for t in range(NT):
                        sp.wait_ge(s_xh, t + 1)
                        sp.dma_start(xh_dram[t * P:(t + 1) * P, :], xhat[:, t, :]).then_inc(s_xst, 16)
                    sp.wait_ge(s_put, 16 * 2 * NT)
                    sp.dma_start(lists[:], list_dram[0:P * NE, :].rearrange("(j e) o -> j (e o)", e=NE)).then_inc(s_list, 16)
                    with sp.Fori(1, NE // 2) as i:
                        for u in range(2):
                            e = sp.snap(2 * i + u)
                            for q, (w, k, used) in enumerate(((wg, KD, s_gate), (wu, KD, s_up), (wd, KE, s_dn))):
                                s = 3 * u + q
                                sp.wait_ge(used, e - 1)
                                put(sp, w, e, s, k).then_inc(s_load[s], 16)

                @block.gpsimd
                def _(pool):
                    link = linker(pool, s_pc)
                    for t in range(NT):
                        pool.wait_ge(s_sq, t + 1)
                        link(nc.gpsimd.tensor_scalar(rstd[:, t:t + 1], stats[:, t:t + 1], 1.0 / D, EPS,
                                                     ALU.mult, ALU.add))
                        nc.gpsimd.tensor_tensor(rstd[:, t:t + 1], rstd[:, t:t + 1], minus_half[:, 0:1],
                                                ALU.pow).then_inc(s_rs, 1)
                    pool.wait_ge(s_rows, 1)
                    for t in range(NT):
                        for c in range(2):
                            pool.indirect_dma_start(
                                out=list_dram, out_offset=bass.IndirectOffsetOnAxis(ap=entry_of[:, c, t:t + 1], axis=0),
                                in_=token[:, t:t + 1], in_offset=None).then_inc(s_put, 16)
                    pool.wait_ge(s_list, 16)
                    pool.wait_ge(s_xst, 16 * NT)
                    pool.wait_ge(s_lg, 1)

                    def gather(u, column):
                        nc.gpsimd.tensor_copy(idx[:, u:u + 1], column).then_inc(s_idx, 1)

                    def fetch(u):
                        pool.indirect_dma_start(out=xg[:, u, :], out_offset=None, in_=xh_dram,
                                                in_offset=bass.IndirectOffsetOnAxis(ap=idx[:, u:u + 1], axis=0)
                                                ).then_inc(s_xg[u], 16)

                    for u in range(2):
                        gather(u, lists[:, u:u + 1])
                        pool.wait_ge(s_idx, u + 1)
                        fetch(u)
                    for e in range(2, NE):
                        u = e % 2
                        pool.wait_ge(s_gt, e - 1)
                        pool.wait_ge(s_xg[u], 16 * (e // 2))
                        gather(u, lists[:, e:e + 1])
                        pool.wait_ge(s_idx, e + 1)
                        fetch(u)

                @block.scalar
                def _(act):
                    for t in range(NT):
                        nc.scalar.activation(xhat[:, t, :], x[:, t, :], ACT.Square,
                                             accum_out=stats[:, t:t + 1]).then_inc(s_sq, 1)
                    for k in range(0, KD, 2):
                        act.wait_ge(s_xt, k + 1)
                        nc.scalar.activation(hT[:, k, :], bank[:, k % 4, :], ACT.Identity,
                                             scale=norm_a[:, na, k:k + 1], bias=mod[:, l, SH2 + k, 0:1]).then_inc(s_hta, 1)
                    act.wait_ge(s_lg, 1)
                    nc.scalar.activation(score[:].rearrange("p t e -> p (t e)"), bank[:, 4, 0:NT * NE],
                                         ACT.Sigmoid).then_inc(s_sc, 1)
                    act.wait_ge(s_gr, 1)
                    nc.scalar.copy(gate2_b[:], bank[:, 6:8, :].rearrange("p b c -> p (b c)")).then_inc(s_grc, 1)

                    def copy_rows(u, n):
                        act.wait_ge(s_gt, n + 1)
                        for k in range(KD):
                            last = nc.scalar.activation(xgT[:, u, k, :], bank[:, k // 4, (k % 4) * P:(k % 4 + 1) * P],
                                                        ACT.Identity, scale=norm_a[:, na, k:k + 1],
                                                        bias=mod[:, l, SH2 + k, 0:1])
                        last.then_inc(s_gtc, 1)

                    def silu(n):
                        act.wait_ge(s_gate, n + 1)
                        nc.scalar.activation(act_g, bank[:, 2, :], ACT.Silu).then_inc(s_silu, 1)

                    def store(e, u, n):
                        act.wait_ge(s_y, n + 2)
                        act.dma_start(y_dram[bass.ds(e * P, P), :], y_sb[:, u, :]).then_inc(s_yst[u], 16)

                    copy_rows(0, 0)
                    copy_rows(1, 1)
                    silu(0)
                    with act.Fori(0, NE // 2 - 1) as i:
                        for u in range(2):
                            e = 2 * i + u
                            act.wait_ge(s_hid, e + 1)
                            silu(e + 1)
                            act.wait_ge(s_up, e + 1)
                            copy_rows(u, e + 2)
                            store(e, u, e)
                    for e in (NE - 2, NE - 1):
                        if e + 1 < NE:
                            act.wait_ge(s_hid, e + 1)
                            silu(e + 1)
                        store(e, e % 2, e)
                    for u in range(2):
                        act.wait_ge(s_yst[u], 16 * (NE // 2 + 1))

                @block.vector
                def _(dve):
                    link = linker(dve, s_dc)
                    nc.vector.memset(g_pad[:], -1e30)
                    for t in range(NT):
                        dve.wait_ge(s_rs, t + 1)
                        nc.vector.tensor_scalar(xhat[:, t, :], x[:, t, :], rstd[:, t:t + 1], None,
                                                ALU.mult).then_inc(s_xh, 1)
                    for k in range(KD):
                        ins = nc.vector.tensor_scalar(diag[:, k, :], ident[:], mod[:, l, G2 + k, 0:1], None, ALU.mult)
                    ins.then_inc(s_dg, 1)
                    for k in range(1, KD, 2):
                        dve.wait_ge(s_xt, k + 1)
                        ins = nc.vector.tensor_scalar(hT[:, k, :], bank[:, k % 4, :], norm_a[:, na, k:k + 1],
                                                      mod[:, l, SH2 + k, 0:1], ALU.mult, ALU.add)
                        ins.then_inc(s_htd, 1)
                    if l == 0:
                        dve.wait_ge(m_const, 16 * 5)
                    V = nc.vector
                    dve.wait_ge(s_sc, 1)
                    link(V.tensor_tensor(biased[:], score[:], router_b[:].unsqueeze(1).to_broadcast([P, NT, NE]), ALU.add))
                    v = biased[:].rearrange("p t (g a b) -> p (t g) a b", a=2, b=2)
                    V.tensor_tensor(g_hi[:], v[:, :, 0, :], v[:, :, 1, :], ALU.max)
                    link(V.tensor_tensor(g_lo[:], v[:, :, 0, :], v[:, :, 1, :], ALU.min))
                    V.tensor_tensor(g_t[:, 0, :], g_hi[:, :, 0], g_hi[:, :, 1], ALU.max)
                    V.tensor_tensor(g_t[:, 1, :], g_hi[:, :, 0], g_hi[:, :, 1], ALU.min)
                    link(V.tensor_tensor(g_t[:, 2, :], g_lo[:, :, 0], g_lo[:, :, 1], ALU.max))
                    link(V.tensor_tensor(g_t[:, 1, :], g_t[:, 1, :], g_t[:, 2, :], ALU.max))
                    link(V.tensor_tensor(g_pad[:, :, 0:NG], g_t[:, 0, :].rearrange("p (t g) -> p t g", g=NG),
                                         g_t[:, 1, :].rearrange("p (t g) -> p t g", g=NG), ALU.add))
                    for t in range(NT):
                        ins = V.max(top8[:, t, :], g_pad[:, t, :])
                    link(ins)
                    for t in range(NT):
                        ins = V.max_index(top8i[:, t, :], top8[:, t, :], g_pad[:, t, :])
                    link(ins)
                    link(V.tensor_copy(g_sel[:], top8i[:, :, 0]))
                    link(V.tensor_tensor(in_grp[:], krows[:, 1, :].unsqueeze(1).to_broadcast([P, NT, NE]),
                                         cols(g_sel[:], NE), ALU.is_equal))
                    V.tensor_scalar(r_tmp[:, 0], in_grp[:], -1.0, 1e30, ALU.add, ALU.mult)
                    link(V.tensor_tensor(masked[:], biased[:], in_grp[:], ALU.mult))
                    link(V.tensor_tensor(masked[:], masked[:], r_tmp[:, 0], ALU.add))
                    for t in range(NT):
                        ins = V.max(top8[:, t, :], masked[:, t, :])
                    link(ins)
                    for t in range(NT):
                        ins = V.max_index(top8i[:, t, :], top8[:, t, :], masked[:, t, :])
                    link(ins)
                    for c in range(2):
                        ins = V.tensor_copy(e_sel[:, c, :], top8i[:, :, c])
                    link(ins)
                    for c in range(2):
                        ins = V.tensor_tensor(pick[:, c], krows[:, 0, :].unsqueeze(1).to_broadcast([P, NT, NE]),
                                              cols(e_sel[:, c, :], NE), ALU.is_equal)
                    link(ins)
                    V.tensor_tensor(e_mask[:], pick[:, 0], pick[:, 1], ALU.add).then_inc(s_mask, 1)
                    for c in range(2):
                        ins = V.tensor_tensor(r_tmp[:, c], pick[:, c], score[:], ALU.mult)
                    link(ins)
                    link(V.tensor_reduce(weight[:], r_tmp[:], AX.X, ALU.add))
                    link(V.tensor_tensor(w_sum[:], weight[:, 0, :], weight[:, 1, :], ALU.add))
                    link(V.reciprocal(w_sum[:], w_sum[:]))
                    link(V.tensor_tensor(weight[:], weight[:], w_sum[:].unsqueeze(1).to_broadcast([P, 2, NT]), ALU.mult))
                    dve.wait_ge(s_pos, 1)
                    pos = bank[:, 5, 0:NT * NE].rearrange("p (t e) -> p t e", e=NE)
                    for c in range(2):
                        ins = V.tensor_tensor(r_tmp[:, c], pick[:, c], pos, ALU.mult)
                    link(ins)
                    link(V.tensor_reduce(place[:], r_tmp[:], AX.X, ALU.add))
                    V.scalar_tensor_tensor(row_tmp[:, 0], e_sel[:], float(P), place[:], ALU.mult, ALU.add)
                    link(V.tensor_scalar(row_tmp[:, 1], place[:], float(P), None, ALU.is_ge))
                    for b in range(2, SEQ // P):
                        link(V.scalar_tensor_tensor(row_tmp[:, 1], place[:], float(b * P), row_tmp[:, 1],
                                                    ALU.is_ge, ALU.add))
                    V.scalar_tensor_tensor(row_of[:], row_tmp[:, 1], float((NE - 1) * P), row_tmp[:, 0],
                                           ALU.mult, ALU.add)
                    V.scalar_tensor_tensor(entry_of[:], place[:], float(NE), e_sel[:], ALU.mult, ALU.add).then_inc(s_rows, 1)
                    V.tensor_reduce(max_count[:], bank[:, 5, NT * NE:(NT + 1) * NE], AX.X, ALU.max).then_inc(s_cnt, 1)

                    dve.wait_ge(s_grc, 1)
                    V.memset(idx_zero[:, 0:1], 0.0).then_inc(s_y, 1)
                    for u in range(2):
                        V.memset(idx_zero[:, u + 1:u + 2], 0.0).then_inc(s_yst[u], 16)

                    def hidden(n):
                        dve.wait_ge(s_up, n + 1)
                        dve.wait_ge(s_silu, n + 1)
                        V.tensor_tensor(hid, act_g, bank[:, 3, :], ALU.mult).then_inc(s_hid, 1)

                    def hidden_T(n):
                        dve.wait_ge(s_ht2, n + 1)
                        V.tensor_copy(hidT.rearrange("p k t -> p (k t)"), bank[:, 4, :]).then_inc(s_ht2c, 1)

                    def rows_out(n, u, uses):
                        dve.wait_ge(s_dn, n + 1)
                        dve.wait_ge(s_yst[u], uses)
                        V.tensor_tensor(y_sb[:, u, :], bank[:, 6:8, :].rearrange("p b c -> p (b c)"), gate2_b[:],
                                        ALU.mult).then_inc(s_y, 1)

                    hidden(0)
                    with dve.Fori(0, NE // 2 - 1) as i:
                        for u in range(2):
                            e = 2 * i + u
                            hidden_T(e)
                            hidden(e + 1)
                            rows_out(e, u, 16 * i + 16)
                    for e in (NE - 2, NE - 1):
                        hidden_T(e)
                        if e + 1 < NE:
                            hidden(e + 1)
                        rows_out(e, e % 2, 16 * (NE // 2))

                @block.tensor
                def _(pe):
                    pe.wait_ge(s_xh, NT)
                    for k in range(KD):
                        if k >= 4:
                            pe.wait_ge(s_hta if k % 2 == 0 else s_htd, (k - 4) // 2 + 1)
                        for t in range(NT):
                            last = pe.transpose(bank[:, k % 4, t * P:(t + 1) * P], xhat[:, t, k * P:(k + 1) * P], ident[:])
                        last.then_inc(s_xt, 1)
                    pe.wait_ge(s_hta, KD // 2)
                    pe.wait_ge(s_htd, KD // 2)
                    if l == 0:
                        pe.wait_ge(m_const, 16 * 5)
                    for t in range(NT):
                        for k in range(KD):
                            last = pe.matmul(bank[:, 4, t * NE:(t + 1) * NE], hT[:, k, t * P:(t + 1) * P], router_w[:, k, :],
                                             start=(k == 0), stop=(k == KD - 1))
                    last.then_inc(s_lg, 1)
                    pe.wait_ge(s_dg, 1)
                    for k in range(KD):
                        last = pe.matmul(bank[:, 6 + k // 4, (k % 4) * P:(k % 4 + 1) * P], ones[:], diag[:, k, :],
                                         start=True, stop=True)
                    last.then_inc(s_gr, 1)
                    pe.wait_ge(s_mask, 1)
                    for t in range(NT + 1):
                        for t2 in range(min(t + 1, NT)):
                            last = pe.matmul(bank[:, 5, t * NE:(t + 1) * NE], before[:] if t2 == t else ones[:],
                                             e_mask[:, t2, :], start=(t2 == 0), stop=(t2 == min(t, NT - 1)))
                    last.then_inc(s_pos, 1)
                    pe.wait_ge(s_cnt, 1)
                    pe.wait_ge(s_grc, 1)

                    def rows_T(u, gathered):
                        pe.wait_ge(s_xg[u], gathered)
                        for k in range(KD):
                            last = pe.transpose(bank[:, k // 4, (k % 4) * P:(k % 4 + 1) * P],
                                                xg[:, u, k * P:(k + 1) * P], ident[:])
                        last.then_inc(s_gt, 1)

                    def product(b, u, q, loaded, done):
                        s = 3 * u + q
                        pe.wait_ge(s_load[s], loaded)
                        w = slot(s).rearrange("p (k c) -> p k c", k=KD)
                        for k in range(KD):
                            last = pe.matmul(bank[:, b, :], xgT[:, u, k, :], w[:, k, :], start=(k == 0), stop=(k == KD - 1))
                        last.then_inc(done, 1)

                    def hid_T():
                        for k in range(KE):
                            last = pe.transpose(bank[:, 4, k * P:(k + 1) * P], hid[:, k * P:(k + 1) * P], ident[:])
                        last.then_inc(s_ht2, 1)

                    def down(u, loaded, n):
                        s = 3 * u + 2
                        pe.wait_ge(s_load[s], loaded)
                        pe.wait_ge(s_ht2c, n + 1)
                        pe.wait_ge(s_y, n + 1)
                        w = slot(s).rearrange("p (k c) -> p k c", k=KE)
                        for hf in range(2):
                            for k in range(KE):
                                last = pe.matmul(bank[:, 6 + hf, :], hidT[:, k, :], w[:, k, hf * HALF:(hf + 1) * HALF],
                                                 start=(k == 0), stop=(k == KE - 1))
                        last.then_inc(s_dn, 1)

                    rows_T(0, 16)
                    pe.wait_ge(s_gtc, 1)
                    rows_T(1, 16)
                    product(2, 0, 0, 16, s_gate)
                    product(3, 0, 1, 16, s_up)

                    def step(e, u, turn, last_gather):
                        nxt = 1 - u
                        loaded = 16 * turn + 16
                        nxt_loaded = loaded if u == 0 else loaded + 16
                        if not last_gather or u == 0:
                            pe.wait_ge(s_gtc, e + 2)
                            pe.wait_ge(s_silu, e + 1)
                            product(2, nxt, 0, nxt_loaded, s_gate)
                        pe.wait_ge(s_hid, e + 1)
                        hid_T()
                        if not last_gather:
                            rows_T(u, loaded + 16)
                        if not last_gather or u == 0:
                            product(3, nxt, 1, nxt_loaded, s_up)
                        down(u, loaded, e)

                    with pe.Fori(0, NE // 2 - 1) as i:
                        for u in range(2):
                            step(2 * i + u, u, i, False)
                    for u in range(2):
                        step(NE - 2 + u, u, NE // 2 - 1, True)

            stage_over()

            o_ = lambda s: sem(f"over{l}_{s}")
            v_ld, v_idx, v_xg = o_("weights"), o_("list"), o_("rows")
            v_t, v_tc, v_g, v_u, v_s, v_h = o_("rows_T"), o_("rows_T_copied"), o_("gate"), o_("up"), o_("silu"), o_("hid")
            v_h2, v_h2c, v_d, v_y, v_st = o_("hid_T"), o_("hid_T_copied"), o_("down"), o_("y"), o_("stored")
            v_small = o_("small_op")
            MORE = SEQ // P - 1
            lists4 = list_dram.rearrange("(b j e) o -> b j (e o)", j=P, e=NE)

            def blocks(eng):
                with eng.Fori(0, MORE) as b:
                    with eng.Fori(0, NE) as e:
                        yield e, b + 1, b * NE + e

            with nc.Block() as block:

                @block.sync
                def _(sp):
                    most = sp.value_load(max_count[0:1, 0:1])
                    with sp.If(most > P):
                        for e, b, n in blocks(sp):
                            sp.wait_ge(v_d, n + 1)
                            put(sp, wg, e, 0, KD).then_inc(v_ld, 16)
                            put(sp, wu, e, 1, KD).then_inc(v_ld, 16)
                            put(sp, wd, e, 2, KE).then_inc(v_ld, 16)

                @block.gpsimd
                def _(pool):
                    most = pool.value_load(max_count[0:1, 0:1])
                    with pool.If(most > P):
                        for e, b, n in blocks(pool):
                            pool.dma_start(idx[:, 0:1].bitcast(I32), lists4[bass.ds(b, 1), :, bass.ds(e, 1)]
                                           .rearrange("b j e -> (b j) e")).then_inc(v_idx, 16)
                            pool.wait_ge(v_idx, 16 * n + 16)
                            nc.gpsimd.tensor_tensor(idx_zero[:], idx_zero[:], idx_zero[:], ALU.add).then_inc(v_small, 1)
                            pool.indirect_dma_start(out=xg[:, 0, :], out_offset=None, in_=xh_dram,
                                                    in_offset=bass.IndirectOffsetOnAxis(ap=idx[:, 0:1], axis=0)
                                                    ).then_inc(v_xg, 16)
                            pool.wait_ge(v_t, n + 1)
                            pool.wait_ge(v_small, n + 1)

                @block.scalar
                def _(act):
                    most = act.value_load(max_count[0:1, 0:1])
                    with act.If(most > P):
                        for e, b, n in blocks(act):
                            act.wait_ge(v_t, n + 1)
                            for k in range(KD):
                                last = nc.scalar.activation(xgT[:, 0, k, :], bank[:, k // 4, (k % 4) * P:(k % 4 + 1) * P],
                                                            ACT.Identity, scale=norm_a[:, na, k:k + 1],
                                                            bias=mod[:, l, SH2 + k, 0:1])
                            last.then_inc(v_tc, 1)
                            act.wait_ge(v_g, n + 1)
                            nc.scalar.activation(act_g, bank[:, 2, :], ACT.Silu).then_inc(v_s, 1)
                            act.wait_ge(v_y, n + 1)
                            act.dma_start(y_dram[bass.ds((b * NE + e) * P, P), :], y_sb[:, 0, :]).then_inc(v_st, 16)
                            act.wait_ge(v_st, 16 * n + 16)

                @block.vector
                def _(dve):
                    most = dve.value_load(max_count[0:1, 0:1])
                    with dve.If(most > P):
                        for e, b, n in blocks(dve):
                            dve.wait_ge(v_u, n + 1)
                            dve.wait_ge(v_s, n + 1)
                            nc.vector.tensor_tensor(hid, act_g, bank[:, 3, :], ALU.mult).then_inc(v_h, 1)
                            dve.wait_ge(v_h2, n + 1)
                            nc.vector.tensor_copy(hidT.rearrange("p k t -> p (k t)"), bank[:, 4, :]).then_inc(v_h2c, 1)
                            dve.wait_ge(v_d, n + 2)
                            nc.vector.tensor_tensor(y_sb[:, 0, :], bank[:, 6:8, :].rearrange("p b c -> p (b c)"),
                                                    gate2_b[:], ALU.mult).then_inc(v_y, 1)
                            dve.wait_ge(v_st, 16 * n + 16)

                @block.tensor
                def _(pe):
                    most = pe.value_load(max_count[0:1, 0:1])
                    with pe.If(most > P):
                        pe.transpose(bank[:, 5, 0:P], ident[:], ident[:]).then_inc(v_d, 1)
                        for e, b, n in blocks(pe):
                            pe.wait_ge(v_xg, 16 * n + 16)
                            for k in range(KD):
                                last = pe.transpose(bank[:, k // 4, (k % 4) * P:(k % 4 + 1) * P],
                                                    xg[:, 0, k * P:(k + 1) * P], ident[:])
                            last.then_inc(v_t, 1)
                            pe.wait_ge(v_tc, n + 1)
                            pe.wait_ge(v_ld, 48 * n + 48)
                            for q, done in ((0, v_g), (1, v_u)):
                                w = slot(q).rearrange("p (k c) -> p k c", k=KD)
                                for k in range(KD):
                                    last = pe.matmul(bank[:, 2 + q, :], xgT[:, 0, k, :], w[:, k, :],
                                                     start=(k == 0), stop=(k == KD - 1))
                                last.then_inc(done, 1)
                            pe.wait_ge(v_h, n + 1)
                            for k in range(KE):
                                last = pe.transpose(bank[:, 4, k * P:(k + 1) * P], hid[:, k * P:(k + 1) * P], ident[:])
                            last.then_inc(v_h2, 1)
                            pe.wait_ge(v_h2c, n + 1)
                            w = slot(2).rearrange("p (k c) -> p k c", k=KE)
                            for hf in range(2):
                                for k in range(KE):
                                    last = pe.matmul(bank[:, 6 + hf, :], hidT[:, k, :], w[:, k, hf * HALF:(hf + 1) * HALF],
                                                     start=(k == 0), stop=(k == KE - 1))
                            last.then_inc(v_d, 1)
                            pe.wait_ge(v_st, 16 * n + 16)

            stage_over()

            c_y = [[sem(f"comb{l}_rows{c}_{t}") for t in range(NT)] for c in range(2)]
            c_ch = sem(f"comb{l}_chain")
            rows, at = carve(moe0, 2, NT, D)

            with nc.Block() as block:

                @block.gpsimd
                def _(pool):
                    def fetch_rows(written):
                        for t in range(NT):
                            for c in range(2):
                                pool.indirect_dma_start(
                                    out=rows[:, c, t, :], out_offset=None, in_=y_dram[0:written, :],
                                    in_offset=bass.IndirectOffsetOnAxis(ap=row_of[:, c, t:t + 1], axis=0)
                                ).then_inc(c_y[c][t], 16)

                    most = pool.value_load(max_count[0:1, 0:1])
                    with pool.If(most > P):
                        fetch_rows(LIST_N)
                    with pool.Else():
                        fetch_rows(NE * P)

                @block.vector
                def _(dve):
                    link = linker(dve, c_ch)
                    for t in range(NT):
                        for c in range(2):
                            dve.wait_ge(c_y[c][t], 16)
                            link(nc.vector.scalar_tensor_tensor(x[:, t, :], rows[:, c, t, :], weight[:, c, t:t + 1],
                                                                x[:, t, :], ALU.mult, ALU.add))

            stage_over()

        idx_zero = sb("credit", [1, 3])

        moe(0)

        bands, at = carve(0, len(WINDOWS), 5, P)
        pool_w, at = carve(at, len(WINDOWS), 2, 2 * P)
        xhat, at = carve(at, NT, D)
        pooledT, at = carve(at, KD, SEQ)
        diag2, at = carve(at, KD, P)
        upd2, at = carve(at, HALF)
        p_ = lambda s: sem(f"pool_{s}")
        p_ld, p_sq, p_rs, p_xh, p_pl, p_plc = p_("tables"), p_("square_sum"), p_("rstd"), p_("xhat"), p_("pooled"), p_("pooled_copied")
        p_dg, p_gr, p_grc, p_mx, p_xr, p_dc, p_pc = (p_("diag"), p_("gate_rows"), p_("gate_rows_copied"), p_("mixed"),
                                                     p_("x_updated"), p_("dve_chain"), p_("pool_chain"))

        with nc.Block() as block:

            @block.sync
            def _(sp):
                sp.dma_start(bands.rearrange("p g b c -> p (g b c)"), a["k_bands"]).then_inc(p_ld, 16)
                sp.dma_start(pool_w.rearrange("p g k c -> p (g k) c"),
                             a["pool_w"][0].rearrange("g (k p) c -> p (g k) c", p=P)).then_inc(p_ld, 16)

            @block.scalar
            def _(act):
                for t in range(NT):
                    nc.scalar.activation(xhat[:, t, :], x[:, t, :], ACT.Square,
                                         accum_out=stats[:, t:t + 1]).then_inc(p_sq, 1)
                act.wait_ge(p_gr, 1)
                nc.scalar.copy(gate1_b[:], bank[:, 6:8, :].rearrange("p b c -> p (b c)")).then_inc(p_grc, 1)
                for k in range(KD):
                    act.wait_ge(p_pl, k + 1)
                    nc.scalar.mul(pooledT[:, k, :], bank[:, k % 4, :], norm_a[:, 3, k:k + 1]).then_inc(p_plc, 1)

            @block.gpsimd
            def _(pool):
                link = linker(pool, p_pc)
                for t in range(NT):
                    pool.wait_ge(p_sq, t + 1)
                    link(nc.gpsimd.tensor_scalar(rstd[:, t:t + 1], stats[:, t:t + 1], 1.0 / D, EPS, ALU.mult, ALU.add))
                    nc.gpsimd.tensor_tensor(rstd[:, t:t + 1], rstd[:, t:t + 1], minus_half[:, 0:1],
                                            ALU.pow).then_inc(p_rs, 1)

            @block.vector
            def _(dve):
                link = linker(dve, p_dc)
                for k in range(KD):
                    ins = nc.vector.tensor_scalar(diag2[:, k, :], ident[:], mod[:, 1, G1 + k, 0:1], None, ALU.mult)
                ins.then_inc(p_dg, 1)
                for t in range(NT):
                    dve.wait_ge(p_rs, t + 1)
                    nc.vector.tensor_scalar(xhat[:, t, :], x[:, t, :], rstd[:, t:t + 1], None, ALU.mult).then_inc(p_xh, 1)
                dve.wait_ge(p_grc, 1)
                for n in range(2 * NT):
                    hf, t = n // NT, n % NT
                    dve.wait_ge(p_mx, n + 1)
                    if n >= 1:
                        dve.wait_ge(p_xr, n)
                    link(nc.vector.tensor_tensor(upd2, bank[:, 4 + n % 2, :], gate1_b[:, hf * HALF:(hf + 1) * HALF],
                                                 ALU.mult))
                    xs = x[:, t, hf * HALF:(hf + 1) * HALF]
                    nc.vector.tensor_tensor(xs, xs, upd2, ALU.add).then_inc(p_xr, 1)

            @block.tensor
            def _(pe):
                pe.wait_ge(p_dg, 1)
                for k in range(KD):
                    last = pe.matmul(bank[:, 6 + k // 4, (k % 4) * P:(k % 4 + 1) * P], ones[:], diag2[:, k, :],
                                     start=True, stop=True)
                last.then_inc(p_gr, 1)
                pe.wait_ge(p_ld, 32)
                pe.wait_ge(p_xh, NT)
                for k in range(KD):
                    if k >= 4:
                        pe.wait_ge(p_plc, k - 3)
                    g = k // 2
                    for t in range(NT):
                        near = [(t2, b) for t2, b in ((t - 1, 3), (t, 0 if t == 0 else 2 if t == NT - 1 else 1), (t + 1, 4))
                                if 0 <= t2 < NT]
                        for n, (t2, b) in enumerate(near):
                            last = pe.matmul(bank[:, k % 4, t * P:(t + 1) * P], xhat[:, t2, k * P:(k + 1) * P],
                                             bands[:, g, b, :], start=(n == 0), stop=(n == len(near) - 1))
                    last.then_inc(p_pl, 1)
                pe.wait_ge(p_plc, KD)
                for n in range(2 * NT):
                    hf, t = n // NT, n % NT
                    if n >= 2:
                        pe.wait_ge(p_xr, n - 1)
                    for g in (2 * hf, 2 * hf + 1):
                        c0 = (g % 2) * 2 * P
                        for k in range(2):
                            last = pe.matmul(bank[:, 4 + n % 2, c0:c0 + 2 * P], pooledT[:, 2 * g + k, t * P:(t + 1) * P],
                                             pool_w[:, g, k, :], start=(k == 0), stop=(k == 1))
                    last.then_inc(p_mx, 1)

        stage_over()

        moe(1)

        f_ld, f_sq, f_rs, f_o, f_st, f_pc = (sem(f"fin_{s}") for s in
                                             ("weight", "square_sum", "rstd", "out", "stored", "pool_chain"))
        fin_w, at = carve(0, D)
        fin, at = carve(at, NT, D)

        with nc.Block() as block:

            @block.sync
            def _(sp):
                sp.dma_start(fin_w, a["final_norm_w"].partition_broadcast(P)).then_inc(f_ld, 16)
                for t in range(NT):
                    sp.wait_ge(f_o, t + 1)
                    sp.dma_start(out[0, t * P:(t + 1) * P, :], fin[:, t, :]).then_inc(f_st, 16)
                sp.wait_ge(f_st, 16 * NT)

            @block.scalar
            def _(act):
                for t in range(NT):
                    nc.scalar.activation(fin[:, t, :], x[:, t, :], ACT.Square, accum_out=stats[:, t:t + 1]).then_inc(f_sq, 1)

            @block.gpsimd
            def _(pool):
                link = linker(pool, f_pc)
                for t in range(NT):
                    pool.wait_ge(f_sq, t + 1)
                    link(nc.gpsimd.tensor_scalar(rstd[:, t:t + 1], stats[:, t:t + 1], 1.0 / D, EPS, ALU.mult, ALU.add))
                    nc.gpsimd.tensor_tensor(rstd[:, t:t + 1], rstd[:, t:t + 1], minus_half[:, 0:1],
                                            ALU.pow).then_inc(f_rs, 1)

            @block.vector
            def _(dve):
                dve.wait_ge(f_ld, 16)
                for t in range(NT):
                    dve.wait_ge(f_rs, t + 1)
                    nc.vector.scalar_tensor_tensor(fin[:, t, :], x[:, t, :], rstd[:, t:t + 1], fin_w,
                                                   ALU.mult, ALU.mult).then_inc(f_o, 1)


_INS = ['x', 'c', 'ctx', 'c_ctx', 'ada_w', 'ada_b', 'norm_mix_w', 'norm_ffn_w', 'w_in', 'w_out', 'ret_log_decay',
        'diff_lambda', 'diff_subln_w', 'pool_w', 'pool_scale', 'router_w', 'router_b', 'moe_w_gate', 'moe_w_up',
        'moe_w_down', 'final_norm_w']


def kernel(**inputs):
    import concourse.bacc as bacc
    from concourse.bass_utils import run_bass_kernel_spmd

    nc = bacc.Bacc("TRN2", target_bir_lowering=False, num_devices=1)
    arrays = {f"in_{n}": np.ascontiguousarray(inputs[n]) for n in _INS}
    arrays.update(constants())
    aps = {}
    for name, arr in arrays.items():
        ap = nc.dram_tensor(name, arr.shape, mybir.dt.from_np(arr.dtype), kind="ExternalInput").ap()
        aps[name.removeprefix("in_")] = ap
    out = nc.dram_tensor("out_0", (1, SEQ, D), F32, kind="ExternalOutput").ap()
    build_program(nc, aps, out)
    r = run_bass_kernel_spmd(nc, [arrays], core_ids=[0])
    return r.results[0]["out_0"]
```

```python
from contextlib import ExitStack
import math

import numpy as np

import concourse.bass as bass
from concourse import mybir

ALU = mybir.AluOpType
ACT = mybir.ActivationFunctionType
AX = mybir.AxisListType
F32 = mybir.dt.float32
I32 = mybir.dt.int32
U32 = mybir.dt.uint32
I16 = mybir.dt.int16

P = 128
D, SEQ, CTX, DEPTH = 1024, 512, 256, 2
KD = D // P
NT, NC = SEQ // P, CTX // P
NK = NT + NC
HEADS, DK, DV = 4, 64, 128
NE, NG, DE = 16, 4, 512
KE = DE // P
HALF = 512
EPS = 1e-6
LAM_INIT = 0.8 - 0.6 * math.exp(-0.3 * 0)
WINDOWS = (2, 4, 8, 16)
GRID_W = 64
SLOT_W = 4096
GAP_W = SEQ + 7 * P
GAP_0 = 5 * P
LIST_N = NE * SEQ

SH1, SC1, G1, SH2, SC2, G2 = range(6)
C_ROW, CC_ROW, NM_ROW, SMALL_ROWS = 0, KD, 2 * KD, 3 * KD


def constants():
    half = DK // 4
    inv = 10000.0 ** (-np.arange(half, dtype=np.float32) / np.float32(half))
    pos = np.arange(SEQ)
    tables = []
    for p in (pos // GRID_W, pos % GRID_W):
        ang = p.astype(np.float32)[:, None] * inv.astype(np.float32)[None, :]
        tables.append((np.cos(ang), np.sin(ang)))
    rope_cos = np.concatenate([tables[0][0], tables[0][0], tables[1][0], tables[1][0]], 1)
    rope_sin = np.concatenate([-tables[0][1], tables[0][1], -tables[1][1], tables[1][1]], 1)
    gap = (np.arange(GAP_W) - GAP_0)[None, :] - np.arange(P)[:, None]
    before = np.triu(np.ones((P, P), np.float32), 1)
    bands = np.zeros((P, len(WINDOWS), 5, P), np.float32)
    for g, w in enumerate(WINDOWS):
        left, right = w // 2, w - 1 - w // 2
        full = np.zeros((SEQ, SEQ), np.float64)
        for t in range(SEQ):
            lo, hi = max(t - left, 0), min(t + right + 1, SEQ)
            full[lo:hi, t] = 1.0 / (hi - lo)
            full[t, t] -= 1.0
        for b, (a, t) in enumerate([(0, 0), (1, 1), (NT - 1, NT - 1), (0, 1), (2, 1)]):
            bands[:, g, b] = full[a * P:(a + 1) * P, t * P:(t + 1) * P]
    rows = np.zeros((2, NE), np.float32)
    rows[0] = np.arange(NE)
    rows[1] = np.arange(NE) // (NE // NG)
    token = np.arange(SEQ, dtype=np.int32).reshape(NT, P).T
    return {
        "k_ident": np.eye(P, dtype=np.float32), "k_cos": rope_cos.astype(np.float32),
        "k_sin": rope_sin.astype(np.float32), "k_gap": gap.astype(np.int16), "k_before": before,
        "k_bands": bands.reshape(P, -1), "k_rows": rows, "k_token": np.ascontiguousarray(token),
        "k_places": np.arange(P, dtype=np.float32)[None, :],
        "k_zero": np.zeros((P, LIST_N // P), np.int32),
    }


def build_program(nc, a, out):
    ctx = ExitStack()
    with ctx, nc.allow_non_contiguous_dma(reason="short rows of small tables"):
        def sb(name, shape, dt=F32):
            return ctx.enter_context(nc.sbuf_tensor(name, shape, dt))

        ring_load = [nc.alloc_semaphore(name=f"ring_slot{i}_loaded") for i in range(6)]
        ring_uses = [0] * 6
        held = []

        def sem(name):
            held.append(nc.alloc_semaphore(name=name))
            return held[-1]

        def stage_over():
            nc.clear_and_free_semaphores(list(held))
            held.clear()
            nc.all_engine_barrier()

        xh_dram = nc.dram_tensor("xh_scratch", [SEQ, D], F32).ap()
        list_dram = nc.dram_tensor("list_scratch", [LIST_N, 1], I32).ap()
        y_dram = nc.dram_tensor("y_scratch", [LIST_N, D], F32).ap()
        mod_dram = nc.dram_tensor("mod_scratch", [DEPTH, 6 * D], F32).ap()

        def mod_row(l, part):
            return mod_dram[l, part * D:(part + 1) * D].partition_broadcast(P)

        bank = ctx.enter_context(nc.psum_tensor("bank", [P, 8, HALF], F32))

        x = sb("x_res", [P, NT, D])
        ident = sb("ident", [P, P])
        ones = sb("ones", [P, P])
        small = sb("small", [P, SMALL_ROWS])
        bias_cols = sb("bias_cols", [P, 2 * KD])
        silu_c = sb("silu_c", [P, 2, KD])
        mod = sb("mod", [P, 2 * KD, 2])
        norm_a = sb("norm_a", [P, 2, KD])
        gate1_b = sb("gate1_b", [P, D])
        gate2_b = sb("gate2_b", [P, D])
        stats = sb("stats", [P, 8])
        rstd = sb("rstd", [P, 8])
        minus_half = sb("minus_half", [P, NT])
        ring = sb("ring", [P, 4, SLOT_W])
        ARENA = 28672
        arena = sb("arena", [P, ARENA])

        def carve(start, *dims):
            n = int(np.prod(dims))
            assert start + n <= ARENA, (start, n)
            v = arena[:, start:start + n]
            if len(dims) > 1:
                names = " ".join(f"d{i}" for i in range(len(dims)))
                v = v.rearrange(f"p ({names}) -> p {names}", **{f"d{i}": d for i, d in enumerate(dims)})
            return v, start + n

        def linker(eng, s):
            n = [0]

            def link(ins):
                n[0] += 1
                ins.then_inc(s, 1)
                eng.wait_ge(s, n[0])
            return link

        def cols(ap, width):
            return ap.unsqueeze(2).to_broadcast([P, ap.shape[1], width])

        qT, at = carve(0, 6, SEQ)
        kT, at = carve(at, 6, NK * P)
        v_tok, at = carve(at, NK, 2 * HEADS * DV)
        gate, late = carve(at, NT, HEADS * DV)
        hT, at = carve(late, KD, SEQ)
        hcT, at = carve(at, KD, CTX)
        xhat2, at = carve(at, 2, D)
        ctx_raw, at = carve(at, NC, D)
        at_rope = at
        rope_x, at = carve(at, HALF)
        rope_y, at = carve(at, HALF)
        roped, at = carve(at, 2, HALF)
        cos_t, at = carve(at, NT, DK)
        sin_t, at = carve(at, NT, DK)
        decay, at = carve(late, 2, GAP_W)
        decay_c, at = carve(at, NC, SEQ)
        retp, _ = carve(at, 4, SEQ)
        prob, at = carve(at, 2, 2, NK * P)
        diffp, at = carve(at, NK * P)
        diffT, at = carve(at, NK, P)
        dif_out, at = carve(at, NT, HEADS * DV)
        squares, at = carve(at, NT, DV)
        decay_arg, at = carve(at, P)
        lam_pr, at = carve(at, 2, DK)
        hstat, at = carve(at, 2 * HEADS, NT)
        hrstd, at = carve(at, 2 * HEADS, NT)
        ada_acc = gate2_b[:].rearrange("p (b c) -> p b c", b=2)
        ada_first = sb("ada_first", [P, HALF])
        ada_row = sb("ada_row", [1, HALF])
        mixT = kT.rearrange("p a b -> p (a b)")[:, 0:KD * SEQ].rearrange("p (k t) -> p k t", k=KD)

        gap = gate1_b[:, 0:GAP_W // 2].bitcast(I16)
        gap_pos = gate1_b[:, GAP_W // 2:GAP_W // 2 + P]
        gap_neg = gate1_b[:, GAP_W // 2 + P:GAP_W // 2 + 2 * P]
        ld = sb("ld", [P, 2 * HEADS])
        ld_neg = sb("ld_neg", [P, 2 * HEADS])
        lam_in = sb("lam_in", [P, 4 * DK])
        lam_s = sb("lam_s", [P, 2])
        lam_e = sb("lam_e", [P, 2])
        lam_v = sb("lam_v", [P, 2])
        subln = sb("subln", [P, DV])
        smax = sb("smax", [P, 2, 2])
        sden = sb("sden", [P, 2, 2])
        srec = sb("srec", [P, 2, 2])

        w_in, w_out, ada_w = a["w_in"], a["w_out"], a["ada_w"]

        def slot(i):
            return ring[:, i, :] if i < 4 else arena[:, (i - 4) * SLOT_W:(i - 3) * SLOT_W]

        def put(eng, w, e, i, k):
            src = w[bass.ds(e, 1)].rearrange("a (k p) c -> p (a k) c", p=P)
            return eng.dma_start(slot(i).rearrange("p (k c) -> p k c", k=k), src)

        def slab(w, c0):
            return w[:, c0:c0 + HALF].rearrange("(k p) c -> p k c", p=P)

        PRE = 2 * D // HALF
        rest = [(0, j) for j in range(PRE, 12)] + [(1, j) for j in range(12)]
        REST_PER = 4

        units = [(j, t) for j in range(6) for t in range(NK if j >= 2 else NT)]

        def parts(j, t):
            p = {0: [(0, 256, "q", 0), (256, 256, "q", 2)], 1: [(0, 256, "q", 4), (256, 256, "g", 0)],
                 2: [(0, 256, "g", 256), (256, 256, "k", 0)], 3: [(0, 512, "v", 0)],
                 4: [(0, 512, "k", 2)], 5: [(0, 512, "v", 512)]}[j]
            return [q for q in p if t < NT or q[2] not in "qg"]

        slabs_after, rows_after = {}, {}
        for i in range(len(rest)):
            u = int(1.45 * i)
            slabs_after.setdefault(u, []).append(i)
            rows_after.setdefault(u + 2, []).append(i)
        assert max(rows_after) < len(units)
        roped_units = [u for u, (j, t) in enumerate(units) if any(q[2] in "qk" for q in parts(j, t))]
        gate_units = [u for u, (j, t) in enumerate(units) if any(q[2] == "g" for q in parts(j, t))]
        v_units = [u for u, (j, t) in enumerate(units) if any(q[2] == "v" for q in parts(j, t))]

        m_ld = {n: sem(f"m_ld_{n}") for n in ("ident", "smallA", "smallB", "rope", "row", "gap", "zero")}
        m_x = [sem(f"m_x{t}") for t in range(NK)]
        m_small = sem("m_small_transposed")
        m_cols = sem("m_small_cols")
        m_silu = sem("m_silu_c")
        m_slot = [sem(f"m_slot{i}_loaded") for i in range(4)]
        m_pre = sem("m_adaln_rows_of_slab")
        m_prc = sem("m_adaln_rows_copied")
        m_prt = sem("m_adaln_rows_transposed")
        m_az = sem("m_adaln_first_zeroed")
        m_ab = sem("m_adaln_bias_loaded")
        m_au = sem("m_adaln_bias_used")
        m_ach = sem("m_adaln_product")
        m_as = sem("m_adaln_slab_summed")
        m_ar = sem("m_adaln_row")
        m_arc = sem("m_adaln_row_copied")
        m_ast = sem("m_adaln_row_stored")
        m_g1 = sem("m_g1_loaded")
        m_na = sem("m_norm_a_ready")
        m_sq = sem("m_square_sum")
        m_rs = sem("m_rstd")
        m_xh = sem("m_xhat")
        m_xt = sem("m_xhat_transposed")
        m_hta = sem("m_hT_by_act")
        m_htd = sem("m_hT_by_dve")
        m_proj = sem("m_projected")
        m_rope = sem("m_roped")
        m_gv = sem("m_gate_or_v_copied")
        m_qkt = sem("m_qk_transposed")
        m_qkc = sem("m_qk_copied")
        m_dchain = sem("m_dve_chain")
        m_pchain = sem("m_pool_chain")
        m_achain = sem("m_act_chain")
        m_lam = sem("m_lambda_sums")
        m_lame = sem("m_lambda_exps")
        m_gapc = sem("m_decay_args")
        m_dk_arg = sem("m_decay_arg")
        m_dk = sem("m_decay_exp")
        m_dkd = sem("m_decay_ready")
        m_rs_s = sem("m_ret_scores")
        m_rs_p = sem("m_ret_masked")
        m_rs_v = sem("m_ret_values_done")
        m_o = sem("m_head_out")
        m_osq = sem("m_head_squares")
        m_ost = sem("m_head_stat")
        m_orr = sem("m_head_rstd")
        m_on = sem("m_head_normed")
        m_ds = sem("m_diff_scores")
        m_dm = sem("m_diff_max")
        m_de = sem("m_diff_exp")
        m_dp = sem("m_diff_combined")
        m_dt = sem("m_diff_transposed")
        m_dc = sem("m_diff_copied")
        m_mt = sem("m_mix_transposed")
        m_mtc = sem("m_mix_copied")
        m_op = sem("m_out_projected")
        m_xr = sem("m_x_updated")
        m_mset = sem("m_memsets")

        RU = HEADS * NK
        DU = HEADS * NT

        def pair(c):
            return bank[:, 2 * c:2 * c + 2, :].rearrange("p b c -> p (b c)")[:, 0:NK * P]

        tr_diff = bank[:, 4:6, :].rearrange("p b c -> p (b c)")[:, 0:NK * P]

        upd = qT.rearrange("p a b -> p (a b)")[:, 0:HALF]
        pre_rows = arena[0:2, at_rope:at_rope + 2 * D]

        with nc.Block() as block:

            @block.sync
            def _(sp):
                def load(i, w, j, k=KD):
                    return sp.dma_start(ring[:, i, :].rearrange("p (k c) -> p k c", k=k), slab(w, j * HALF)
                                        ).then_inc(ring_load[i], 16)

                for j in range(PRE):
                    load(j, ada_w[0], j)
                sp.wait_ge(m_pre, 3)
                load(2, w_in[0], 0)
                sp.wait_ge(m_pre, 4)
                load(3, w_in[0], 1)
                sp.wait_ge(m_az, 1)
                for i, (l, j) in enumerate(rest):
                    if i >= 2:
                        sp.wait_ge(m_as, i - 1)
                    load(i % 2, ada_w[l], j)
                    if i >= 1:
                        sp.wait_ge(m_au, i)
                    sp.dma_start(ada_first[0:1, :], a["ada_b"][l:l + 1, j * HALF:(j + 1) * HALF]).then_inc(m_ab, 16)
                    if i % REST_PER == REST_PER - 1 and i // REST_PER < 4:
                        n = i // REST_PER
                        sp.wait_ge(m_proj, max(u for u, (s, _) in enumerate(units) if s == n) + 1)
                        load(2 + n % 2, w_in[0], n + 2)
                for j in range(2):
                    sp.wait_ge(m_proj, max(u for u, (s, _) in enumerate(units) if s == 4 + j) + 1)
                    load(2 + j, w_out[0], j)
                sp.wait_ge(m_dk, 2 * HEADS)
                sp.wait_ge(m_ast, 16 * len(rest))
                sp.dma_start(gate1_b[:], mod_row(0, G1)).then_inc(m_g1, 16)
                sp.wait_ge(m_as, len(rest))
                put(sp, a["moe_w_gate"][0], 0, 0, KD).then_inc(ring_load[0], 16)
                put(sp, a["moe_w_up"][0], 0, 1, KD).then_inc(ring_load[1], 16)
                sp.wait_ge(m_op, NT)
                put(sp, a["moe_w_down"][0], 0, 2, KE).then_inc(ring_load[2], 16)
                sp.wait_ge(m_op, 2 * NT)
                put(sp, a["moe_w_gate"][0], 1, 3, KD).then_inc(ring_load[3], 16)

            @block.scalar
            def _(act):
                link = linker(act, m_achain)
                act.dma_start(ident[:], a["k_ident"]).then_inc(m_ld["ident"], 16)
                for r0, src in ((C_ROW, a["c"][0]), (CC_ROW, a["c_ctx"]), (NM_ROW, a["norm_mix_w"][0])):
                    act.dma_start(arena[r0:r0 + KD, 0:P], src.rearrange("(r c) -> r c", c=P)).then_inc(m_ld["smallA"], 16)
                act.dma_start(arena[0:2 * KD, P:2 * P],
                              a["ada_b"][0, 0:2 * D].rearrange("(r c) -> r c", c=P)).then_inc(m_ld["smallB"], 16)
                for t in range(NK):
                    if t < NT:
                        act.dma_start(x[:, t, :], a["x"][0, t * P:(t + 1) * P, :]).then_inc(m_x[t], 16)
                    else:
                        act.dma_start(ctx_raw[:, t - NT, :],
                                      a["ctx"][0, (t - NT) * P:(t - NT + 1) * P, :]).then_inc(m_x[t], 16)
                act.dma_start(cos_t, a["k_cos"].rearrange("(t p) c -> p t c", p=P)).then_inc(m_ld["rope"], 16)
                act.dma_start(sin_t, a["k_sin"].rearrange("(t p) c -> p t c", p=P)).then_inc(m_ld["rope"], 16)
                act.dma_start(gap, a["k_gap"]).then_inc(m_ld["gap"], 16)
                act.dma_start(list_dram.rearrange("(p c) o -> p (c o)", p=P), a["k_zero"]).then_inc(m_ld["zero"], 16)
                act.dma_start(ld[:], a["ret_log_decay"].rearrange("n d h -> n (d h)").partition_broadcast(P)
                              .rearrange("p n c -> p (n c)")).then_inc(m_ld["row"], 16)
                act.dma_start(lam_in[:], a["diff_lambda"].rearrange("n d h -> n (d h)").partition_broadcast(P)
                              .rearrange("p n c -> p (n c)")).then_inc(m_ld["row"], 16)
                act.dma_start(subln[:], a["diff_subln_w"].partition_broadcast(P)
                              .rearrange("p n c -> p (n c)")).then_inc(m_ld["row"], 16)
                act.wait_ge(m_cols, 1)
                nc.scalar.activation(silu_c[:].rearrange("p v k -> p (v k)"), small[:, C_ROW:C_ROW + 2 * KD],
                                     ACT.Silu).then_inc(m_silu, 1)

                def squares_of(t):
                    act.wait_ge(m_x[t], 16)
                    if t >= 2:
                        act.wait_ge(m_xt, t - 1)
                    src = x[:, t, :] if t < NT else ctx_raw[:, t - NT, :]
                    nc.scalar.activation(xhat2[:, t % 2, :], src, ACT.Square,
                                         accum_out=stats[:, t:t + 1]).then_inc(m_sq, 1)

                def hT_of(t):
                    act.wait_ge(m_xt, t + 1)
                    act.wait_ge(m_na, 1)
                    v, na = (0, 0) if t < NT else (1, 1)
                    for k in range(KD // 2):
                        dst = hT[:, k, t * P:(t + 1) * P] if t < NT else hcT[:, k, (t - NT) * P:(t - NT + 1) * P]
                        last = nc.scalar.activation(dst, bank[:, (t % 2) * 2 + k // 4, (k % 4) * P:(k % 4 + 1) * P],
                                                    ACT.Identity, scale=norm_a[:, na, k:k + 1],
                                                    bias=mod[:, k, v:v + 1])
                    last.then_inc(m_hta, 1)

                squares_of(0)
                squares_of(1)
                for t in range(NK):
                    hT_of(t)
                    if t + 2 < NK:
                        squares_of(t + 2)

                def copy_qk(r):
                    j, t = units[roped_units[r]]
                    act.wait_ge(m_qkt, r + 1)
                    for c0, w, kind, b0 in parts(j, t):
                        if kind in "qk":
                            dst = (qT if kind == "q" else kT)[:, b0:b0 + w // P, t * P:(t + 1) * P]
                            last = nc.scalar.copy(dst, bank[:, 4 + r % 2, c0:c0 + w].rearrange("p (b c) -> p b c", c=P))
                    last.then_inc(m_qkc, 1)

                def copy_ada_row(i):
                    act.wait_ge(m_ar, i + 1)
                    if i >= 1:
                        act.wait_ge(m_ast, 16 * i)
                    nc.scalar.copy(ada_row[:], bank[0:1, 6 + i % 2, :]).then_inc(m_arc, 1)
                    act.wait_ge(m_arc, i + 1)
                    l, j = rest[i]
                    act.dma_start(mod_dram[l:l + 1, j * HALF:(j + 1) * HALF], ada_row[:]).then_inc(m_ast, 16)

                r = 0
                for u, (j, t) in enumerate(units):
                    for c0, w, kind, b0 in parts(j, t):
                        if kind not in "gv":
                            continue
                        act.wait_ge(m_proj, u + 1)
                        if u in roped_units:
                            act.wait_ge(m_rope, roped_units.index(u) + 1)
                        ps = bank[:, u % 3, c0:c0 + w]
                        if kind == "g":
                            nc.scalar.activation(gate[:, t, b0:b0 + w], ps, ACT.Silu).then_inc(m_gv, 1)
                        else:
                            nc.scalar.copy(v_tok[:, t, b0:b0 + w], ps).then_inc(m_gv, 1)
                    while r < len(roped_units) and roped_units[r] <= u - 1:
                        copy_qk(r)
                        r += 1
                    for i in rows_after.get(u - 1, ()):
                        copy_ada_row(i)
                for i in rows_after.get(len(units) - 1, ()):
                    copy_ada_row(i)
                while r < len(roped_units):
                    copy_qk(r)
                    r += 1

                act.wait_ge(m_lam, 1)
                nc.scalar.activation(lam_e[:], lam_s[:], ACT.Exp).then_inc(m_lame, 1)

                def decay_of(h):
                    act.wait_ge(m_proj, len(units))
                    if h >= 2:
                        act.wait_ge(m_rs_p, NK * (h - 1))
                    d = decay[:, h % 2, :]
                    nc.scalar.activation(d[:, GAP_0 + P:], gap[:, GAP_0 + P:], ACT.Exp, scale=ld[:, h:h + 1])
                    nc.scalar.activation(d[:, 0:GAP_0], gap[:, 0:GAP_0], ACT.Exp,
                                         scale=ld_neg[:, HEADS + h:HEADS + h + 1]).then_inc(m_dk, 1)
                    act.wait_ge(m_dk_arg, h + 1)
                    nc.scalar.activation(d[:, GAP_0:GAP_0 + P], decay_arg, ACT.Exp).then_inc(m_dk, 1)

                def head_squares(n):
                    if n < HEADS:
                        act.wait_ge(m_rs_v, NK * (n + 1))
                    else:
                        act.wait_ge(m_o, n - HEADS + 1)
                    if n >= 1:
                        act.wait_ge(m_ost, n)
                    nc.scalar.activation(squares, bank[:, 6 + n % 2, :].rearrange("p (t c) -> p t c", c=DV),
                                         ACT.Square).then_inc(m_osq, 1)

                act.wait_ge(m_gapc, 1)
                decay_of(0)
                decay_of(1)
                for h in range(HEADS):
                    head_squares(h)
                    if h + 2 < HEADS:
                        decay_of(h + 2)

                def exps(u):
                    act.wait_ge(m_dm, u + 1)
                    if u >= 2:
                        act.wait_ge(m_dp, u - 1)
                    for c in range(2):
                        nc.scalar.activation(prob[:, u % 2, c, :], pair(c), ACT.Exp, scale=DK ** -0.5,
                                             bias=smax[:, u % 2, c:c + 1],
                                             accum_out=sden[:, u % 2, c:c + 1]).then_inc(m_de, 1)

                def copy_T(u):
                    act.wait_ge(m_dt, u + 1)
                    nc.scalar.copy(diffT.rearrange("p t c -> p (t c)"), tr_diff).then_inc(m_dc, 1)

                for u in range(DU):
                    exps(u)
                    if u >= 1:
                        copy_T(u - 1)
                    if u >= 3 and (u - 3) % NT == NT - 1:
                        head_squares(HEADS + (u - 3) // NT)
                copy_T(DU - 1)
                for h in range((DU - 3) // NT, HEADS):
                    head_squares(HEADS + h)
                for hh in range(2 * HEADS):
                    act.wait_ge(m_mt, hh + 1)
                    nc.scalar.copy(mixT[:, hh, :], bank[:, hh % 4, :]).then_inc(m_mtc, 1)

            @block.gpsimd
            def _(pool):
                link = linker(pool, m_pchain)
                link(nc.gpsimd.memset(minus_half[:], -0.5))
                for t in range(NK):
                    pool.wait_ge(m_sq, t + 1)
                    link(nc.gpsimd.tensor_scalar(rstd[:, t:t + 1], stats[:, t:t + 1], 1.0 / D, EPS, ALU.mult, ALU.add))
                    nc.gpsimd.tensor_tensor(rstd[:, t:t + 1], rstd[:, t:t + 1], minus_half[:, 0:1],
                                            ALU.pow).then_inc(m_rs, 1)
                nc.gpsimd.memset(ada_first[:], 0.0).then_inc(m_az, 1)
                for n in range(2 * HEADS):
                    pool.wait_ge(m_ost, n + 1)
                    link(nc.gpsimd.tensor_scalar(hrstd[:, n, :], hstat[:, n, :], 1.0 / DV, EPS, ALU.mult, ALU.add))
                    nc.gpsimd.tensor_tensor(hrstd[:, n, :], hrstd[:, n, :], minus_half[:], ALU.pow).then_inc(m_orr, 1)

            @block.vector
            def _(dve):
                link = linker(dve, m_dchain)
                nc.vector.memset(ones[:], 1.0).then_inc(m_mset, 1)
                dve.wait_ge(m_small, 1)
                nc.vector.tensor_copy(small[:], bank[:, 6, 0:SMALL_ROWS]).then_inc(m_cols, 1)
                nc.vector.tensor_copy(bias_cols[:], bank[:, 6, P:P + 2 * KD]).then_inc(m_cols, 1)

                def xhat_of(t):
                    dve.wait_ge(m_rs, t + 1)
                    src = x[:, t, :] if t < NT else ctx_raw[:, t - NT, :]
                    nc.vector.tensor_scalar(xhat2[:, t % 2, :], src, rstd[:, t:t + 1], None, ALU.mult).then_inc(m_xh, 1)

                def hT_of(t):
                    dve.wait_ge(m_xt, t + 1)
                    v, na = (0, 0) if t < NT else (1, 1)
                    for k in range(KD // 2, KD):
                        dst = hT[:, k, t * P:(t + 1) * P] if t < NT else hcT[:, k, (t - NT) * P:(t - NT + 1) * P]
                        last = nc.vector.tensor_scalar(dst, bank[:, (t % 2) * 2 + k // 4, (k % 4) * P:(k % 4 + 1) * P],
                                                       norm_a[:, na, k:k + 1], mod[:, k, v:v + 1],
                                                       ALU.mult, ALU.add)
                    last.then_inc(m_htd, 1)

                xhat_of(0)
                xhat_of(1)
                dve.wait_ge(m_cols, 2)
                for j in range(PRE):
                    dve.wait_ge(m_pre, j + 1)
                    nc.vector.tensor_copy(pre_rows[:, j * HALF:(j + 1) * HALF], bank[0:2, 4 + j, :]).then_inc(m_prc, 1)
                dve.wait_ge(m_prt, 1)
                link(nc.vector.tensor_tensor(mod[:], bank[:, 4, 0:4 * KD].rearrange("p (j v) -> p j v", v=2),
                                             cols(bias_cols[:], 2), ALU.add))
                for v in range(2):
                    ins = nc.vector.scalar_tensor_tensor(norm_a[:, v, :], mod[:, KD:2 * KD, v], 1.0,
                                                         small[:, NM_ROW:NM_ROW + KD], ALU.add, ALU.mult)
                ins.then_inc(m_na, 1)
                dve.wait_ge(m_na, 1)
                for t in range(NK):
                    hT_of(t)
                    if t + 2 < NK:
                        xhat_of(t + 2)

                def ada_slab(i):
                    dve.wait_ge(ring_load[i % 2], 16 * (i // 2 + 2))
                    dve.wait_ge(m_ab, 16 * (i + 1))
                    if i >= 2:
                        dve.wait_ge(m_ar, i - 1)
                    w = ring[:, i % 2, :].rearrange("p (k c) -> p k c", k=KD)
                    for k in range(KD):
                        onto = ada_first[:] if k == 0 else ada_acc[:, i % 2, :]
                        ins = nc.vector.scalar_tensor_tensor(ada_acc[:, i % 2, :], w[:, k, :], silu_c[:, 0, k:k + 1],
                                                             onto, ALU.mult, ALU.add)
                        if k == 0:
                            ins.then_inc(m_au, 1)
                            dve.wait_ge(m_au, i + 1)
                        elif k < KD - 1:
                            link(ins)
                    ins.then_inc(m_as, 1)

                def rope(r, u):
                    j, t = units[u]
                    dve.wait_ge(m_proj, u + 1)
                    if r >= 2:
                        dve.wait_ge(m_qkt, r - 1)
                    if r >= 1:
                        dve.wait_ge(m_rope, r)
                    ps = bank[:, u % 3, :]
                    got = [q for q in parts(j, t) if q[2] in "qk"]
                    c0, w = got[0][0], sum(q[1] for q in got)
                    dst = roped[:, r % 2, c0:c0 + w]
                    if t >= NT:
                        nc.vector.tensor_copy(dst, ps[:, c0:c0 + w]).then_inc(m_rope, 1)
                        return
                    n = w // DK
                    nc.vector.tensor_tensor(
                        rope_x[:, 0:w].rearrange("p (h c) -> p h c", c=DK),
                        ps[:, c0:c0 + w].rearrange("p (h c) -> p h c", c=DK),
                        cos_t[:, t, :].unsqueeze(1).to_broadcast([P, n, DK]), ALU.mult)
                    swap = ps[:, c0:c0 + w].rearrange("p (h g s c) -> p h g s c", g=2, s=2, c=DK // 4)
                    turned = rope_y[:, 0:w].rearrange("p (h g s c) -> p h g s c", g=2, s=2, c=DK // 4)
                    sine = sin_t[:, t, :].rearrange("p (g s c) -> p g s c", g=2, s=2)
                    for s in range(2):
                        ins = nc.vector.tensor_tensor(
                            turned[:, :, :, s, :], swap[:, :, :, 1 - s, :],
                            sine[:, :, s, :].unsqueeze(1).to_broadcast([P, n, 2, DK // 4]), ALU.mult)
                    link(ins)
                    nc.vector.tensor_tensor(dst, rope_x[:, 0:w], rope_y[:, 0:w], ALU.add).then_inc(m_rope, 1)
                dve.wait_ge(m_ld["rope"], 32)
                dve.wait_ge(m_az, 1)
                for u in range(len(units)):
                    if u in roped_units:
                        rope(roped_units.index(u), u)
                    for i in slabs_after.get(u, ()):
                        ada_slab(i)

                dve.wait_ge(m_ld["row"], 48)
                dve.wait_ge(m_proj, len(units))
                lv = lam_in[:].rearrange("p (a b c) -> p a b c", a=2, b=2)
                link(nc.vector.tensor_tensor(lam_pr, lv[:, :, 0, :], lv[:, :, 1, :], ALU.mult))
                nc.vector.tensor_reduce(lam_s[:], lam_pr, AX.X, ALU.add).then_inc(m_lam, 1)
                nc.vector.tensor_scalar(subln[:], subln[:], 1.0 - LAM_INIT, None, ALU.mult)
                nc.vector.tensor_scalar(ld_neg[:], ld[:], -1.0, None, ALU.mult)
                dve.wait_ge(m_ld["gap"], 16)
                nc.vector.tensor_scalar(gap_pos, gap[:, GAP_0:GAP_0 + P], 0.0, None, ALU.max)
                nc.vector.tensor_scalar(gap_neg, gap[:, GAP_0:GAP_0 + P], 0.0, None, ALU.min).then_inc(m_gapc, 1)
                dve.wait_ge(m_gapc, 1)
                nc.vector.memset(lam_v[:, 0:1], 1.0)
                dve.wait_ge(m_lame, 1)
                link(nc.vector.tensor_tensor(lam_v[:, 1:2], lam_e[:, 1:2], lam_e[:, 0:1], ALU.subtract))
                link(nc.vector.tensor_scalar(lam_v[:, 1:2], lam_v[:, 1:2], -LAM_INIT, None, ALU.add))

                def decay_arg_of(h):
                    if h >= 1:
                        dve.wait_ge(m_dk, 2 * h)
                    link(nc.vector.tensor_scalar(decay_arg, gap_pos, ld[:, h:h + 1], None, ALU.mult))
                    nc.vector.scalar_tensor_tensor(decay_arg, gap_neg, ld_neg[:, HEADS + h:HEADS + h + 1],
                                                   decay_arg, ALU.mult, ALU.add).then_inc(m_dk_arg, 1)

                def decay_finish(h):
                    dve.wait_ge(m_dk, 2 * h + 2)
                    d = decay[:, h % 2, :]
                    ins = nc.vector.tensor_tensor(d[:, GAP_0:GAP_0 + P], d[:, GAP_0:GAP_0 + P], ident[:], ALU.add)
                    for cp in range(NC):
                        f0, b0 = GAP_0 - P * (cp - NC), GAP_0 - P * (NT + cp)
                        ins = nc.vector.tensor_tensor(decay_c[:, cp, :], d[:, f0:f0 + SEQ], d[:, b0:b0 + SEQ], ALU.add)
                    link(ins)

                def head_stat(n):
                    dve.wait_ge(m_osq, n + 1)
                    nc.vector.tensor_reduce(hstat[:, n, :], squares, AX.X, ALU.add).then_inc(m_ost, 1)

                def head_norm(n):
                    dve.wait_ge(m_orr, n + 1)
                    o = bank[:, 6 + n % 2, :].rearrange("p (t c) -> p t c", c=DV)
                    for t in range(NT):
                        if n < HEADS:
                            dst = gate[:, t, n * DV:(n + 1) * DV]
                            with_ = dst
                        else:
                            dst = dif_out[:, t, (n - HEADS) * DV:(n - HEADS + 1) * DV]
                            with_ = subln[:]
                        ins = nc.vector.scalar_tensor_tensor(dst, o[:, t, :], hrstd[:, n, t:t + 1], with_,
                                                             ALU.mult, ALU.mult)
                    ins.then_inc(m_on, 1)

                decay_arg_of(0)
                decay_arg_of(1)
                for h in range(HEADS):
                    decay_finish(h)
                    for m in range(NK):
                        u = h * NK + m
                        dve.wait_ge(m_rs_s, u + 1)
                        if u >= 4:
                            dve.wait_ge(m_rs_v, u - 3)
                        win = (decay[:, h % 2, GAP_0 - P * m:GAP_0 - P * m + SEQ] if m < NT
                               else decay_c[:, m - NT, :])
                        nc.vector.tensor_tensor(retp[:, u % 4, :], bank[:, u % 4, :], win, ALU.mult).then_inc(m_rs_p, 1)
                        if m == 2 and h >= 1:
                            head_stat(h - 1)
                        if m == 4 and h >= 1:
                            head_norm(h - 1)
                    if h + 2 < HEADS:
                        decay_arg_of(h + 2)
                    dve.wait_ge(m_rs_p, NK * (h + 1))
                head_stat(HEADS - 1)
                head_norm(HEADS - 1)

                def combine(u):
                    b = u % 2
                    dve.wait_ge(m_de, 2 * u + 2)
                    link(nc.vector.reciprocal(srec[:, b, :], sden[:, b, :]))
                    link(nc.vector.tensor_tensor(srec[:, b, :], srec[:, b, :], lam_v[:], ALU.mult))
                    if u >= 1:
                        dve.wait_ge(m_dt, u)
                    link(nc.vector.tensor_scalar(diffp, prob[:, b, 0, :], srec[:, b, 0:1], None, ALU.mult))
                    nc.vector.scalar_tensor_tensor(diffp, prob[:, b, 1, :], srec[:, b, 1:2], diffp,
                                                   ALU.mult, ALU.add).then_inc(m_dp, 1)

                for u in range(DU):
                    dve.wait_ge(m_ds, u + 1)
                    both = bank[:, 0:4, :].rearrange("p (c b) n -> p c (b n)", c=2)[:, :, 0:NK * P]
                    link(nc.vector.tensor_reduce(smax[:, u % 2, :], both, AX.X, ALU.max))
                    nc.vector.tensor_scalar(smax[:, u % 2, :], smax[:, u % 2, :], -(DK ** -0.5), None,
                                            ALU.mult).then_inc(m_dm, 1)
                    if u >= 1:
                        combine(u - 1)
                    if u >= 4 and (u - 4) % NT == NT - 1:
                        head_stat(HEADS + (u - 4) // NT)
                        head_norm(HEADS + (u - 4) // NT)
                combine(DU - 1)
                for h in range((DU - 4) // NT, HEADS):
                    head_stat(HEADS + h)
                    head_norm(HEADS + h)

                dve.wait_ge(m_g1, 16)
                for n in range(2 * NT):
                    hf, t = n // NT, n % NT
                    dve.wait_ge(m_op, n + 1)
                    if n >= 1:
                        dve.wait_ge(m_xr, n)
                    link(nc.vector.tensor_tensor(upd, bank[:, 4 + n % 2, :], gate1_b[:, hf * HALF:(hf + 1) * HALF],
                                                 ALU.mult))
                    xs = x[:, t, hf * HALF:(hf + 1) * HALF]
                    nc.vector.tensor_tensor(xs, xs, upd, ALU.add).then_inc(m_xr, 1)

            @block.tensor
            def _(pe):
                pe.wait_ge(m_ld["ident"], 16)
                pe.wait_ge(m_ld["smallA"], 3 * 16)
                pe.wait_ge(m_ld["smallB"], 16)
                pe.transpose(bank[:, 6, 0:SMALL_ROWS], arena[0:SMALL_ROWS, 0:P], ident[0:SMALL_ROWS, 0:SMALL_ROWS])
                nb = 2 * KD
                pe.transpose(bank[:, 6, P:P + nb], arena[0:nb, P:2 * P], ident[0:nb, 0:nb]).then_inc(m_small, 1)

                def slab_in(i, loads):
                    pe.wait_ge(ring_load[i], 16 * loads)
                    return ring[:, i, :].rearrange("p (k c) -> p k c", k=KD)

                pe.wait_ge(m_silu, 1)
                pe.wait_ge(m_cols, 2)
                for j in range(PRE):
                    w = slab_in(j, 1)
                    for k in range(KD):
                        last = pe.matmul(bank[0:2, 4 + j, :], silu_c[:, :, k], w[:, k, :], start=(k == 0), stop=(k == KD - 1))
                    last.then_inc(m_pre, 1)
                pe.wait_ge(m_prc, PRE)
                for j in range(2 * KD):
                    last = pe.transpose(bank[:, 4, 2 * j:2 * j + 2], pre_rows[:, j * P:(j + 1) * P], ident[0:2, 0:2])
                last.then_inc(m_prt, 1)

                for t in range(NK):
                    pe.wait_ge(m_xh, t + 1)
                    if t >= 2:
                        pe.wait_ge(m_hta, t - 1)
                        pe.wait_ge(m_htd, t - 1)
                    for k in range(KD):
                        last = pe.transpose(bank[:, (t % 2) * 2 + k // 4, (k % 4) * P:(k % 4 + 1) * P],
                                            xhat2[:, t % 2, k * P:(k + 1) * P], ident[:])
                    last.then_inc(m_xt, 1)
                pe.wait_ge(m_hta, NK)
                pe.wait_ge(m_htd, NK)

                def unit_read(u):
                    if u in rope_at:
                        pe.wait_ge(m_rope, rope_at[u] + 1)
                    if u in gv_at:
                        pe.wait_ge(m_gv, gv_at[u] + 1)

                rope_at = {u: i for i, u in enumerate(roped_units)}
                gv_at = {u: i for i, u in enumerate(sorted(gate_units + v_units))}

                def transpose_unit(u):
                    if u not in rope_at:
                        return
                    r = rope_at[u]
                    pe.wait_ge(m_rope, r + 1)
                    if r >= 2:
                        pe.wait_ge(m_qkc, r - 1)
                    for c0, w, kind, b0 in parts(*units[u]):
                        if kind in "qk":
                            for c in range(c0, c0 + w, P):
                                last = pe.transpose(bank[:, 4 + r % 2, c:c + P], roped[:, r % 2, c:c + P], ident[:])
                    last.then_inc(m_qkt, 1)

                def ada_row_sum(i):
                    pe.wait_ge(m_as, i + 1)
                    if i >= 2:
                        pe.wait_ge(m_arc, i - 1)
                    pe.matmul(bank[0:1, 6 + i % 2, :], ones[:, 0:1], ada_acc[:, i % 2, :],
                              start=True, stop=True).then_inc(m_ar, 1)

                pe.wait_ge(m_mset, 1)
                at_slab = {}
                for u, (j, t) in enumerate(units):
                    if j not in at_slab:
                        at_slab[j] = slab_in(2 + j % 2, 2 + j // 2)
                    w = at_slab[j]
                    if u >= 3:
                        unit_read(u - 3)
                    got = parts(j, t)
                    c0, c1 = got[0][0], got[-1][0] + got[-1][1]
                    for k in range(KD):
                        h = hT[:, k, t * P:(t + 1) * P] if t < NT else hcT[:, k, (t - NT) * P:(t - NT + 1) * P]
                        last = pe.matmul(bank[:, u % 3, c0:c1], h, w[:, k, c0:c1], start=(k == 0), stop=(k == KD - 1))
                    last.then_inc(m_proj, 1)
                    if u >= 1:
                        transpose_unit(u - 1)
                    for i in rows_after.get(u, ()):
                        ada_row_sum(i)
                transpose_unit(len(units) - 1)
                for u in range(len(units) - 3, len(units)):
                    unit_read(u)

                pe.wait_ge(m_arc, len(rest))

                pe.wait_ge(m_qkc, len(roped_units))

                def ret_scores(u):
                    h, m = divmod(u, NK)
                    if u >= 4:
                        pe.wait_ge(m_rs_p, u - 3)
                    lo = DK * (h % 2)
                    pe.matmul(bank[:, u % 4, :], kT[lo:lo + DK, h // 2, m * P:(m + 1) * P], qT[lo:lo + DK, h // 2, :],
                              start=True, stop=True).then_inc(m_rs_s, 1)

                def ret_values(u):
                    h, m = divmod(u, NK)
                    if m == 0 and h >= 2:
                        pe.wait_ge(m_on, h - 1)
                    pe.wait_ge(m_rs_p, u + 1)
                    for t in range(NT):
                        last = pe.matmul(bank[:, 6 + h % 2, t * DV:(t + 1) * DV], retp[:, u % 4, t * P:(t + 1) * P],
                                         v_tok[:, m, h * DV:(h + 1) * DV], start=(m == 0 and t == 0),
                                         stop=(m == NK - 1 and t == NT - 1), skip_group_check=True)
                    last.then_inc(m_rs_v, 1)

                for u in range(RU + 2):
                    if u < RU:
                        ret_scores(u)
                    if u >= 2:
                        ret_values(u - 2)

                def diff_scores(u):
                    h, t = divmod(u, NT)
                    if u == 0:
                        pe.wait_ge(m_rs_p, RU)
                    else:
                        pe.wait_ge(m_de, 2 * u)
                    for c in range(2):
                        for b, (k0, k1) in enumerate(((0, HALF), (HALF, NK * P))):
                            last = pe.matmul(bank[:, 2 * c + b, 0:k1 - k0], qT[c * DK:(c + 1) * DK, 2 + h, t * P:(t + 1) * P],
                                             kT[c * DK:(c + 1) * DK, 2 + h, k0:k1], start=True, stop=True)
                    last.then_inc(m_ds, 1)

                def diff_transpose(u):
                    pe.wait_ge(m_dp, u + 1)
                    if u >= 1:
                        pe.wait_ge(m_dc, u)
                    for m in range(NK):
                        last = pe.transpose(tr_diff[:, m * P:(m + 1) * P], diffp[:, m * P:(m + 1) * P], ident[:])
                    last.then_inc(m_dt, 1)

                def diff_values(u):
                    h, t = divmod(u, NT)
                    n = HEADS + h
                    if t == 0:
                        pe.wait_ge(m_on, n - 1)
                    pe.wait_ge(m_dc, u + 1)
                    for m in range(NK):
                        last = pe.matmul(bank[:, 6 + n % 2, t * DV:(t + 1) * DV], diffT[:, m, :],
                                         v_tok[:, m, n * DV:(n + 1) * DV], start=(m == 0), stop=(m == NK - 1))
                    if t == NT - 1:
                        last.then_inc(m_o, 1)

                for u in range(DU + 2):
                    if u < DU:
                        diff_scores(u)
                    if u >= 2:
                        diff_values(u - 2)
                    if 1 <= u <= DU:
                        diff_transpose(u - 1)

                for hh in range(2 * HEADS):
                    pe.wait_ge(m_on, 2 * HEADS)
                    if hh >= 4:
                        pe.wait_ge(m_mtc, hh - 3)
                    src = gate if hh < HEADS else dif_out
                    c0 = (hh % HEADS) * DV
                    for t in range(NT):
                        last = pe.transpose(bank[:, hh % 4, t * P:(t + 1) * P], src[:, t, c0:c0 + DV], ident[:])
                    last.then_inc(m_mt, 1)
                pe.wait_ge(m_mtc, 2 * HEADS)
                for hf in range(2):
                    w = slab_in(2 + hf, 5)
                    for t in range(NT):
                        i = hf * NT + t
                        if i >= 2:
                            pe.wait_ge(m_xr, i - 1)
                        for k in range(KD):
                            last = pe.matmul(bank[:, 4 + i % 2, :], mixT[:, k, t * P:(t + 1) * P], w[:, k, :],
                                             start=(k == 0), stop=(k == KD - 1))
                        last.then_inc(m_op, 1)
        ring_uses[:] = [1 + len(rest) // 2, 1 + len(rest) // 2, 1 + 4, 1 + 4, 0, 0]

        stage_over()

        moe0 = 2 * SLOT_W
        at_small = [26000]

        def small_tile(name, shape, dt=F32):
            v, at_small[0] = carve(at_small[0], *shape[1:])
            return v if dt == F32 else v.bitcast(dt)

        router_w = small_tile("router_w_sb", [P, KD, NE])
        router_b = small_tile("router_b_sb", [P, NE])
        krows = small_tile("krows", [P, 2, NE])
        token = small_tile("token", [P, NT], I32)
        before = small_tile("before", [P, P])
        score = small_tile("score", [P, NT, NE])
        biased = small_tile("biased", [P, NT, NE])
        g_hi = small_tile("g_hi", [P, NT * NG, 2])
        g_lo = small_tile("g_lo", [P, NT * NG, 2])
        g_t = small_tile("g_t", [P, 3, NT * NG])
        g_pad = small_tile("g_pad", [P, NT, 8])
        top8 = small_tile("top8", [P, NT, 8])
        top8i = small_tile("top8i", [P, NT, 8], U32)
        g_sel = small_tile("g_sel", [P, NT])
        in_grp = small_tile("in_grp", [P, NT, NE])
        masked = small_tile("masked", [P, NT, NE])
        e_sel = small_tile("e_sel", [P, 2, NT])
        pick = small_tile("pick", [P, 2, NT, NE])
        e_mask = small_tile("e_mask", [P, NT, NE])
        r_tmp = small_tile("r_tmp", [P, 2, NT, NE])
        weight = small_tile("weight", [P, 2, NT])
        w_sum = small_tile("w_sum", [P, NT])
        row_tmp = small_tile("row_tmp", [P, 2, 2, NT])
        place = small_tile("place", [P, 2, NT])
        row_of = small_tile("row_of", [P, 2, NT], U32)
        entry_of = small_tile("entry_of", [P, 2, NT], U32)
        max_count = small_tile("max_count", [P, 1], I32)
        places = small_tile("places", [P, P])
        token_f = small_tile("token_f", [P, NT])
        token_in = small_tile("token_in", [P, NT, 2])
        pos_in = small_tile("pos_in", [P, NT, 2])
        lists = small_tile("lists", [P, NE], I32)
        idx = small_tile("idx", [P, 2], U32)

        def moe(l):
            m_const = sem(f"moe{l}_tables_loaded")
            e_ = lambda s: sem(f"moe{l}_{s}")
            ahead = 4 if l == 0 else 6
            base = list(ring_uses)
            wg, wu, wd = a["moe_w_gate"][l], a["moe_w_up"][l], a["moe_w_down"][l]
            xhat, at = carve(moe0, NT, D)
            hT, at = carve(at, KD, SEQ)
            scale_b, at = carve(at, D)
            shift_b, at = carve(at, D)
            normw_b, at = carve(at, D)
            at_place, at = carve(at, NT, 2, P)
            xg, at = carve(moe0, 2, D)
            xgT, at = carve(at, 2, KD, P)
            act_g, at = carve(at, DE)
            hid, at = carve(at, DE)
            hidT, at = carve(at, KE, P)
            y_sb, at = carve(at, 2, D)

            s_sq, s_rs, s_xh, s_xst, s_xt = e_("square_sum"), e_("rstd"), e_("xhat"), e_("xhat_stored"), e_("xhat_T")
            s_hta = e_("hT_copied")
            s_lg, s_sc, s_mask, s_pos = e_("logits"), e_("scores"), e_("mask"), e_("places")
            s_rows, s_cnt = e_("rows_ready"), e_("count_ready")
            s_put, s_list = e_("lists_written"), e_("lists_loaded")
            s_hot, s_first = e_("place_rows_ready"), e_("first_lists_ready")
            s_sh, s_g2 = e_("shift_loaded"), e_("g2_loaded")
            s_mod, s_ab = e_("adaln_rows_loaded"), e_("scale_ready")
            s_load = ring_load
            s_gtd = e_("rows_T_copied_by_dve")
            s_idx = e_("idx_ready")
            s_xg = [e_(f"rows_gathered{u}") for u in range(2)]
            s_gt, s_gtc = e_("rows_T"), e_("rows_T_copied")
            s_gate, s_up, s_silu, s_hid = e_("gate_done"), e_("up_done"), e_("silu_done"), e_("hid_ready")
            s_ht2, s_ht2c, s_dn, s_y = e_("hid_T"), e_("hid_T_copied"), e_("down_done"), e_("y_ready")
            s_yst = [e_(f"y_stored{u}") for u in range(2)]
            s_dc, s_pc = e_("dve_chain"), e_("pool_chain")

            with nc.Block() as block:

                @block.sync
                def _(sp):
                    sp.dma_start(scale_b, mod_row(l, SC2)).then_inc(s_mod, 16)
                    sp.dma_start(normw_b, a["norm_ffn_w"][l].partition_broadcast(P)).then_inc(s_mod, 16)
                    sp.dma_start(shift_b, mod_row(l, SH2)).then_inc(s_sh, 16)
                    if l == 0:
                        sp.dma_start(router_w[:], a["router_w"].rearrange("(k p) e -> p k e", p=P)).then_inc(m_const, 16)
                        sp.dma_start(router_b[:], a["router_b"].partition_broadcast(P)).then_inc(m_const, 16)
                        sp.dma_start(krows[:], a["k_rows"].partition_broadcast(P)).then_inc(m_const, 16)
                        sp.dma_start(token[:], a["k_token"]).then_inc(m_const, 16)
                        sp.dma_start(before[:], a["k_before"]).then_inc(m_const, 16)
                        sp.dma_start(places[:], a["k_places"].partition_broadcast(P).rearrange("p a c -> p (a c)")
                                     ).then_inc(m_const, 16)
                    for t in range(NT):
                        sp.wait_ge(s_xh, t + 1)
                        sp.dma_start(xh_dram[t * P:(t + 1) * P, :], xhat[:, t, :]).then_inc(s_xst, 16)
                    sp.dma_start(gate2_b[:], mod_row(l, G2)).then_inc(s_g2, 16)
                    for s in range(ahead, 6):
                        u, q = divmod(s, 3)
                        put(sp, (wg, wu, wd)[q], u, s, (KD, KD, KE)[q]).then_inc(s_load[s], 16)
                    sp.wait_ge(s_put, 16 * 2 * NT)
                    sp.dma_start(lists[:], list_dram[0:P * NE, :].rearrange("(j e) o -> j (e o)", e=NE)).then_inc(s_list, 16)
                    with sp.Fori(1, NE // 2) as i:
                        for u in range(2):
                            e = sp.snap(2 * i + u)
                            for q, (w, k, used) in enumerate(((wg, KD, s_gate), (wu, KD, s_up), (wd, KE, s_dn))):
                                s = 3 * u + q
                                sp.wait_ge(used, e - 1)
                                put(sp, w, e, s, k).then_inc(s_load[s], 16)
                    if l + 1 < DEPTH:
                        for s in range(3):
                            u, q = divmod(s, 3)
                            sp.wait_ge((s_gate, s_up, s_dn)[q], NE - 1 + u)
                            put(sp, (a["moe_w_gate"], a["moe_w_up"], a["moe_w_down"])[q][l + 1], u, s,
                                (KD, KD, KE)[q]).then_inc(s_load[s], 16)

                @block.gpsimd
                def _(pool):
                    link = linker(pool, s_pc)
                    for t in range(NT):
                        pool.wait_ge(s_sq, t + 1)
                        link(nc.gpsimd.tensor_scalar(rstd[:, t:t + 1], stats[:, t:t + 1], 1.0 / D, EPS,
                                                     ALU.mult, ALU.add))
                        nc.gpsimd.tensor_tensor(rstd[:, t:t + 1], rstd[:, t:t + 1], minus_half[:, 0:1],
                                                ALU.pow).then_inc(s_rs, 1)

                    def fetch(u):
                        pool.indirect_dma_start(out=xg[:, u, :], out_offset=None, in_=xh_dram,
                                                in_offset=bass.IndirectOffsetOnAxis(ap=idx[:, u:u + 1], axis=0)
                                                ).then_inc(s_xg[u], 16)

                    pool.wait_ge(s_lg, 1)
                    pool.wait_ge(s_xst, 16 * NT)
                    pool.wait_ge(s_idx, 1)
                    for u in range(2):
                        fetch(u)
                    pool.wait_ge(s_rows, 1)
                    for t in range(NT):
                        for c in range(2):
                            pool.indirect_dma_start(
                                out=list_dram, out_offset=bass.IndirectOffsetOnAxis(ap=entry_of[:, c, t:t + 1], axis=0),
                                in_=token[:, t:t + 1], in_offset=None).then_inc(s_put, 16)
                    pool.wait_ge(s_list, 16)
                    for e in range(2, NE):
                        u = e % 2
                        pool.wait_ge(s_gt, e - 1)
                        pool.wait_ge(s_xg[u], 16 * (e // 2))
                        nc.gpsimd.tensor_copy(idx[:, u:u + 1], lists[:, e:e + 1]).then_inc(s_idx, 1)
                        pool.wait_ge(s_idx, e)
                        fetch(u)

                @block.scalar
                def _(act):
                    for t in range(NT):
                        nc.scalar.activation(xhat[:, t, :], x[:, t, :], ACT.Square,
                                             accum_out=stats[:, t:t + 1]).then_inc(s_sq, 1)
                    for t in range(NT):
                        act.wait_ge(s_xt, t + 1)
                        nc.scalar.copy(hT[:, :, t * P:(t + 1) * P],
                                       bank[:, 2 * (t % 2):2 * (t % 2) + 2, :].rearrange("p b (k c) -> p (b k) c", c=P)
                                       ).then_inc(s_hta, 1)
                    act.wait_ge(s_lg, 1)
                    nc.scalar.activation(score[:].rearrange("p t e -> p (t e)"), bank[:, 4, 0:NT * NE],
                                         ACT.Sigmoid).then_inc(s_sc, 1)

                    def copy_rows(u, n):
                        act.wait_ge(s_gt, n + 1)
                        nc.scalar.copy(xgT[:, u, 0:KD // 2, :], bank[:, 0, :].rearrange("p (k t) -> p k t", k=KD // 2)
                                       ).then_inc(s_gtc, 1)

                    def silu(n):
                        act.wait_ge(s_gate, n + 1)
                        nc.scalar.activation(act_g, bank[:, 2, :], ACT.Silu).then_inc(s_silu, 1)

                    def store(e, u, n):
                        act.wait_ge(s_y, n + 2)
                        act.dma_start(y_dram[bass.ds(e * P, P), :], y_sb[:, u, :]).then_inc(s_yst[u], 16)

                    copy_rows(0, 0)
                    copy_rows(1, 1)
                    silu(0)
                    with act.Fori(0, NE // 2 - 1) as i:
                        for u in range(2):
                            e = 2 * i + u
                            act.wait_ge(s_hid, e + 1)
                            silu(e + 1)
                            act.wait_ge(s_up, e + 1)
                            copy_rows(u, e + 2)
                            store(e, u, e)
                    for e in (NE - 2, NE - 1):
                        if e + 1 < NE:
                            act.wait_ge(s_hid, e + 1)
                            silu(e + 1)
                        store(e, e % 2, e)
                    for u in range(2):
                        act.wait_ge(s_yst[u], 16 * (NE // 2 + 1))

                @block.vector
                def _(dve):
                    link = linker(dve, s_dc)
                    nc.vector.memset(g_pad[:], -1e30)
                    dve.wait_ge(s_mod, 16 * 2)
                    link(nc.vector.scalar_tensor_tensor(scale_b, scale_b, 1.0, normw_b, ALU.add, ALU.mult))
                    for t in range(NT):
                        dve.wait_ge(s_rs, t + 1)
                        if t == 0:
                            dve.wait_ge(s_sh, 16)
                        link(nc.vector.scalar_tensor_tensor(xhat[:, t, :], x[:, t, :], rstd[:, t:t + 1], scale_b,
                                                            ALU.mult, ALU.mult))
                        nc.vector.tensor_tensor(xhat[:, t, :], xhat[:, t, :], shift_b, ALU.add).then_inc(s_xh, 1)
                    if l == 0:
                        dve.wait_ge(m_const, 16 * 6)
                    V = nc.vector
                    dve.wait_ge(s_sc, 1)
                    link(V.tensor_tensor(biased[:], score[:], router_b[:].unsqueeze(1).to_broadcast([P, NT, NE]), ALU.add))
                    v = biased[:].rearrange("p t (g a b) -> p (t g) a b", a=2, b=2)
                    V.tensor_tensor(g_hi[:], v[:, :, 0, :], v[:, :, 1, :], ALU.max)
                    link(V.tensor_tensor(g_lo[:], v[:, :, 0, :], v[:, :, 1, :], ALU.min))
                    V.tensor_tensor(g_t[:, 0, :], g_hi[:, :, 0], g_hi[:, :, 1], ALU.max)
                    V.tensor_tensor(g_t[:, 1, :], g_hi[:, :, 0], g_hi[:, :, 1], ALU.min)
                    link(V.tensor_tensor(g_t[:, 2, :], g_lo[:, :, 0], g_lo[:, :, 1], ALU.max))
                    link(V.tensor_tensor(g_t[:, 1, :], g_t[:, 1, :], g_t[:, 2, :], ALU.max))
                    link(V.tensor_tensor(g_pad[:, :, 0:NG], g_t[:, 0, :].rearrange("p (t g) -> p t g", g=NG),
                                         g_t[:, 1, :].rearrange("p (t g) -> p t g", g=NG), ALU.add))
                    for t in range(NT):
                        ins = V.max(top8[:, t, :], g_pad[:, t, :])
                    link(ins)
                    for t in range(NT):
                        ins = V.max_index(top8i[:, t, :], top8[:, t, :], g_pad[:, t, :])
                    link(ins)
                    link(V.tensor_copy(g_sel[:], top8i[:, :, 0]))
                    link(V.tensor_tensor(in_grp[:], krows[:, 1, :].unsqueeze(1).to_broadcast([P, NT, NE]),
                                         cols(g_sel[:], NE), ALU.is_equal))
                    V.tensor_scalar(r_tmp[:, 0], in_grp[:], -1.0, 1e30, ALU.add, ALU.mult)
                    link(V.tensor_tensor(masked[:], biased[:], in_grp[:], ALU.mult))
                    link(V.tensor_tensor(masked[:], masked[:], r_tmp[:, 0], ALU.add))
                    for t in range(NT):
                        ins = V.max(top8[:, t, :], masked[:, t, :])
                    link(ins)
                    for t in range(NT):
                        ins = V.max_index(top8i[:, t, :], top8[:, t, :], masked[:, t, :])
                    link(ins)
                    for c in range(2):
                        ins = V.tensor_copy(e_sel[:, c, :], top8i[:, :, c])
                    link(ins)
                    for c in range(2):
                        ins = V.tensor_tensor(pick[:, c], krows[:, 0, :].unsqueeze(1).to_broadcast([P, NT, NE]),
                                              cols(e_sel[:, c, :], NE), ALU.is_equal)
                    link(ins)
                    V.tensor_tensor(e_mask[:], pick[:, 0], pick[:, 1], ALU.add).then_inc(s_mask, 1)
                    link(V.tensor_copy(token_f[:], token[:]))
                    dve.wait_ge(s_mask, 1)
                    V.tensor_tensor(token_in[:], e_mask[:, :, 0:2], cols(token_f[:], 2), ALU.mult)
                    for c in range(2):
                        ins = V.tensor_tensor(r_tmp[:, c], pick[:, c], score[:], ALU.mult)
                    link(ins)
                    link(V.tensor_reduce(weight[:], r_tmp[:], AX.X, ALU.add))
                    link(V.tensor_tensor(w_sum[:], weight[:, 0, :], weight[:, 1, :], ALU.add))
                    link(V.reciprocal(w_sum[:], w_sum[:]))
                    link(V.tensor_tensor(weight[:], weight[:], w_sum[:].unsqueeze(1).to_broadcast([P, 2, NT]), ALU.mult))
                    dve.wait_ge(s_pos, 1)
                    pos = bank[:, 5, 0:NT * NE].rearrange("p (t e) -> p t e", e=NE)
                    link(V.tensor_copy(pos_in[:], pos[:, :, 0:2]))
                    V.tensor_tensor(at_place, places[:].unsqueeze(1).unsqueeze(1).to_broadcast([P, NT, 2, P]),
                                    pos_in[:].unsqueeze(3).to_broadcast([P, NT, 2, P]), ALU.is_equal).then_inc(s_hot, 1)
                    for c in range(2):
                        ins = V.tensor_tensor(r_tmp[:, c], pick[:, c], pos, ALU.mult)
                    link(ins)
                    link(V.tensor_reduce(place[:], r_tmp[:], AX.X, ALU.add))
                    V.scalar_tensor_tensor(row_tmp[:, 0], e_sel[:], float(P), place[:], ALU.mult, ALU.add)
                    link(V.tensor_scalar(row_tmp[:, 1], place[:], float(P), None, ALU.is_ge))
                    for b in range(2, SEQ // P):
                        link(V.scalar_tensor_tensor(row_tmp[:, 1], place[:], float(b * P), row_tmp[:, 1],
                                                    ALU.is_ge, ALU.add))
                    V.scalar_tensor_tensor(row_of[:], row_tmp[:, 1], float((NE - 1) * P), row_tmp[:, 0],
                                           ALU.mult, ALU.add)
                    V.scalar_tensor_tensor(entry_of[:], place[:], float(NE), e_sel[:], ALU.mult, ALU.add).then_inc(s_rows, 1)
                    V.tensor_reduce(max_count[:], bank[:, 5, NT * NE:(NT + 1) * NE], AX.X, ALU.max).then_inc(s_cnt, 1)

                    dve.wait_ge(s_first, 1)
                    V.tensor_copy(idx[:], bank[:, 4, NT * NE:NT * NE + 2]).then_inc(s_idx, 1)

                    V.memset(idx_zero[:, 0:1], 0.0).then_inc(s_y, 1)
                    for u in range(2):
                        V.memset(idx_zero[:, u + 1:u + 2], 0.0).then_inc(s_yst[u], 16)

                    def hidden(n):
                        dve.wait_ge(s_up, n + 1)
                        dve.wait_ge(s_silu, n + 1)
                        V.tensor_tensor(hid, act_g, bank[:, 3, :], ALU.mult).then_inc(s_hid, 1)

                    def copy_rows(u, n):
                        dve.wait_ge(s_gt, n + 1)
                        V.tensor_copy(xgT[:, u, KD // 2:KD, :], bank[:, 1, :].rearrange("p (k t) -> p k t", k=KD // 2)
                                      ).then_inc(s_gtd, 1)

                    def hidden_T(n):
                        dve.wait_ge(s_ht2, n + 1)
                        V.tensor_copy(hidT.rearrange("p k t -> p (k t)"), bank[:, 4, :]).then_inc(s_ht2c, 1)

                    def rows_out(n, u, uses):
                        dve.wait_ge(s_dn, n + 1)
                        dve.wait_ge(s_yst[u], uses)
                        V.tensor_tensor(y_sb[:, u, :], bank[:, 6:8, :].rearrange("p b c -> p (b c)"), gate2_b[:],
                                        ALU.mult).then_inc(s_y, 1)

                    copy_rows(0, 0)
                    copy_rows(1, 1)
                    hidden(0)
                    dve.wait_ge(s_g2, 16)
                    with dve.Fori(0, NE // 2 - 1) as i:
                        for u in range(2):
                            e = 2 * i + u
                            hidden_T(e)
                            copy_rows(u, e + 2)
                            hidden(e + 1)
                            rows_out(e, u, 16 * i + 16)
                    for e in (NE - 2, NE - 1):
                        hidden_T(e)
                        if e + 1 < NE:
                            hidden(e + 1)
                        rows_out(e, e % 2, 16 * (NE // 2))

                @block.tensor
                def _(pe):
                    def tile_T(t):
                        pe.wait_ge(s_xh, t + 1)
                        if t >= 2:
                            pe.wait_ge(s_hta, t - 1)
                        for k in range(KD):
                            last = pe.transpose(bank[:, 2 * (t % 2) + k // 4, (k % 4) * P:(k % 4 + 1) * P],
                                                xhat[:, t, k * P:(k + 1) * P], ident[:])
                        last.then_inc(s_xt, 1)

                    def logits(t):
                        pe.wait_ge(s_hta, t + 1)
                        for k in range(KD):
                            last = pe.matmul(bank[:, 4, t * NE:(t + 1) * NE], hT[:, k, t * P:(t + 1) * P], router_w[:, k, :],
                                             start=(k == 0), stop=(k == KD - 1))
                        return last

                    tile_T(0)
                    if l == 0:
                        pe.wait_ge(m_const, 16 * 6)
                    for t in range(NT):
                        if t + 1 < NT:
                            tile_T(t + 1)
                        last = logits(t)
                    last.then_inc(s_lg, 1)
                    pe.wait_ge(s_mask, 1)
                    for t in range(NT + 1):
                        for t2 in range(min(t + 1, NT)):
                            last = pe.matmul(bank[:, 5, t * NE:(t + 1) * NE], before[:] if t2 == t else ones[:],
                                             e_mask[:, t2, :], start=(t2 == 0), stop=(t2 == min(t, NT - 1)))
                    last.then_inc(s_pos, 1)
                    pe.wait_ge(s_hot, 1)
                    for e in range(2):
                        for t in range(NT):
                            last = pe.matmul(bank[:, 4, NT * NE + e:NT * NE + e + 1], at_place[:, t, e, :],
                                             token_in[:, t, e:e + 1], start=(t == 0), stop=(t == NT - 1))
                    last.then_inc(s_first, 1)
                    pe.wait_ge(s_cnt, 1)

                    def rows_T(u, gathered):
                        pe.wait_ge(s_xg[u], gathered)
                        for k in range(KD):
                            last = pe.transpose(bank[:, k // 4, (k % 4) * P:(k % 4 + 1) * P],
                                                xg[:, u, k * P:(k + 1) * P], ident[:])
                        last.then_inc(s_gt, 1)

                    first = [16 * (base[s] + 1) for s in range(6)]

                    def product(b, u, q, turn, done):
                        s = 3 * u + q
                        pe.wait_ge(s_load[s], 16 * turn + first[s])
                        w = slot(s).rearrange("p (k c) -> p k c", k=KD)
                        for k in range(KD):
                            last = pe.matmul(bank[:, b, :], xgT[:, u, k, :], w[:, k, :], start=(k == 0), stop=(k == KD - 1))
                        last.then_inc(done, 1)

                    def hid_T():
                        for k in range(KE):
                            last = pe.transpose(bank[:, 4, k * P:(k + 1) * P], hid[:, k * P:(k + 1) * P], ident[:])
                        last.then_inc(s_ht2, 1)

                    def down(u, turn, n):
                        s = 3 * u + 2
                        pe.wait_ge(s_load[s], 16 * turn + first[s])
                        pe.wait_ge(s_ht2c, n + 1)
                        pe.wait_ge(s_y, n + 1)
                        w = slot(s).rearrange("p (k c) -> p k c", k=KE)
                        for hf in range(2):
                            for k in range(KE):
                                last = pe.matmul(bank[:, 6 + hf, :], hidT[:, k, :], w[:, k, hf * HALF:(hf + 1) * HALF],
                                                 start=(k == 0), stop=(k == KE - 1))
                        last.then_inc(s_dn, 1)

                    rows_T(0, 16)
                    pe.wait_ge(s_gtc, 1)
                    pe.wait_ge(s_gtd, 1)
                    rows_T(1, 16)
                    product(2, 0, 0, 0, s_gate)
                    product(3, 0, 1, 0, s_up)

                    def step(e, u, turn, last_gather):
                        nxt = 1 - u
                        nxt_turn = turn + u
                        if not last_gather or u == 0:
                            pe.wait_ge(s_gtc, e + 2)
                            pe.wait_ge(s_gtd, e + 2)
                            pe.wait_ge(s_silu, e + 1)
                            product(2, nxt, 0, nxt_turn, s_gate)
                        pe.wait_ge(s_hid, e + 1)
                        hid_T()
                        if not last_gather:
                            rows_T(u, 16 * turn + 32)
                        if not last_gather or u == 0:
                            product(3, nxt, 1, nxt_turn, s_up)
                        down(u, turn, e)

                    with pe.Fori(0, NE // 2 - 1) as i:
                        for u in range(2):
                            step(2 * i + u, u, i, False)
                    for u in range(2):
                        step(NE - 2 + u, u, NE // 2 - 1, True)

            stage_over()

            ring_uses[:] = [n + NE // 2 for n in base]

            o_ = lambda s: sem(f"over{l}_{s}")
            v_ld, v_idx, v_xg = o_("weights"), o_("list"), o_("rows")
            v_t, v_tc, v_g, v_u, v_s, v_h = o_("rows_T"), o_("rows_T_copied"), o_("gate"), o_("up"), o_("silu"), o_("hid")
            v_h2, v_h2c, v_d, v_y, v_st = o_("hid_T"), o_("hid_T_copied"), o_("down"), o_("y"), o_("stored")
            v_small, v_re = o_("small_op"), o_("slots_refilled")
            MORE = SEQ // P - 1
            lists4 = list_dram.rearrange("(b j e) o -> b j (e o)", j=P, e=NE)

            def blocks(eng):
                with eng.Fori(0, MORE) as b:
                    with eng.Fori(0, NE) as e:
                        yield e, b + 1, b * NE + e

            with nc.Block() as block:

                @block.sync
                def _(sp):
                    most = sp.value_load(max_count[0:1, 0:1])
                    with sp.If(most > P):
                        if l + 1 < DEPTH:
                            for s in range(3):
                                sp.wait_ge(ring_load[s], 16 * (ring_uses[s] + 1))
                        for e, b, n in blocks(sp):
                            sp.wait_ge(v_d, n + 1)
                            put(sp, wg, e, 0, KD).then_inc(v_ld, 16)
                            put(sp, wu, e, 1, KD).then_inc(v_ld, 16)
                            put(sp, wd, e, 2, KE).then_inc(v_ld, 16)
                        if l + 1 < DEPTH:
                            sp.wait_ge(v_d, MORE * NE + 1)
                            put(sp, a["moe_w_gate"][l + 1], 0, 0, KD).then_inc(v_re, 16)
                            put(sp, a["moe_w_up"][l + 1], 0, 1, KD).then_inc(v_re, 16)
                            put(sp, a["moe_w_down"][l + 1], 0, 2, KE).then_inc(v_re, 16)
                            sp.wait_ge(v_re, 48)

                @block.gpsimd
                def _(pool):
                    most = pool.value_load(max_count[0:1, 0:1])
                    with pool.If(most > P):
                        for e, b, n in blocks(pool):
                            pool.dma_start(idx[:, 0:1].bitcast(I32), lists4[bass.ds(b, 1), :, bass.ds(e, 1)]
                                           .rearrange("b j e -> (b j) e")).then_inc(v_idx, 16)
                            pool.wait_ge(v_idx, 16 * n + 16)
                            nc.gpsimd.tensor_tensor(idx_zero[:], idx_zero[:], idx_zero[:], ALU.add).then_inc(v_small, 1)
                            pool.indirect_dma_start(out=xg[:, 0, :], out_offset=None, in_=xh_dram,
                                                    in_offset=bass.IndirectOffsetOnAxis(ap=idx[:, 0:1], axis=0)
                                                    ).then_inc(v_xg, 16)
                            pool.wait_ge(v_t, n + 1)
                            pool.wait_ge(v_small, n + 1)

                @block.scalar
                def _(act):
                    most = act.value_load(max_count[0:1, 0:1])
                    with act.If(most > P):
                        for e, b, n in blocks(act):
                            act.wait_ge(v_t, n + 1)
                            nc.scalar.copy(xgT[:, 0].rearrange("p k t -> p (k t)"),
                                           bank[:, 0:2, :].rearrange("p b c -> p (b c)")).then_inc(v_tc, 1)
                            act.wait_ge(v_g, n + 1)
                            nc.scalar.activation(act_g, bank[:, 2, :], ACT.Silu).then_inc(v_s, 1)
                            act.wait_ge(v_y, n + 1)
                            act.dma_start(y_dram[bass.ds((b * NE + e) * P, P), :], y_sb[:, 0, :]).then_inc(v_st, 16)
                            act.wait_ge(v_st, 16 * n + 16)

                @block.vector
                def _(dve):
                    most = dve.value_load(max_count[0:1, 0:1])
                    with dve.If(most > P):
                        for e, b, n in blocks(dve):
                            dve.wait_ge(v_u, n + 1)
                            dve.wait_ge(v_s, n + 1)
                            nc.vector.tensor_tensor(hid, act_g, bank[:, 3, :], ALU.mult).then_inc(v_h, 1)
                            dve.wait_ge(v_h2, n + 1)
                            nc.vector.tensor_copy(hidT.rearrange("p k t -> p (k t)"), bank[:, 4, :]).then_inc(v_h2c, 1)
                            dve.wait_ge(v_d, n + 2)
                            nc.vector.tensor_tensor(y_sb[:, 0, :], bank[:, 6:8, :].rearrange("p b c -> p (b c)"),
                                                    gate2_b[:], ALU.mult).then_inc(v_y, 1)
                            dve.wait_ge(v_st, 16 * n + 16)

                @block.tensor
                def _(pe):
                    most = pe.value_load(max_count[0:1, 0:1])
                    with pe.If(most > P):
                        pe.transpose(bank[:, 5, 0:P], ident[:], ident[:]).then_inc(v_d, 1)
                        for e, b, n in blocks(pe):
                            pe.wait_ge(v_xg, 16 * n + 16)
                            for k in range(KD):
                                last = pe.transpose(bank[:, k // 4, (k % 4) * P:(k % 4 + 1) * P],
                                                    xg[:, 0, k * P:(k + 1) * P], ident[:])
                            last.then_inc(v_t, 1)
                            pe.wait_ge(v_tc, n + 1)
                            pe.wait_ge(v_ld, 48 * n + 48)
                            for q, done in ((0, v_g), (1, v_u)):
                                w = slot(q).rearrange("p (k c) -> p k c", k=KD)
                                for k in range(KD):
                                    last = pe.matmul(bank[:, 2 + q, :], xgT[:, 0, k, :], w[:, k, :],
                                                     start=(k == 0), stop=(k == KD - 1))
                                last.then_inc(done, 1)
                            pe.wait_ge(v_h, n + 1)
                            for k in range(KE):
                                last = pe.transpose(bank[:, 4, k * P:(k + 1) * P], hid[:, k * P:(k + 1) * P], ident[:])
                            last.then_inc(v_h2, 1)
                            pe.wait_ge(v_h2c, n + 1)
                            w = slot(2).rearrange("p (k c) -> p k c", k=KE)
                            for hf in range(2):
                                for k in range(KE):
                                    last = pe.matmul(bank[:, 6 + hf, :], hidT[:, k, :], w[:, k, hf * HALF:(hf + 1) * HALF],
                                                     start=(k == 0), stop=(k == KE - 1))
                            last.then_inc(v_d, 1)
                            pe.wait_ge(v_st, 16 * n + 16)

            stage_over()

            c_y = [[sem(f"comb{l}_rows{c}_{t}") for t in range(NT)] for c in range(2)]
            c_ch = sem(f"comb{l}_chain")
            rows, at = carve(moe0, 2, NT, D)

            with nc.Block() as block:

                @block.gpsimd
                def _(pool):
                    def fetch_rows(written):
                        for t in range(NT):
                            for c in range(2):
                                pool.indirect_dma_start(
                                    out=rows[:, c, t, :], out_offset=None, in_=y_dram[0:written, :],
                                    in_offset=bass.IndirectOffsetOnAxis(ap=row_of[:, c, t:t + 1], axis=0)
                                ).then_inc(c_y[c][t], 16)

                    most = pool.value_load(max_count[0:1, 0:1])
                    with pool.If(most > P):
                        fetch_rows(LIST_N)
                    with pool.Else():
                        fetch_rows(NE * P)

                @block.vector
                def _(dve):
                    link = linker(dve, c_ch)
                    for t in range(NT):
                        for c in range(2):
                            dve.wait_ge(c_y[c][t], 16)
                            link(nc.vector.scalar_tensor_tensor(x[:, t, :], rows[:, c, t, :], weight[:, c, t:t + 1],
                                                                x[:, t, :], ALU.mult, ALU.add))

            stage_over()

        idx_zero = sb("credit", [1, 3])

        moe(0)

        bands, at = carve(moe0, len(WINDOWS), 5, P)
        pool_w, at = carve(at, len(WINDOWS), 2, 2 * P)
        xhat, at = carve(at, NT, D)
        pooledT, at = carve(at, KD, SEQ)
        scale1_b, at = carve(at, D)
        shift1_b, at = carve(at, D)
        normw1_b, at = carve(at, D)
        upd2, at = carve(at, HALF)
        assert at <= 26000
        p_ = lambda s: sem(f"pool_{s}")
        p_ld, p_sq, p_rs, p_xh, p_pl, p_plc = p_("tables"), p_("square_sum"), p_("rstd"), p_("xhat"), p_("pooled"), p_("pooled_copied")
        p_mod, p_ps, p_nw, p_mx, p_xr, p_dc, p_pc = (p_("adaln_rows_loaded"), p_("scale_loaded"), p_("norm_weight_used"),
                                                     p_("mixed"), p_("x_updated"), p_("dve_chain"), p_("pool_chain"))

        with nc.Block() as block:

            @block.sync
            def _(sp):
                for dst, src in ((scale1_b, mod_row(1, SC1)), (normw1_b, a["norm_mix_w"][1].partition_broadcast(P)),
                                 (shift1_b, mod_row(1, SH1)), (gate1_b[:], mod_row(1, G1))):
                    sp.dma_start(dst, src).then_inc(p_mod, 16)
                sp.dma_start(bands.rearrange("p g b c -> p (g b c)"), a["k_bands"]).then_inc(p_ld, 16)
                sp.dma_start(pool_w.rearrange("p g k c -> p (g k) c"),
                             a["pool_w"][0].rearrange("g (k p) c -> p (g k) c", p=P)).then_inc(p_ld, 16)
                sp.wait_ge(p_nw, 1)
                sp.dma_start(normw1_b, a["pool_scale"][0].partition_broadcast(P)).then_inc(p_ps, 16)
                for q, (w, k) in enumerate((("moe_w_gate", KD), ("moe_w_up", KD), ("moe_w_down", KE))):
                    put(sp, a[w][1], 1, 3 + q, k).then_inc(ring_load[3 + q], 16)

            @block.scalar
            def _(act):
                for t in range(NT):
                    nc.scalar.activation(xhat[:, t, :], x[:, t, :], ACT.Square,
                                         accum_out=stats[:, t:t + 1]).then_inc(p_sq, 1)
                for k in range(KD):
                    act.wait_ge(p_pl, k + 1)
                    nc.scalar.copy(pooledT[:, k, :], bank[:, k % 4, :]).then_inc(p_plc, 1)

            @block.gpsimd
            def _(pool):
                link = linker(pool, p_pc)
                for t in range(NT):
                    pool.wait_ge(p_sq, t + 1)
                    link(nc.gpsimd.tensor_scalar(rstd[:, t:t + 1], stats[:, t:t + 1], 1.0 / D, EPS, ALU.mult, ALU.add))
                    nc.gpsimd.tensor_tensor(rstd[:, t:t + 1], rstd[:, t:t + 1], minus_half[:, 0:1],
                                            ALU.pow).then_inc(p_rs, 1)

            @block.vector
            def _(dve):
                link = linker(dve, p_dc)
                dve.wait_ge(p_mod, 16 * 4)
                nc.vector.scalar_tensor_tensor(scale1_b, scale1_b, 1.0, normw1_b, ALU.add, ALU.mult).then_inc(p_nw, 1)
                dve.wait_ge(p_nw, 1)
                for t in range(NT):
                    dve.wait_ge(p_rs, t + 1)
                    link(nc.vector.scalar_tensor_tensor(xhat[:, t, :], x[:, t, :], rstd[:, t:t + 1], scale1_b,
                                                        ALU.mult, ALU.mult))
                    nc.vector.tensor_tensor(xhat[:, t, :], xhat[:, t, :], shift1_b, ALU.add).then_inc(p_xh, 1)
                dve.wait_ge(p_ps, 16)
                link(nc.vector.tensor_tensor(gate1_b[:], gate1_b[:], normw1_b, ALU.mult))
                for n in range(2 * NT):
                    hf, t = n // NT, n % NT
                    dve.wait_ge(p_mx, n + 1)
                    if n >= 1:
                        dve.wait_ge(p_xr, n)
                    link(nc.vector.tensor_tensor(upd2, bank[:, 4 + n % 2, :], gate1_b[:, hf * HALF:(hf + 1) * HALF],
                                                 ALU.mult))
                    xs = x[:, t, hf * HALF:(hf + 1) * HALF]
                    nc.vector.tensor_tensor(xs, xs, upd2, ALU.add).then_inc(p_xr, 1)

            @block.tensor
            def _(pe):
                pe.wait_ge(p_ld, 32)
                pe.wait_ge(p_xh, NT)
                for k in range(KD):
                    if k >= 4:
                        pe.wait_ge(p_plc, k - 3)
                    g = k // 2
                    for t in range(NT):
                        near = [(t2, b) for t2, b in ((t - 1, 3), (t, 0 if t == 0 else 2 if t == NT - 1 else 1), (t + 1, 4))
                                if 0 <= t2 < NT]
                        for n, (t2, b) in enumerate(near):
                            last = pe.matmul(bank[:, k % 4, t * P:(t + 1) * P], xhat[:, t2, k * P:(k + 1) * P],
                                             bands[:, g, b, :], start=(n == 0), stop=(n == len(near) - 1))
                    last.then_inc(p_pl, 1)
                pe.wait_ge(p_plc, KD)
                for n in range(2 * NT):
                    hf, t = n // NT, n % NT
                    if n >= 2:
                        pe.wait_ge(p_xr, n - 1)
                    for g in (2 * hf, 2 * hf + 1):
                        c0 = (g % 2) * 2 * P
                        for k in range(2):
                            last = pe.matmul(bank[:, 4 + n % 2, c0:c0 + 2 * P], pooledT[:, 2 * g + k, t * P:(t + 1) * P],
                                             pool_w[:, g, k, :], start=(k == 0), stop=(k == 1))
                    last.then_inc(p_mx, 1)

        stage_over()

        moe(1)

        f_ld, f_sq, f_rs, f_o, f_st, f_pc = (sem(f"fin_{s}") for s in
                                             ("weight", "square_sum", "rstd", "out", "stored", "pool_chain"))
        fin_w, at = carve(0, D)
        fin, at = carve(at, NT, D)

        with nc.Block() as block:

            @block.sync
            def _(sp):
                sp.dma_start(fin_w, a["final_norm_w"].partition_broadcast(P)).then_inc(f_ld, 16)
                for t in range(NT):
                    sp.wait_ge(f_o, t + 1)
                    sp.dma_start(out[0, t * P:(t + 1) * P, :], fin[:, t, :]).then_inc(f_st, 16)
                sp.wait_ge(f_st, 16 * NT)

            @block.scalar
            def _(act):
                for t in range(NT):
                    nc.scalar.activation(fin[:, t, :], x[:, t, :], ACT.Square, accum_out=stats[:, t:t + 1]).then_inc(f_sq, 1)

            @block.gpsimd
            def _(pool):
                link = linker(pool, f_pc)
                for t in range(NT):
                    pool.wait_ge(f_sq, t + 1)
                    link(nc.gpsimd.tensor_scalar(rstd[:, t:t + 1], stats[:, t:t + 1], 1.0 / D, EPS, ALU.mult, ALU.add))
                    nc.gpsimd.tensor_tensor(rstd[:, t:t + 1], rstd[:, t:t + 1], minus_half[:, 0:1],
                                            ALU.pow).then_inc(f_rs, 1)

            @block.vector
            def _(dve):
                dve.wait_ge(f_ld, 16)
                for t in range(NT):
                    dve.wait_ge(f_rs, t + 1)
                    nc.vector.scalar_tensor_tensor(fin[:, t, :], x[:, t, :], rstd[:, t:t + 1], fin_w,
                                                   ALU.mult, ALU.mult).then_inc(f_o, 1)


_INS = ['x', 'c', 'ctx', 'c_ctx', 'ada_w', 'ada_b', 'norm_mix_w', 'norm_ffn_w', 'w_in', 'w_out', 'ret_log_decay',
        'diff_lambda', 'diff_subln_w', 'pool_w', 'pool_scale', 'router_w', 'router_b', 'moe_w_gate', 'moe_w_up',
        'moe_w_down', 'final_norm_w']


def kernel(**inputs):
    import concourse.bacc as bacc
    from concourse.bass_utils import run_bass_kernel_spmd

    nc = bacc.Bacc("TRN2", target_bir_lowering=False, num_devices=1)
    arrays = {f"in_{n}": np.ascontiguousarray(inputs[n]) for n in _INS}
    arrays.update(constants())
    aps = {}
    for name, arr in arrays.items():
        ap = nc.dram_tensor(name, arr.shape, mybir.dt.from_np(arr.dtype), kind="ExternalInput").ap()
        aps[name.removeprefix("in_")] = ap
    out = nc.dram_tensor("out_0", (1, SEQ, D), F32, kind="ExternalOutput").ap()
    build_program(nc, aps, out)
    r = run_bass_kernel_spmd(nc, [arrays], core_ids=[0])
    return r.results[0]["out_0"]
```

```python
from contextlib import ExitStack
import math

import numpy as np

import concourse.bass as bass
from concourse import mybir

ALU = mybir.AluOpType
ACT = mybir.ActivationFunctionType
AX = mybir.AxisListType
F32 = mybir.dt.float32
I32 = mybir.dt.int32
U32 = mybir.dt.uint32
I16 = mybir.dt.int16

P = 128
D, SEQ, CTX, DEPTH = 1024, 512, 256, 2
KD = D // P
NT, NC = SEQ // P, CTX // P
NK = NT + NC
HEADS, DK, DV = 4, 64, 128
NE, NG, DE = 16, 4, 512
KE = DE // P
HALF = 512
EPS = 1e-6
LAM_INIT = 0.8 - 0.6 * math.exp(-0.3 * 0)
WINDOWS = (2, 4, 8, 16)
GRID_W = 64
SLOT_W = 4096
GAP_W = SEQ + 7 * P
GAP_0 = 5 * P
LIST_N = NE * SEQ

SH1, SC1, G1, SH2, SC2, G2 = range(6)
C_ROW, CC_ROW, NM_ROW, SMALL_ROWS = 0, KD, 2 * KD, 3 * KD


def constants():
    half = DK // 4
    inv = 10000.0 ** (-np.arange(half, dtype=np.float32) / np.float32(half))
    pos = np.arange(SEQ)
    tables = []
    for p in (pos // GRID_W, pos % GRID_W):
        ang = p.astype(np.float32)[:, None] * inv.astype(np.float32)[None, :]
        tables.append((np.cos(ang), np.sin(ang)))
    rope_cos = np.concatenate([tables[0][0], tables[0][0], tables[1][0], tables[1][0]], 1)
    rope_sin = np.concatenate([-tables[0][1], tables[0][1], -tables[1][1], tables[1][1]], 1)
    gap = (np.arange(GAP_W) - GAP_0)[None, :] - np.arange(P)[:, None]
    before = np.triu(np.ones((P, P), np.float32), 1)
    bands = np.zeros((P, len(WINDOWS), 5, P), np.float32)
    for g, w in enumerate(WINDOWS):
        left, right = w // 2, w - 1 - w // 2
        full = np.zeros((SEQ, SEQ), np.float64)
        for t in range(SEQ):
            lo, hi = max(t - left, 0), min(t + right + 1, SEQ)
            full[lo:hi, t] = 1.0 / (hi - lo)
            full[t, t] -= 1.0
        for b, (a, t) in enumerate([(0, 0), (1, 1), (NT - 1, NT - 1), (0, 1), (2, 1)]):
            bands[:, g, b] = full[a * P:(a + 1) * P, t * P:(t + 1) * P]
    rows = np.zeros((2, NE), np.float32)
    rows[0] = np.arange(NE)
    rows[1] = np.arange(NE) // (NE // NG)
    token = np.arange(SEQ, dtype=np.int32).reshape(NT, P).T
    return {
        "k_ident": np.eye(P, dtype=np.float32), "k_cos": rope_cos.astype(np.float32),
        "k_sin": rope_sin.astype(np.float32), "k_gap": gap.astype(np.int16), "k_before": before,
        "k_bands": bands.reshape(P, -1), "k_rows": rows, "k_token": np.ascontiguousarray(token),
        "k_places": np.arange(P, dtype=np.float32)[None, :],
        "k_zero": np.zeros((P, LIST_N // P), np.int32),
    }


def build_program(nc, a, out):
    ctx = ExitStack()
    with ctx, nc.allow_non_contiguous_dma(reason="short rows of small tables"):
        def sb(name, shape, dt=F32):
            return ctx.enter_context(nc.sbuf_tensor(name, shape, dt))

        half_load = [nc.alloc_semaphore(name=f"half_slot{r}_loaded") for r in range(6)]
        held = []

        def sem(name):
            held.append(nc.alloc_semaphore(name=name))
            return held[-1]

        def stage_over():
            nc.clear_and_free_semaphores(list(held))
            held.clear()
            nc.all_engine_barrier()

        xh_dram = nc.dram_tensor("xh_scratch", [SEQ, D], F32).ap()
        list_dram = nc.dram_tensor("list_scratch", [LIST_N, 1], I32).ap()
        y_dram = nc.dram_tensor("y_scratch", [LIST_N, D], F32).ap()
        mod_dram = nc.dram_tensor("mod_scratch", [DEPTH, 6 * D], F32).ap()

        def mod_row(l, part):
            return mod_dram[l, part * D:(part + 1) * D].partition_broadcast(P)

        bank = ctx.enter_context(nc.psum_tensor("bank", [P, 8, HALF], F32))

        x = sb("x_res", [P, NT, D])
        ident = sb("ident", [P, P])
        ones = sb("ones", [P, P])
        small = sb("small", [P, SMALL_ROWS])
        bias_cols = sb("bias_cols", [P, 2 * KD])
        silu_c = sb("silu_c", [P, 2, KD])
        mod = sb("mod", [P, 2 * KD, 2])
        norm_a = sb("norm_a", [P, 2, KD])
        gate1_b = sb("gate1_b", [P, D])
        gate2_b = sb("gate2_b", [P, D])
        stats = sb("stats", [P, 8])
        rstd = sb("rstd", [P, 8])
        minus_half = sb("minus_half", [P, NT])
        idx_zero = sb("credit", [1, 2])
        weight = sb("weight", [P, 2, NT])
        row_of = sb("row_of", [P, 2, NT], U32)
        max_count = sb("max_count", [P, 1], I32)
        ring = sb("ring", [P, 3, SLOT_W])

        mem = {"stack": None, "arena": None, "stages": 0}

        def stage_memory(words):
            if mem["stack"]:
                mem["stack"].close()
            mem["stack"] = ctx.enter_context(ExitStack())
            mem["stages"] += 1
            mem["arena"] = stage_sb("arena", [P, words])

        def stage_sb(name, shape, dt=F32):
            return mem["stack"].enter_context(nc.sbuf_tensor(f"{name}{mem['stages']}", shape, dt))

        def carve(start, *dims):
            arena = mem["arena"]
            n = int(np.prod(dims))
            v = arena[:, start:start + n]
            if len(dims) > 1:
                names = " ".join(f"d{i}" for i in range(len(dims)))
                v = v.rearrange(f"p ({names}) -> p {names}", **{f"d{i}": d for i, d in enumerate(dims)})
            return v, start + n

        def linker(eng, s):
            n = [0]

            def link(ins):
                n[0] += 1
                ins.then_inc(s, 1)
                eng.wait_ge(s, n[0])
            return link

        def cols(ap, width):
            return ap.unsqueeze(2).to_broadcast([P, ap.shape[1], width])

        stage_memory(28672)
        arena = mem["arena"]
        ring_last = stage_sb("ring_last", [P, SLOT_W])
        qT, at = carve(0, 6, SEQ)
        kT, at = carve(at, 6, NK * P)
        v_tok, at = carve(at, NK, 2 * HEADS * DV)
        gate, late = carve(at, NT, HEADS * DV)
        hT, at = carve(late, KD, SEQ)
        hcT, at = carve(at, KD, CTX)
        xhat2, at = carve(at, 2, D)
        ctx_raw, at = carve(at, NC, D)
        at_rope = at
        rope_x, at = carve(at, HALF)
        rope_y, at = carve(at, HALF)
        roped, at = carve(at, 2, HALF)
        cos_t, at = carve(at, NT, DK)
        sin_t, at = carve(at, NT, DK)
        decay, at = carve(late, 2, GAP_W)
        decay_c, at = carve(at, NC, SEQ)
        retp, _ = carve(at, 4, SEQ)
        prob, at = carve(at, 2, 2, NK * P)
        diffp, at = carve(at, NK * P)
        diffT, at = carve(at, NK, P)
        dif_out, at = carve(at, NT, HEADS * DV)
        squares, at = carve(at, NT, DV)
        decay_arg, at = carve(at, P)
        lam_pr, at = carve(at, 2, DK)
        hstat, at = carve(at, 2 * HEADS, NT)
        hrstd, at = carve(at, 2 * HEADS, NT)
        ada_acc = gate2_b[:].rearrange("p (b c) -> p b c", b=2)
        ada_first = stage_sb("ada_first", [P, HALF])
        ada_row = stage_sb("ada_row", [1, HALF])
        mixT = kT.rearrange("p a b -> p (a b)")[:, 0:KD * SEQ].rearrange("p (k t) -> p k t", k=KD)

        gap = gate1_b[:, 0:GAP_W // 2].bitcast(I16)
        gap_pos = gate1_b[:, GAP_W // 2:GAP_W // 2 + P]
        gap_neg = gate1_b[:, GAP_W // 2 + P:GAP_W // 2 + 2 * P]
        ld = stage_sb("ld", [P, 2 * HEADS])
        ld_neg = stage_sb("ld_neg", [P, 2 * HEADS])
        lam_in = stage_sb("lam_in", [P, 4 * DK])
        lam_s = stage_sb("lam_s", [P, 2])
        lam_e = stage_sb("lam_e", [P, 2])
        lam_v = stage_sb("lam_v", [P, 2])
        subln = stage_sb("subln", [P, DV])
        smax = stage_sb("smax", [P, 2, 2])
        sden = stage_sb("sden", [P, 2, 2])
        srec = stage_sb("srec", [P, 2, 2])

        w_in, w_out, ada_w = a["w_in"], a["w_out"], a["ada_w"]

        def slot(i):
            return ring[:, i, :] if i < 3 else ring_last[:]

        HALF_W = SLOT_W // 2

        def half(r):
            return ring[:, r // 2, (r % 2) * HALF_W:(r % 2 + 1) * HALF_W]

        def put_half(eng, l, e, r, into=None):
            into = r if into is None else into
            w, rows, k = ((a["moe_w_gate"], D // 2, KD // 2), (a["moe_w_up"], D // 2, KD // 2),
                          (a["moe_w_down"], DE // 2, KE // 2))[r // 2]
            src = w[l][bass.ds(e, 1), (r % 2) * rows:(r % 2 + 1) * rows].rearrange("a (k p) c -> p (a k) c", p=P)
            eng.dma_start(half(into).rearrange("p (k c) -> p k c", k=k), src).then_inc(half_load[into], 16)

        def put(eng, w, e, i, k):
            src = w[bass.ds(e, 1)].rearrange("a (k p) c -> p (a k) c", p=P)
            return eng.dma_start(slot(i).rearrange("p (k c) -> p k c", k=k), src)

        def slab(w, c0):
            return w[:, c0:c0 + HALF].rearrange("(k p) c -> p k c", p=P)

        PRE = 2 * D // HALF
        rest = [(0, j) for j in range(PRE, 12)] + [(1, j) for j in range(12)]
        REST_PER = 4

        units = [(j, t) for j in range(6) for t in range(NK if j >= 2 else NT)]

        def parts(j, t):
            p = {0: [(0, 256, "q", 0), (256, 256, "q", 2)], 1: [(0, 256, "q", 4), (256, 256, "g", 0)],
                 2: [(0, 256, "g", 256), (256, 256, "k", 0)], 3: [(0, 512, "v", 0)],
                 4: [(0, 512, "k", 2)], 5: [(0, 512, "v", 512)]}[j]
            return [q for q in p if t < NT or q[2] not in "qg"]

        slabs_after, rows_after = {}, {}
        for i in range(len(rest)):
            u = int(1.45 * i)
            slabs_after.setdefault(u, []).append(i)
            rows_after.setdefault(u + 2, []).append(i)
        assert max(rows_after) < len(units)
        roped_units = [u for u, (j, t) in enumerate(units) if any(q[2] in "qk" for q in parts(j, t))]
        gate_units = [u for u, (j, t) in enumerate(units) if any(q[2] == "g" for q in parts(j, t))]
        v_units = [u for u, (j, t) in enumerate(units) if any(q[2] == "v" for q in parts(j, t))]

        m_ld = {n: sem(f"m_ld_{n}") for n in ("ident", "smallA", "smallB", "rope", "row", "gap", "zero")}
        m_x = [sem(f"m_x{t}") for t in range(NK)]
        m_small = sem("m_small_transposed")
        m_cols = sem("m_small_cols")
        m_silu = sem("m_silu_c")
        m_slot = [sem(f"m_slot{i}_loaded") for i in range(4)]
        m_pre = sem("m_adaln_rows_of_slab")
        m_prc = sem("m_adaln_rows_copied")
        m_prt = sem("m_adaln_rows_transposed")
        m_az = sem("m_adaln_first_zeroed")
        m_ab = sem("m_adaln_bias_loaded")
        m_au = sem("m_adaln_bias_used")
        m_as = sem("m_adaln_slab_summed")
        m_ar = sem("m_adaln_row")
        m_arc = sem("m_adaln_row_copied")
        m_ast = sem("m_adaln_row_stored")
        m_g1 = sem("m_g1_loaded")
        m_na = sem("m_norm_a_ready")
        m_sq = sem("m_square_sum")
        m_rs = sem("m_rstd")
        m_xh = sem("m_xhat")
        m_xt = sem("m_xhat_transposed")
        m_hta = sem("m_hT_by_act")
        m_htd = sem("m_hT_by_dve")
        m_proj = sem("m_projected")
        m_rope = sem("m_roped")
        m_gv = sem("m_gate_or_v_copied")
        m_qkt = sem("m_qk_transposed")
        m_qkc = sem("m_qk_copied")
        m_dchain = sem("m_dve_chain")
        m_pchain = sem("m_pool_chain")
        m_lam = sem("m_lambda_sums")
        m_lame = sem("m_lambda_exps")
        m_gapc = sem("m_decay_args")
        m_dk_arg = sem("m_decay_arg")
        m_dk = sem("m_decay_exp")
        m_rs_s = sem("m_ret_scores")
        m_rs_p = sem("m_ret_masked")
        m_rs_v = sem("m_ret_values_done")
        m_o = sem("m_head_out")
        m_osq = sem("m_head_squares")
        m_ost = sem("m_head_stat")
        m_orr = sem("m_head_rstd")
        m_on = sem("m_head_normed")
        m_ds = sem("m_diff_scores")
        m_db = sem("m_diff_pair0_scores")
        m_dm = sem("m_diff_max")
        m_de = sem("m_diff_exp")
        m_dp = sem("m_diff_combined")
        m_dt = sem("m_diff_transposed")
        m_dc = sem("m_diff_copied")
        m_mt = sem("m_mix_transposed")
        m_mtc = sem("m_mix_copied")
        m_op = sem("m_out_projected")
        m_xr = sem("m_x_updated")
        m_mset = sem("m_memsets")

        RU = HEADS * NK
        DU = HEADS * NT

        def three_banks(u):
            return bank[:, 3 * (u % 2):3 * (u % 2) + 3, :].rearrange("p b c -> p (b c)")

        def pair(u, c):
            return three_banks(u)[:, c * NK * P:(c + 1) * NK * P]

        PAIR_PIECES = [((0, HALF), (HALF, NK * P)), ((2 * HALF - NK * P, NK * P), (0, 2 * HALF - NK * P))]

        upd = qT.rearrange("p a b -> p (a b)")[:, 0:HALF]
        pre_rows = arena[0:2, at_rope:at_rope + 2 * D]

        with nc.Block() as block:

            @block.sync
            def _(sp):
                def load(i, w, j, k=KD):
                    return sp.dma_start(slot(i).rearrange("p (k c) -> p k c", k=k), slab(w, j * HALF)
                                        ).then_inc(m_slot[i], 16)

                sp.wait_ge(m_ld["ident"], 16)
                sp.wait_ge(m_ld["smallA"], 3 * 16)
                sp.wait_ge(m_ld["smallB"], 16)
                load(0, ada_w[0], 0)
                for j in range(1, PRE):
                    load(j, ada_w[0], j)
                    for t in (2 * j - 2, 2 * j - 1):
                        src, dst, r0 = ((a["x"][0], x[:, t, :], t * P) if t < NT else
                                        (a["ctx"][0], ctx_raw[:, t - NT, :], (t - NT) * P))
                        sp.dma_start(dst, src[r0:r0 + P, :]).then_inc(m_x[t], 16)
                sp.wait_ge(m_pre, 3)
                load(2, w_in[0], 0)
                sp.wait_ge(m_pre, 4)
                load(3, w_in[0], 1)
                sp.wait_ge(m_az, 1)
                for i, (l, j) in enumerate(rest):
                    if i >= 2:
                        sp.wait_ge(m_as, i - 1)
                    load(i % 2, ada_w[l], j)
                    if i >= 1:
                        sp.wait_ge(m_au, i)
                    sp.dma_start(ada_first[0:1, :], a["ada_b"][l:l + 1, j * HALF:(j + 1) * HALF]).then_inc(m_ab, 16)
                    if i % REST_PER == REST_PER - 1 and i // REST_PER < 4:
                        n = i // REST_PER
                        sp.wait_ge(m_proj, max(u for u, (s, _) in enumerate(units) if s == n) + 1)
                        load(2 + n % 2, w_in[0], n + 2)
                for j in range(2):
                    sp.wait_ge(m_proj, max(u for u, (s, _) in enumerate(units) if s == 4 + j) + 1)
                    load(2 + j, w_out[0], j)
                sp.wait_ge(m_dk, 2 * HEADS)
                sp.wait_ge(m_ast, 16 * len(rest))
                sp.dma_start(gate1_b[:], mod_row(0, G1)).then_inc(m_g1, 16)
                sp.wait_ge(m_as, len(rest))
                for h in range(4):
                    put_half(sp, 0, 0, h)
                sp.wait_ge(m_op, NT)
                for h in (4, 5):
                    put_half(sp, 0, 0, h)

            @block.scalar
            def _(act):
                act.dma_start(ident[:], a["k_ident"]).then_inc(m_ld["ident"], 16)
                for r0, src in ((C_ROW, a["c"][0]), (CC_ROW, a["c_ctx"]), (NM_ROW, a["norm_mix_w"][0])):
                    act.dma_start(arena[r0:r0 + KD, 0:P], src.rearrange("(r c) -> r c", c=P)).then_inc(m_ld["smallA"], 16)
                act.dma_start(arena[0:2 * KD, P:2 * P],
                              a["ada_b"][0, 0:2 * D].rearrange("(r c) -> r c", c=P)).then_inc(m_ld["smallB"], 16)
                act.wait_ge(m_cols, 1)
                nc.scalar.activation(silu_c[:].rearrange("p v k -> p (v k)"), small[:, C_ROW:C_ROW + 2 * KD],
                                     ACT.Silu).then_inc(m_silu, 1)

                def squares_of(t):
                    act.wait_ge(m_x[t], 16)
                    if t >= 2:
                        act.wait_ge(m_xt, t - 1)
                    src = x[:, t, :] if t < NT else ctx_raw[:, t - NT, :]
                    nc.scalar.activation(xhat2[:, t % 2, :], src, ACT.Square,
                                         accum_out=stats[:, t:t + 1]).then_inc(m_sq, 1)

                def hT_of(t):
                    act.wait_ge(m_xt, t + 1)
                    act.wait_ge(m_na, 1)
                    v, na = (0, 0) if t < NT else (1, 1)
                    for k in range(KD // 2):
                        dst = hT[:, k, t * P:(t + 1) * P] if t < NT else hcT[:, k, (t - NT) * P:(t - NT + 1) * P]
                        last = nc.scalar.activation(dst, bank[:, (t % 2) * 2 + k // 4, (k % 4) * P:(k % 4 + 1) * P],
                                                    ACT.Identity, scale=norm_a[:, na, k:k + 1],
                                                    bias=mod[:, k, v:v + 1])
                    last.then_inc(m_hta, 1)

                squares_of(0)
                squares_of(1)
                act.wait_ge(m_slot[PRE - 1], 16)
                act.dma_start(cos_t, a["k_cos"].rearrange("(t p) c -> p t c", p=P)).then_inc(m_ld["rope"], 16)
                act.dma_start(sin_t, a["k_sin"].rearrange("(t p) c -> p t c", p=P)).then_inc(m_ld["rope"], 16)
                act.dma_start(gap, a["k_gap"]).then_inc(m_ld["gap"], 16)
                act.dma_start(list_dram.rearrange("(p c) o -> p (c o)", p=P), a["k_zero"]).then_inc(m_ld["zero"], 16)
                act.dma_start(ld[:], a["ret_log_decay"].rearrange("n d h -> n (d h)").partition_broadcast(P)
                              .rearrange("p n c -> p (n c)")).then_inc(m_ld["row"], 16)
                act.dma_start(lam_in[:], a["diff_lambda"].rearrange("n d h -> n (d h)").partition_broadcast(P)
                              .rearrange("p n c -> p (n c)")).then_inc(m_ld["row"], 16)
                act.dma_start(subln[:], a["diff_subln_w"].partition_broadcast(P)
                              .rearrange("p n c -> p (n c)")).then_inc(m_ld["row"], 16)
                for t in range(NK):
                    hT_of(t)
                    if t + 2 < NK:
                        squares_of(t + 2)

                def copy_qk(r):
                    j, t = units[roped_units[r]]
                    act.wait_ge(m_qkt, r + 1)
                    for c0, w, kind, b0 in parts(j, t):
                        if kind in "qk":
                            dst = (qT if kind == "q" else kT)[:, b0:b0 + w // P, t * P:(t + 1) * P]
                            last = nc.scalar.copy(dst, bank[:, 4 + r % 2, c0:c0 + w].rearrange("p (b c) -> p b c", c=P))
                    last.then_inc(m_qkc, 1)

                def copy_ada_row(i):
                    act.wait_ge(m_ar, i + 1)
                    if i >= 1:
                        act.wait_ge(m_ast, 16 * i)
                    nc.scalar.copy(ada_row[:], bank[0:1, 6 + i % 2, :]).then_inc(m_arc, 1)
                    act.wait_ge(m_arc, i + 1)
                    l, j = rest[i]
                    act.dma_start(mod_dram[l:l + 1, j * HALF:(j + 1) * HALF], ada_row[:]).then_inc(m_ast, 16)

                r = 0
                for u, (j, t) in enumerate(units):
                    for c0, w, kind, b0 in parts(j, t):
                        if kind not in "gv":
                            continue
                        act.wait_ge(m_proj, u + 1)
                        if u in roped_units:
                            act.wait_ge(m_rope, roped_units.index(u) + 1)
                        ps = bank[:, u % 3, c0:c0 + w]
                        if kind == "g":
                            nc.scalar.activation(gate[:, t, b0:b0 + w], ps, ACT.Silu).then_inc(m_gv, 1)
                        else:
                            nc.scalar.copy(v_tok[:, t, b0:b0 + w], ps).then_inc(m_gv, 1)
                    while r < len(roped_units) and roped_units[r] <= u - 1:
                        copy_qk(r)
                        r += 1
                    for i in rows_after.get(u - 1, ()):
                        copy_ada_row(i)
                for i in rows_after.get(len(units) - 1, ()):
                    copy_ada_row(i)
                while r < len(roped_units):
                    copy_qk(r)
                    r += 1

                act.wait_ge(m_lam, 1)
                nc.scalar.activation(lam_e[:], lam_s[:], ACT.Exp).then_inc(m_lame, 1)

                def decay_of(h):
                    act.wait_ge(m_proj, len(units))
                    if h >= 2:
                        act.wait_ge(m_rs_p, NK * (h - 1))
                    d = decay[:, h % 2, :]
                    nc.scalar.activation(d[:, GAP_0 + P:], gap[:, GAP_0 + P:], ACT.Exp, scale=ld[:, h:h + 1])
                    nc.scalar.activation(d[:, 0:GAP_0], gap[:, 0:GAP_0], ACT.Exp,
                                         scale=ld_neg[:, HEADS + h:HEADS + h + 1]).then_inc(m_dk, 1)
                    act.wait_ge(m_dk_arg, h + 1)
                    nc.scalar.activation(d[:, GAP_0:GAP_0 + P], decay_arg, ACT.Exp).then_inc(m_dk, 1)

                def head_squares(n):
                    if n < HEADS:
                        act.wait_ge(m_rs_v, NK * (n + 1))
                    else:
                        act.wait_ge(m_o, n - HEADS + 1)
                    if n >= 1:
                        act.wait_ge(m_ost, n)
                    nc.scalar.activation(squares, bank[:, 6 + n % 2, :].rearrange("p (t c) -> p t c", c=DV),
                                         ACT.Square).then_inc(m_osq, 1)

                act.wait_ge(m_gapc, 1)
                decay_of(0)
                decay_of(1)
                for h in range(HEADS):
                    head_squares(h)
                    if h + 2 < HEADS:
                        decay_of(h + 2)

                def exps(u):
                    act.wait_ge(m_dm, u + 1)
                    if u >= 2:
                        act.wait_ge(m_dp, u - 1)
                    for c in range(2):
                        nc.scalar.activation(prob[:, u % 2, c, :], pair(u, c), ACT.Exp, scale=DK ** -0.5,
                                             bias=smax[:, u % 2, c:c + 1],
                                             accum_out=sden[:, u % 2, c:c + 1]).then_inc(m_de, 1)

                def copy_T(u):
                    act.wait_ge(m_dt, u + 1)
                    nc.scalar.copy(diffT.rearrange("p t c -> p (t c)"), pair(u, 0)).then_inc(m_dc, 1)

                for u in range(DU):
                    if u >= 1:
                        copy_T(u - 1)
                    exps(u)
                    if u >= 3 and (u - 3) % NT == NT - 1:
                        head_squares(HEADS + (u - 3) // NT)
                copy_T(DU - 1)
                for h in range((DU - 3) // NT, HEADS):
                    head_squares(HEADS + h)
                for hh in range(2 * HEADS):
                    act.wait_ge(m_mt, hh + 1)
                    nc.scalar.copy(mixT[:, hh, :], bank[:, hh % 4, :]).then_inc(m_mtc, 1)

            @block.gpsimd
            def _(pool):
                link = linker(pool, m_pchain)
                link(nc.gpsimd.memset(minus_half[:], -0.5))
                for t in range(NK):
                    pool.wait_ge(m_sq, t + 1)
                    link(nc.gpsimd.tensor_scalar(rstd[:, t:t + 1], stats[:, t:t + 1], 1.0 / D, EPS, ALU.mult, ALU.add))
                    nc.gpsimd.tensor_tensor(rstd[:, t:t + 1], rstd[:, t:t + 1], minus_half[:, 0:1],
                                            ALU.pow).then_inc(m_rs, 1)
                nc.gpsimd.memset(ada_first[:], 0.0).then_inc(m_az, 1)
                for n in range(2 * HEADS):
                    pool.wait_ge(m_ost, n + 1)
                    link(nc.gpsimd.tensor_scalar(hrstd[:, n, :], hstat[:, n, :], 1.0 / DV, EPS, ALU.mult, ALU.add))
                    nc.gpsimd.tensor_tensor(hrstd[:, n, :], hrstd[:, n, :], minus_half[:], ALU.pow).then_inc(m_orr, 1)

            @block.vector
            def _(dve):
                link = linker(dve, m_dchain)
                nc.vector.memset(ones[:], 1.0).then_inc(m_mset, 1)
                dve.wait_ge(m_small, 1)
                nc.vector.tensor_copy(small[:], bank[:, 6, 0:SMALL_ROWS]).then_inc(m_cols, 1)
                nc.vector.tensor_copy(bias_cols[:], bank[:, 6, P:P + 2 * KD]).then_inc(m_cols, 1)

                def xhat_of(t):
                    dve.wait_ge(m_rs, t + 1)
                    src = x[:, t, :] if t < NT else ctx_raw[:, t - NT, :]
                    nc.vector.tensor_scalar(xhat2[:, t % 2, :], src, rstd[:, t:t + 1], None, ALU.mult).then_inc(m_xh, 1)

                def hT_of(t):
                    dve.wait_ge(m_xt, t + 1)
                    v, na = (0, 0) if t < NT else (1, 1)
                    for k in range(KD // 2, KD):
                        dst = hT[:, k, t * P:(t + 1) * P] if t < NT else hcT[:, k, (t - NT) * P:(t - NT + 1) * P]
                        last = nc.vector.tensor_scalar(dst, bank[:, (t % 2) * 2 + k // 4, (k % 4) * P:(k % 4 + 1) * P],
                                                       norm_a[:, na, k:k + 1], mod[:, k, v:v + 1],
                                                       ALU.mult, ALU.add)
                    last.then_inc(m_htd, 1)

                xhat_of(0)
                xhat_of(1)
                dve.wait_ge(m_cols, 2)
                for j in range(PRE):
                    dve.wait_ge(m_pre, j + 1)
                    nc.vector.tensor_copy(pre_rows[:, j * HALF:(j + 1) * HALF], bank[0:2, 4 + j, :]).then_inc(m_prc, 1)
                dve.wait_ge(m_prt, 1)
                link(nc.vector.tensor_tensor(mod[:], bank[:, 4, 0:4 * KD].rearrange("p (j v) -> p j v", v=2),
                                             cols(bias_cols[:], 2), ALU.add))
                for v in range(2):
                    ins = nc.vector.scalar_tensor_tensor(norm_a[:, v, :], mod[:, KD:2 * KD, v], 1.0,
                                                         small[:, NM_ROW:NM_ROW + KD], ALU.add, ALU.mult)
                ins.then_inc(m_na, 1)
                dve.wait_ge(m_na, 1)
                for t in range(NK):
                    hT_of(t)
                    if t + 2 < NK:
                        xhat_of(t + 2)

                def ada_slab(i):
                    dve.wait_ge(m_slot[i % 2], 16 * (i // 2 + 2))
                    dve.wait_ge(m_ab, 16 * (i + 1))
                    if i >= 2:
                        dve.wait_ge(m_ar, i - 1)
                    w = slot(i % 2).rearrange("p (k c) -> p k c", k=KD)
                    for k in range(KD):
                        onto = ada_first[:] if k == 0 else ada_acc[:, i % 2, :]
                        ins = nc.vector.scalar_tensor_tensor(ada_acc[:, i % 2, :], w[:, k, :], silu_c[:, 0, k:k + 1],
                                                             onto, ALU.mult, ALU.add)
                        if k == 0:
                            ins.then_inc(m_au, 1)
                            dve.wait_ge(m_au, i + 1)
                        elif k < KD - 1:
                            link(ins)
                    ins.then_inc(m_as, 1)

                def rope(r, u):
                    j, t = units[u]
                    dve.wait_ge(m_proj, u + 1)
                    if r >= 2:
                        dve.wait_ge(m_qkt, r - 1)
                    if r >= 1:
                        dve.wait_ge(m_rope, r)
                    ps = bank[:, u % 3, :]
                    got = [q for q in parts(j, t) if q[2] in "qk"]
                    c0, w = got[0][0], sum(q[1] for q in got)
                    dst = roped[:, r % 2, c0:c0 + w]
                    if t >= NT:
                        nc.vector.tensor_copy(dst, ps[:, c0:c0 + w]).then_inc(m_rope, 1)
                        return
                    n = w // DK
                    nc.vector.tensor_tensor(
                        rope_x[:, 0:w].rearrange("p (h c) -> p h c", c=DK),
                        ps[:, c0:c0 + w].rearrange("p (h c) -> p h c", c=DK),
                        cos_t[:, t, :].unsqueeze(1).to_broadcast([P, n, DK]), ALU.mult)
                    swap = ps[:, c0:c0 + w].rearrange("p (h g s c) -> p h g s c", g=2, s=2, c=DK // 4)
                    turned = rope_y[:, 0:w].rearrange("p (h g s c) -> p h g s c", g=2, s=2, c=DK // 4)
                    sine = sin_t[:, t, :].rearrange("p (g s c) -> p g s c", g=2, s=2)
                    for s in range(2):
                        ins = nc.vector.tensor_tensor(
                            turned[:, :, :, s, :], swap[:, :, :, 1 - s, :],
                            sine[:, :, s, :].unsqueeze(1).to_broadcast([P, n, 2, DK // 4]), ALU.mult)
                    link(ins)
                    nc.vector.tensor_tensor(dst, rope_x[:, 0:w], rope_y[:, 0:w], ALU.add).then_inc(m_rope, 1)
                dve.wait_ge(m_ld["rope"], 32)
                dve.wait_ge(m_az, 1)
                for u in range(len(units)):
                    if u in roped_units:
                        rope(roped_units.index(u), u)
                    for i in slabs_after.get(u, ()):
                        ada_slab(i)

                dve.wait_ge(m_ld["row"], 48)
                dve.wait_ge(m_proj, len(units))
                lv = lam_in[:].rearrange("p (a b c) -> p a b c", a=2, b=2)
                link(nc.vector.tensor_tensor(lam_pr, lv[:, :, 0, :], lv[:, :, 1, :], ALU.mult))
                nc.vector.tensor_reduce(lam_s[:], lam_pr, AX.X, ALU.add).then_inc(m_lam, 1)
                nc.vector.tensor_scalar(subln[:], subln[:], 1.0 - LAM_INIT, None, ALU.mult)
                nc.vector.tensor_scalar(ld_neg[:], ld[:], -1.0, None, ALU.mult)
                dve.wait_ge(m_ld["gap"], 16)
                nc.vector.tensor_scalar(gap_pos, gap[:, GAP_0:GAP_0 + P], 0.0, None, ALU.max)
                nc.vector.tensor_scalar(gap_neg, gap[:, GAP_0:GAP_0 + P], 0.0, None, ALU.min).then_inc(m_gapc, 1)
                dve.wait_ge(m_gapc, 1)
                nc.vector.memset(lam_v[:, 0:1], 1.0)
                dve.wait_ge(m_lame, 1)
                link(nc.vector.tensor_tensor(lam_v[:, 1:2], lam_e[:, 1:2], lam_e[:, 0:1], ALU.subtract))
                link(nc.vector.tensor_scalar(lam_v[:, 1:2], lam_v[:, 1:2], -LAM_INIT, None, ALU.add))

                def decay_arg_of(h):
                    if h >= 1:
                        dve.wait_ge(m_dk, 2 * h)
                    link(nc.vector.tensor_scalar(decay_arg, gap_pos, ld[:, h:h + 1], None, ALU.mult))
                    nc.vector.scalar_tensor_tensor(decay_arg, gap_neg, ld_neg[:, HEADS + h:HEADS + h + 1],
                                                   decay_arg, ALU.mult, ALU.add).then_inc(m_dk_arg, 1)

                def decay_finish(h):
                    dve.wait_ge(m_dk, 2 * h + 2)
                    d = decay[:, h % 2, :]
                    ins = nc.vector.tensor_tensor(d[:, GAP_0:GAP_0 + P], d[:, GAP_0:GAP_0 + P], ident[:], ALU.add)
                    for cp in range(NC):
                        f0, b0 = GAP_0 - P * (cp - NC), GAP_0 - P * (NT + cp)
                        ins = nc.vector.tensor_tensor(decay_c[:, cp, :], d[:, f0:f0 + SEQ], d[:, b0:b0 + SEQ], ALU.add)
                    link(ins)

                def head_stat(n):
                    dve.wait_ge(m_osq, n + 1)
                    nc.vector.tensor_reduce(hstat[:, n, :], squares, AX.X, ALU.add).then_inc(m_ost, 1)

                def head_norm(n):
                    dve.wait_ge(m_orr, n + 1)
                    o = bank[:, 6 + n % 2, :].rearrange("p (t c) -> p t c", c=DV)
                    for t in range(NT):
                        if n < HEADS:
                            dst = gate[:, t, n * DV:(n + 1) * DV]
                            with_ = dst
                        else:
                            dst = dif_out[:, t, (n - HEADS) * DV:(n - HEADS + 1) * DV]
                            with_ = subln[:]
                        ins = nc.vector.scalar_tensor_tensor(dst, o[:, t, :], hrstd[:, n, t:t + 1], with_,
                                                             ALU.mult, ALU.mult)
                    ins.then_inc(m_on, 1)

                decay_arg_of(0)
                decay_arg_of(1)
                for h in range(HEADS):
                    decay_finish(h)
                    for m in range(NK):
                        u = h * NK + m
                        dve.wait_ge(m_rs_s, u + 1)
                        if u >= 4:
                            dve.wait_ge(m_rs_v, u - 3)
                        win = (decay[:, h % 2, GAP_0 - P * m:GAP_0 - P * m + SEQ] if m < NT
                               else decay_c[:, m - NT, :])
                        nc.vector.tensor_tensor(retp[:, u % 4, :], bank[:, u % 4, :], win, ALU.mult).then_inc(m_rs_p, 1)
                        if m == 2 and h >= 1:
                            head_stat(h - 1)
                        if m == 4 and h >= 1:
                            head_norm(h - 1)
                    if h + 2 < HEADS:
                        decay_arg_of(h + 2)
                    dve.wait_ge(m_rs_p, NK * (h + 1))
                head_stat(HEADS - 1)
                head_norm(HEADS - 1)

                def combine(u):
                    b = u % 2
                    dve.wait_ge(m_de, 2 * u + 2)
                    link(nc.vector.reciprocal(srec[:, b, :], sden[:, b, :]))
                    link(nc.vector.tensor_tensor(srec[:, b, :], srec[:, b, :], lam_v[:], ALU.mult))
                    if u >= 1:
                        dve.wait_ge(m_dt, u)
                    link(nc.vector.tensor_scalar(diffp, prob[:, b, 0, :], srec[:, b, 0:1], None, ALU.mult))
                    nc.vector.scalar_tensor_tensor(diffp, prob[:, b, 1, :], srec[:, b, 1:2], diffp,
                                                   ALU.mult, ALU.add).then_inc(m_dp, 1)

                for u in range(DU):
                    if u >= 1:
                        combine(u - 1)
                    dve.wait_ge(m_ds, u + 1)
                    both = three_banks(u).rearrange("p (c n) -> p c n", c=2)
                    link(nc.vector.tensor_reduce(smax[:, u % 2, :], both, AX.X, ALU.max))
                    nc.vector.tensor_scalar(smax[:, u % 2, :], smax[:, u % 2, :], -(DK ** -0.5), None,
                                            ALU.mult).then_inc(m_dm, 1)
                    if u >= 4 and (u - 4) % NT == NT - 1:
                        head_stat(HEADS + (u - 4) // NT)
                        head_norm(HEADS + (u - 4) // NT)
                combine(DU - 1)
                for h in range((DU - 4) // NT, HEADS):
                    head_stat(HEADS + h)
                    head_norm(HEADS + h)

                dve.wait_ge(m_g1, 16)
                for n in range(2 * NT):
                    hf, t = n // NT, n % NT
                    dve.wait_ge(m_op, n + 1)
                    if n >= 1:
                        dve.wait_ge(m_xr, n)
                    link(nc.vector.tensor_tensor(upd, bank[:, 4 + n % 2, :], gate1_b[:, hf * HALF:(hf + 1) * HALF],
                                                 ALU.mult))
                    xs = x[:, t, hf * HALF:(hf + 1) * HALF]
                    nc.vector.tensor_tensor(xs, xs, upd, ALU.add).then_inc(m_xr, 1)

            @block.tensor
            def _(pe):
                pe.wait_ge(m_ld["ident"], 16)
                pe.wait_ge(m_ld["smallA"], 3 * 16)
                pe.wait_ge(m_ld["smallB"], 16)
                pe.transpose(bank[:, 6, 0:SMALL_ROWS], arena[0:SMALL_ROWS, 0:P], ident[0:SMALL_ROWS, 0:SMALL_ROWS])
                nb = 2 * KD
                pe.transpose(bank[:, 6, P:P + nb], arena[0:nb, P:2 * P], ident[0:nb, 0:nb]).then_inc(m_small, 1)

                def slab_in(i, loads):
                    pe.wait_ge(m_slot[i], 16 * loads)
                    return slot(i).rearrange("p (k c) -> p k c", k=KD)

                pe.wait_ge(m_silu, 1)
                pe.wait_ge(m_cols, 2)
                for j in range(PRE):
                    w = slab_in(j, 1)
                    for k in range(KD):
                        last = pe.matmul(bank[0:2, 4 + j, :], silu_c[:, :, k], w[:, k, :], start=(k == 0), stop=(k == KD - 1))
                    last.then_inc(m_pre, 1)
                pe.wait_ge(m_prc, PRE)
                for j in range(2 * KD):
                    last = pe.transpose(bank[:, 4, 2 * j:2 * j + 2], pre_rows[:, j * P:(j + 1) * P], ident[0:2, 0:2])
                last.then_inc(m_prt, 1)

                for t in range(NK):
                    pe.wait_ge(m_xh, t + 1)
                    if t >= 2:
                        pe.wait_ge(m_hta, t - 1)
                        pe.wait_ge(m_htd, t - 1)
                    for k in range(KD):
                        last = pe.transpose(bank[:, (t % 2) * 2 + k // 4, (k % 4) * P:(k % 4 + 1) * P],
                                            xhat2[:, t % 2, k * P:(k + 1) * P], ident[:])
                    last.then_inc(m_xt, 1)
                pe.wait_ge(m_hta, NK)
                pe.wait_ge(m_htd, NK)

                def unit_read(u):
                    if u in rope_at:
                        pe.wait_ge(m_rope, rope_at[u] + 1)
                    if u in gv_at:
                        pe.wait_ge(m_gv, gv_at[u] + 1)

                rope_at = {u: i for i, u in enumerate(roped_units)}
                gv_at = {u: i for i, u in enumerate(sorted(gate_units + v_units))}

                def transpose_unit(u):
                    if u not in rope_at:
                        return
                    r = rope_at[u]
                    pe.wait_ge(m_rope, r + 1)
                    if r >= 2:
                        pe.wait_ge(m_qkc, r - 1)
                    for c0, w, kind, b0 in parts(*units[u]):
                        if kind in "qk":
                            for c in range(c0, c0 + w, P):
                                last = pe.transpose(bank[:, 4 + r % 2, c:c + P], roped[:, r % 2, c:c + P], ident[:])
                    last.then_inc(m_qkt, 1)

                def ada_row_sum(i):
                    pe.wait_ge(m_as, i + 1)
                    if i >= 2:
                        pe.wait_ge(m_arc, i - 1)
                    pe.matmul(bank[0:1, 6 + i % 2, :], ones[:, 0:1], ada_acc[:, i % 2, :],
                              start=True, stop=True).then_inc(m_ar, 1)

                pe.wait_ge(m_mset, 1)
                at_slab = {}
                for u, (j, t) in enumerate(units):
                    if j not in at_slab:
                        at_slab[j] = slab_in(2 + j % 2, 2 + j // 2)
                    w = at_slab[j]
                    if u >= 3:
                        unit_read(u - 3)
                    got = parts(j, t)
                    c0, c1 = got[0][0], got[-1][0] + got[-1][1]
                    for k in range(KD):
                        h = hT[:, k, t * P:(t + 1) * P] if t < NT else hcT[:, k, (t - NT) * P:(t - NT + 1) * P]
                        last = pe.matmul(bank[:, u % 3, c0:c1], h, w[:, k, c0:c1], start=(k == 0), stop=(k == KD - 1))
                    last.then_inc(m_proj, 1)
                    if u >= 1:
                        transpose_unit(u - 1)
                    for i in rows_after.get(u, ()):
                        ada_row_sum(i)
                transpose_unit(len(units) - 1)
                for u in range(len(units) - 3, len(units)):
                    unit_read(u)

                pe.wait_ge(m_arc, len(rest))

                pe.wait_ge(m_qkc, len(roped_units))

                def ret_scores(u):
                    h, m = divmod(u, NK)
                    if u >= 4:
                        pe.wait_ge(m_rs_p, u - 3)
                    lo = DK * (h % 2)
                    pe.matmul(bank[:, u % 4, :], kT[lo:lo + DK, h // 2, m * P:(m + 1) * P], qT[lo:lo + DK, h // 2, :],
                              start=True, stop=True).then_inc(m_rs_s, 1)

                def ret_values(u):
                    h, m = divmod(u, NK)
                    if m == 0 and h >= 2:
                        pe.wait_ge(m_on, h - 1)
                    pe.wait_ge(m_rs_p, u + 1)
                    for t in range(NT):
                        last = pe.matmul(bank[:, 6 + h % 2, t * DV:(t + 1) * DV], retp[:, u % 4, t * P:(t + 1) * P],
                                         v_tok[:, m, h * DV:(h + 1) * DV], start=(m == 0 and t == 0),
                                         stop=(m == NK - 1 and t == NT - 1), skip_group_check=True)
                    last.then_inc(m_rs_v, 1)

                for u in range(RU + 2):
                    if u < RU:
                        ret_scores(u)
                    if u >= 2:
                        ret_values(u - 2)

                def diff_scores(u):
                    h, t = divmod(u, NT)
                    if u == 0:
                        pe.wait_ge(m_rs_p, RU)
                    elif u >= 2:
                        pe.wait_ge(m_dc, u - 1)
                    for c in range(2):
                        for k0, k1 in PAIR_PIECES[c]:
                            if (c, k0) == (1, 0):
                                pe.wait_ge(m_db, u + 1)
                            last = pe.matmul(pair(u, c)[:, k0:k1], qT[c * DK:(c + 1) * DK, 2 + h, t * P:(t + 1) * P],
                                             kT[c * DK:(c + 1) * DK, 2 + h, k0:k1], start=True, stop=True)
                            if c == 0 and k0 > 0:
                                last.then_inc(m_db, 1)
                    last.then_inc(m_ds, 1)

                def diff_transpose(u):
                    pe.wait_ge(m_dp, u + 1)
                    for m in range(NK):
                        last = pe.transpose(pair(u, 0)[:, m * P:(m + 1) * P], diffp[:, m * P:(m + 1) * P], ident[:])
                    last.then_inc(m_dt, 1)

                def diff_values(u):
                    h, t = divmod(u, NT)
                    n = HEADS + h
                    if t == 0:
                        pe.wait_ge(m_on, n - 1)
                    pe.wait_ge(m_dc, u + 1)
                    for m in range(NK):
                        last = pe.matmul(bank[:, 6 + n % 2, t * DV:(t + 1) * DV], diffT[:, m, :],
                                         v_tok[:, m, n * DV:(n + 1) * DV], start=(m == 0), stop=(m == NK - 1))
                    if t == NT - 1:
                        last.then_inc(m_o, 1)

                for u in range(DU + 2):
                    if u < DU:
                        diff_scores(u)
                    if u >= 2:
                        diff_values(u - 2)
                    if 1 <= u <= DU:
                        diff_transpose(u - 1)

                for hh in range(2 * HEADS):
                    pe.wait_ge(m_on, 2 * HEADS)
                    if hh >= 4:
                        pe.wait_ge(m_mtc, hh - 3)
                    src = gate if hh < HEADS else dif_out
                    c0 = (hh % HEADS) * DV
                    for t in range(NT):
                        last = pe.transpose(bank[:, hh % 4, t * P:(t + 1) * P], src[:, t, c0:c0 + DV], ident[:])
                    last.then_inc(m_mt, 1)
                pe.wait_ge(m_mtc, 2 * HEADS)
                for hf in range(2):
                    w = slab_in(2 + hf, 5)
                    for t in range(NT):
                        i = hf * NT + t
                        if i >= 2:
                            pe.wait_ge(m_xr, i - 1)
                        for k in range(KD):
                            last = pe.matmul(bank[:, 4 + i % 2, :], mixT[:, k, t * P:(t + 1) * P], w[:, k, :],
                                             start=(k == 0), stop=(k == KD - 1))
                        last.then_inc(m_op, 1)
        stage_over()

        def moe(l):
            m_const = sem(f"moe{l}_tables_loaded")
            e_ = lambda s: sem(f"moe{l}_{s}")
            stage_memory(14000)
            xhat, at = carve(0, NT, D)
            hT, at = carve(at, KD, SEQ)
            scale_b, at = carve(at, D)
            shift_b, at = carve(at, D)
            normw_b = gate1_b[:]
            at_small = [at]
            score_rows = scale_b[:, 0:SEQ]
            at_place, at = carve(NT * D, NT, 3, P)
            xg, at = carve(0, 2, D)
            act_g, at = carve(at, DE)
            hid, at = carve(at, DE)
            y_sb, at = carve(at, 2, D)
            F32R = mybir.dt.float32r
            w_hi = stage_sb("w_hi", [P, 4, HALF_W], F32R)
            w_lo = stage_sb("w_lo", [P, 4, HALF_W], F32R)
            xT_hi = stage_sb("xT_hi", [P, KD, P], F32R)
            xT_lo = stage_sb("xT_lo", [P, KD, P], F32R)
            hT_hi = stage_sb("hT_hi", [P, KE, P], F32R)
            hT_lo = stage_sb("hT_lo", [P, KE, P], F32R)

            def small_tile(name, shape, dt=F32):
                v, at_small[0] = carve(at_small[0], *shape[1:])
                return v if dt == F32 else v.bitcast(dt)

            router_w = small_tile("router_w_sb", [P, KD, NE])
            router_b = small_tile("router_b_sb", [P, NE])
            krows = small_tile("krows", [P, 2, NE])
            token = small_tile("token", [P, NT], I32)
            before = small_tile("before", [P, P])
            score = small_tile("score", [P, NT, NE])
            biased = small_tile("biased", [P, NT, NE])
            g_hi = small_tile("g_hi", [P, NT * NG, 2])
            g_lo = small_tile("g_lo", [P, NT * NG, 2])
            g_t = small_tile("g_t", [P, 3, NT * NG])
            g_pad = small_tile("g_pad", [P, NT, 8])
            top8 = small_tile("top8", [P, NT, 8])
            top8i = small_tile("top8i", [P, NT, 8], U32)
            g_sel = small_tile("g_sel", [P, NT])
            in_grp = small_tile("in_grp", [P, NT, NE])
            masked = small_tile("masked", [P, NT, NE])
            e_sel = small_tile("e_sel", [P, 2, NT])
            pick = small_tile("pick", [P, 2, NT, NE])
            e_mask = small_tile("e_mask", [P, NT, NE])
            e_cum = small_tile("e_cum", [P, NT + 1, NE])
            r_tmp = small_tile("r_tmp", [P, 2, NT, NE])
            w_sum = small_tile("w_sum", [P, NT])
            row_tmp = small_tile("row_tmp", [P, 2, 2, NT])
            place = small_tile("place", [P, 2, NT])
            entry_of = small_tile("entry_of", [P, 2, NT], U32)
            places = small_tile("places", [P, P])
            token_f = small_tile("token_f", [P, NT])
            token_in = small_tile("token_in", [P, NT, 3])
            pos_in = small_tile("pos_in", [P, NT, 3])
            lists = small_tile("lists", [P, NE], I32)
            idx = small_tile("idx", [P, 3], U32)

            s_sq, s_rs, s_xh, s_xst, s_xt = e_("square_sum"), e_("rstd"), e_("xhat"), e_("xhat_stored"), e_("xhat_T")
            s_hta = e_("hT_copied")
            s_lr, s_lrc, s_lg = e_("logit_rows"), e_("score_rows"), e_("scores_transposed")
            s_mask, s_pos = e_("mask"), e_("places")
            s_rows, s_cnt = e_("rows_ready"), e_("count_ready")
            s_put, s_list = e_("lists_written"), e_("lists_loaded")
            s_hot, s_first = e_("place_rows_ready"), e_("first_lists_ready")
            s_sh, s_g2 = e_("shift_loaded"), e_("g2_loaded")
            s_mod = e_("adaln_rows_loaded")
            s_idx = e_("idx_ready")
            s_xg = [e_(f"rows_gathered{u}") for u in range(2)]
            s_gt, s_xhi, s_xlo = e_("rows_T"), e_("rows_T_high_parts"), e_("rows_T_low_parts")
            s_silu, s_hid, s_ht2 = e_("silu_done"), e_("hid_ready"), e_("hid_T")
            s_hhi, s_hlo, s_y = e_("hid_T_high_parts"), e_("hid_T_low_parts"), e_("y_ready")
            s_hi, s_lod, s_lop = e_("high_parts"), e_("low_parts_by_dve"), e_("low_parts_by_pool")
            s_used = e_("half_used")
            s_yst = [e_(f"y_stored{u}") for u in range(2)]
            s_dc, s_pc = e_("dve_chain"), e_("pool_chain")

            BY_POOL = (2, 4)
            LAST = NE - 1

            def last_step(e):
                return isinstance(e, int) and e == LAST

            def buf(u, p):
                return (2 * u + p) % 4

            def count(per_step, rank, e):
                return per_step * (e + 1) + rank + 1

            def pos_count(e, p):
                return count(6, p - 4 if last_step(e) else p, e)

            def low_count(e, p):
                mine = [q for q in range(4 if last_step(e) else 0, 6) if (q in BY_POOL) == (p in BY_POOL)]
                return (s_lop, count(2, mine.index(p), e)) if p in BY_POOL else (s_lod, count(4, mine.index(p), e))

            def raw(e, p):
                return p - 4 if last_step(e) else p

            def loaded(e, p):
                if last_step(e):
                    return 16 * (l + 1) * (NE + 1)
                return 16 * (l * (NE + 1, NE, NE - 1)[p // 2] + 1 + (e + 1 if p < 4 else e))

            with nc.Block() as block:

                @block.sync
                def _(sp):
                    sp.dma_start(scale_b, mod_row(l, SC2)).then_inc(s_mod, 16)
                    sp.dma_start(normw_b, a["norm_ffn_w"][l].partition_broadcast(P)).then_inc(s_mod, 16)
                    sp.dma_start(shift_b, mod_row(l, SH2)).then_inc(s_sh, 16)
                    sp.dma_start(router_w[:], a["router_w"].rearrange("(k p) e -> p k e", p=P)).then_inc(m_const, 16)
                    sp.dma_start(router_b[:], a["router_b"].partition_broadcast(P)).then_inc(m_const, 16)
                    sp.dma_start(krows[:], a["k_rows"].partition_broadcast(P)).then_inc(m_const, 16)
                    sp.dma_start(token[:], a["k_token"]).then_inc(m_const, 16)
                    sp.dma_start(before[:], a["k_before"]).then_inc(m_const, 16)
                    sp.dma_start(places[:], a["k_places"].partition_broadcast(P).rearrange("p a c -> p (a c)")
                                 ).then_inc(m_const, 16)
                    for t in range(NT):
                        sp.wait_ge(s_xh, t + 1)
                        sp.dma_start(xh_dram[t * P:(t + 1) * P, :], xhat[:, t, :]).then_inc(s_xst, 16)
                    sp.dma_start(gate2_b[:], mod_row(l, G2)).then_inc(s_g2, 16)

                    for p in range(4):
                        split_by, n = low_count(-1, p)
                        sp.wait_ge(split_by, n)
                        put_half(sp, l, 1, p)
                    with sp.Fori(0, NE - 2) as i:
                        for p in range(6):
                            split_by, n = low_count(i, p)
                            sp.wait_ge(split_by, n)
                            put_half(sp, l, sp.snap(i + 2) if p < 4 else sp.snap(i + 1), p)
                    for p in (4, 5):
                        split_by, n = low_count(NE - 2, p - 4)
                        sp.wait_ge(split_by, n)
                        put_half(sp, l, LAST, p, raw(LAST, p))

                @block.gpsimd
                def _(pool):
                    link = linker(pool, s_pc)
                    for t in range(NT):
                        pool.wait_ge(s_sq, t + 1)
                        link(nc.gpsimd.tensor_scalar(rstd[:, t:t + 1], stats[:, t:t + 1], 1.0 / D, EPS,
                                                     ALU.mult, ALU.add))
                        nc.gpsimd.tensor_tensor(rstd[:, t:t + 1], rstd[:, t:t + 1], minus_half[:, 0:1],
                                                ALU.pow).then_inc(s_rs, 1)

                    def fetch(u, c):
                        pool.indirect_dma_start(out=xg[:, u, :], out_offset=None, in_=xh_dram,
                                                in_offset=bass.IndirectOffsetOnAxis(ap=idx[:, c:c + 1], axis=0)
                                                ).then_inc(s_xg[u], 16)

                    def low(e, u, p):
                        pool.wait_ge(s_hi, pos_count(e, p))
                        nc.gpsimd.tensor_tensor(w_lo[:, buf(u, p), :], half(raw(e, p)), w_hi[:, buf(u, p), :].bitcast(F32),
                                                ALU.subtract).then_inc(s_lop, 2 if e == -1 else 1)

                    low(-1, 0, 2)
                    pool.wait_ge(s_lg, 1)
                    pool.wait_ge(s_xst, 16 * NT)
                    pool.wait_ge(s_idx, 1)
                    for u in range(2):
                        fetch(u, u)
                    pool.wait_ge(s_rows, 1)
                    for t in range(NT):
                        for c in range(2):
                            pool.indirect_dma_start(
                                out=list_dram, out_offset=bass.IndirectOffsetOnAxis(ap=entry_of[:, c, t:t + 1], axis=0),
                                in_=token[:, t:t + 1], in_offset=None).then_inc(s_put, 16)
                        if t == 1:
                            pool.wait_ge(s_gt, 1)
                            fetch(0, 2)
                    for e in range(LAST + 1):
                        for p in BY_POOL:
                            if e < LAST or p >= 4:
                                low(e, e % 2, p)
                        if e == 0:
                            pool.wait_ge(s_put, 16 * 2 * NT)
                            pool.dma_start(lists[:], list_dram[0:P * NE, :].rearrange("(j e) o -> j (e o)", e=NE)
                                           ).then_inc(s_list, 16)
                            pool.wait_ge(s_list, 16)
                        m = e + 3
                        if m < NE:
                            u = m % 2
                            pool.wait_ge(s_gt, m - 1)
                            pool.wait_ge(s_xg[u], 16 * (m // 2))
                            nc.gpsimd.tensor_copy(idx[:, u:u + 1], lists[:, m:m + 1]).then_inc(s_idx, 1)
                            pool.wait_ge(s_idx, m - 1)
                            fetch(u, u)

                @block.scalar
                def _(act):
                    for t in range(NT):
                        nc.scalar.activation(xhat[:, t, :], x[:, t, :], ACT.Square,
                                             accum_out=stats[:, t:t + 1]).then_inc(s_sq, 1)
                    for t in range(NT):
                        act.wait_ge(s_xt, t + 1)
                        nc.scalar.copy(hT[:, :, t * P:(t + 1) * P],
                                       bank[:, 2 * (t % 2):2 * (t % 2) + 2, :].rearrange("p b (k c) -> p (b k) c", c=P)
                                       ).then_inc(s_hta, 1)
                    act.wait_ge(s_lr, 1)
                    nc.scalar.activation(score_rows[0:NE, :], bank[0:NE, 5, :], ACT.Sigmoid).then_inc(s_lrc, 1)

                    def high(e, u, p):
                        act.wait_ge(half_load[raw(e, p)], loaded(e, p))
                        if not (isinstance(e, int) and e == -1):
                            act.wait_ge(s_used, pos_count(e, p) - 4)
                        nc.scalar.copy(w_hi[:, buf(u, p), :], half(raw(e, p))).then_inc(s_hi, 3 if isinstance(e, int) and (e, p) == (-1, 3) else 1)

                    def rows_high(n, up_used):
                        act.wait_ge(s_gt, n + 1)
                        if up_used is not None:
                            act.wait_ge(s_used, up_used)
                        nc.scalar.copy(xT_hi[:].rearrange("p k t -> p (k t)"),
                                       bank[:, 0:2, :].rearrange("p b c -> p (b c)")).then_inc(s_xhi, 1)

                    def silu(n, gate_used):
                        act.wait_ge(s_used, gate_used)
                        nc.scalar.activation(act_g, bank[:, 2, :], ACT.Silu).then_inc(s_silu, 1)

                    def hid_high(n):
                        act.wait_ge(s_ht2, n + 1)
                        nc.scalar.copy(hT_hi[:].rearrange("p k t -> p (k t)"), bank[:, 4, :]).then_inc(s_hhi, 1)

                    def store(e, u):
                        act.wait_ge(s_y, e + 1)
                        act.dma_start(y_dram[bass.ds(e * P, P), :], y_sb[:, u, :]).then_inc(s_yst[u], 16)

                    def step(e, u):
                        if not last_step(e):
                            high(e, u, 0)
                            rows_high(e + 1, pos_count(e, 3) - 6)
                            for p in (1, 2, 3):
                                high(e, u, p)
                        high(e, u, 4)
                        hid_high(e)
                        if not last_step(e):
                            act.wait_ge(s_hid, e + 1)
                            silu(e + 1, pos_count(e, 1))
                        if not (isinstance(e, int) and e == 0):
                            store(e - 1, 1 - u)
                        high(e, u, 5)

                    for p in range(4):
                        high(-1, 0, p)
                    rows_high(0, None)
                    silu(0, pos_count(-1, 1))
                    step(0, 0)
                    with act.Fori(0, (NE - 4) // 2) as i:
                        for v in range(2):
                            step(2 * i + 1 + v, 1 - v)
                    for e in range(NE - 3, NE):
                        step(e, e % 2)
                    store(NE - 1, 1)
                    for u in range(2):
                        act.wait_ge(s_yst[u], 16 * (NE // 2 + 1))

                @block.vector
                def _(dve):
                    link = linker(dve, s_dc)
                    nc.vector.memset(g_pad[:], -1e30)
                    dve.wait_ge(s_mod, 16 * 2)
                    link(nc.vector.scalar_tensor_tensor(scale_b, scale_b, 1.0, normw_b, ALU.add, ALU.mult))
                    for t in range(NT):
                        dve.wait_ge(s_rs, t + 1)
                        if t == 0:
                            dve.wait_ge(s_sh, 16)
                        link(nc.vector.scalar_tensor_tensor(xhat[:, t, :], x[:, t, :], rstd[:, t:t + 1], scale_b,
                                                            ALU.mult, ALU.mult))
                        nc.vector.tensor_tensor(xhat[:, t, :], xhat[:, t, :], shift_b, ALU.add).then_inc(s_xh, 1)
                    dve.wait_ge(m_const, 16 * 6)
                    V = nc.vector
                    dve.wait_ge(s_lg, 1)
                    link(V.tensor_copy(score[:].rearrange("p t e -> p (t e)"), bank[:, 4, 0:NT * NE]))
                    link(V.tensor_tensor(biased[:], score[:], router_b[:].unsqueeze(1).to_broadcast([P, NT, NE]), ALU.add))
                    v = biased[:].rearrange("p t (g a b) -> p (t g) a b", a=2, b=2)
                    V.tensor_tensor(g_hi[:], v[:, :, 0, :], v[:, :, 1, :], ALU.max)
                    link(V.tensor_tensor(g_lo[:], v[:, :, 0, :], v[:, :, 1, :], ALU.min))
                    V.tensor_tensor(g_t[:, 0, :], g_hi[:, :, 0], g_hi[:, :, 1], ALU.max)
                    V.tensor_tensor(g_t[:, 1, :], g_hi[:, :, 0], g_hi[:, :, 1], ALU.min)
                    link(V.tensor_tensor(g_t[:, 2, :], g_lo[:, :, 0], g_lo[:, :, 1], ALU.max))
                    link(V.tensor_tensor(g_t[:, 1, :], g_t[:, 1, :], g_t[:, 2, :], ALU.max))
                    link(V.tensor_tensor(g_pad[:, :, 0:NG], g_t[:, 0, :].rearrange("p (t g) -> p t g", g=NG),
                                         g_t[:, 1, :].rearrange("p (t g) -> p t g", g=NG), ALU.add))
                    for t in range(NT):
                        ins = V.max(top8[:, t, :], g_pad[:, t, :])
                    link(ins)
                    for t in range(NT):
                        ins = V.max_index(top8i[:, t, :], top8[:, t, :], g_pad[:, t, :])
                    link(ins)
                    link(V.tensor_copy(g_sel[:], top8i[:, :, 0]))
                    link(V.tensor_tensor(in_grp[:], krows[:, 1, :].unsqueeze(1).to_broadcast([P, NT, NE]),
                                         cols(g_sel[:], NE), ALU.is_equal))
                    V.tensor_scalar(r_tmp[:, 0], in_grp[:], -1.0, 1e30, ALU.add, ALU.mult)
                    link(V.tensor_tensor(masked[:], biased[:], in_grp[:], ALU.mult))
                    link(V.tensor_tensor(masked[:], masked[:], r_tmp[:, 0], ALU.add))
                    for t in range(NT):
                        ins = V.max(top8[:, t, :], masked[:, t, :])
                    link(ins)
                    for t in range(NT):
                        ins = V.max_index(top8i[:, t, :], top8[:, t, :], masked[:, t, :])
                    link(ins)
                    for c in range(2):
                        ins = V.tensor_copy(e_sel[:, c, :], top8i[:, :, c])
                    link(ins)
                    for c in range(2):
                        ins = V.tensor_tensor(pick[:, c], krows[:, 0, :].unsqueeze(1).to_broadcast([P, NT, NE]),
                                              cols(e_sel[:, c, :], NE), ALU.is_equal)
                    link(ins)
                    V.memset(e_cum[:, 0, :], 0.0)
                    link(V.tensor_tensor(e_mask[:], pick[:, 0], pick[:, 1], ALU.add))
                    link(V.tensor_copy(e_cum[:, 1, :], e_mask[:, 0, :]))
                    for t in range(1, NT):
                        ins = V.tensor_tensor(e_cum[:, t + 1, :], e_cum[:, t, :], e_mask[:, t, :], ALU.add)
                        if t < NT - 1:
                            link(ins)
                    ins.then_inc(s_mask, 1)
                    link(V.tensor_copy(token_f[:], token[:]))
                    dve.wait_ge(s_mask, 1)
                    V.tensor_tensor(token_in[:], e_mask[:, :, 0:3], cols(token_f[:], 3), ALU.mult)
                    for c in range(2):
                        ins = V.tensor_tensor(r_tmp[:, c], pick[:, c], score[:], ALU.mult)
                    link(ins)
                    link(V.tensor_reduce(weight[:], r_tmp[:], AX.X, ALU.add))
                    link(V.tensor_tensor(w_sum[:], weight[:, 0, :], weight[:, 1, :], ALU.add))
                    link(V.reciprocal(w_sum[:], w_sum[:]))
                    link(V.tensor_tensor(weight[:], weight[:], w_sum[:].unsqueeze(1).to_broadcast([P, 2, NT]), ALU.mult))
                    dve.wait_ge(s_pos, 1)
                    pos = bank[:, 5, 0:NT * NE].rearrange("p (t e) -> p t e", e=NE)
                    link(V.tensor_copy(pos_in[:], pos[:, :, 0:3]))
                    for t in range(NT):
                        for e in range(3):
                            ins = V.tensor_scalar(at_place[:, t, e, :], places[:], pos_in[:, t, e:e + 1],
                                                  token_in[:, t, e:e + 1], ALU.is_equal, ALU.mult)
                    link(ins)
                    link(V.tensor_tensor(at_place[:, 0:2], at_place[:, 0:2], at_place[:, 2:4], ALU.add))
                    V.tensor_tensor(at_place[:, 0], at_place[:, 0], at_place[:, 1], ALU.add).then_inc(s_hot, 1)
                    for c in range(2):
                        ins = V.tensor_tensor(r_tmp[:, c], pick[:, c], pos, ALU.mult)
                    link(ins)
                    link(V.tensor_reduce(place[:], r_tmp[:], AX.X, ALU.add))
                    V.scalar_tensor_tensor(row_tmp[:, 0], e_sel[:], float(P), place[:], ALU.mult, ALU.add)
                    link(V.tensor_scalar(row_tmp[:, 1], place[:], float(P), None, ALU.is_ge))
                    for b in range(2, SEQ // P):
                        link(V.scalar_tensor_tensor(row_tmp[:, 1], place[:], float(b * P), row_tmp[:, 1],
                                                    ALU.is_ge, ALU.add))
                    V.scalar_tensor_tensor(row_of[:], row_tmp[:, 1], float((NE - 1) * P), row_tmp[:, 0],
                                           ALU.mult, ALU.add)
                    V.scalar_tensor_tensor(entry_of[:], place[:], float(NE), e_sel[:], ALU.mult, ALU.add).then_inc(s_rows, 1)
                    V.tensor_reduce(max_count[:], bank[:, 5, NT * NE:(NT + 1) * NE], AX.X, ALU.max).then_inc(s_cnt, 1)

                    dve.wait_ge(s_first, 1)
                    V.tensor_copy(idx[:], bank[:, 4, NT * NE:NT * NE + 3]).then_inc(s_idx, 1)

                    for u in range(2):
                        V.memset(idx_zero[:, u:u + 1], 0.0).then_inc(s_yst[u], 16)

                    def low(e, u, p):
                        dve.wait_ge(s_hi, pos_count(e, p))
                        V.tensor_tensor(w_lo[:, buf(u, p), :], half(raw(e, p)), w_hi[:, buf(u, p), :].bitcast(F32),
                                        ALU.subtract).then_inc(s_lod, 2 if isinstance(e, int) and (e, p) == (-1, 3) else 1)

                    def rows_low(n):
                        dve.wait_ge(s_xhi, n + 1)
                        V.tensor_tensor(xT_lo[:].rearrange("p k t -> p (k t)"), bank[:, 0:2, :].rearrange("p b c -> p (b c)"),
                                        xT_hi[:].rearrange("p k t -> p (k t)").bitcast(F32), ALU.subtract).then_inc(s_xlo, 1)

                    def hidden(n, up_used):
                        dve.wait_ge(s_used, up_used)
                        dve.wait_ge(s_silu, n + 1)
                        V.tensor_tensor(hid, act_g, bank[:, 3, :], ALU.mult).then_inc(s_hid, 1)

                    def hid_low(n):
                        dve.wait_ge(s_hhi, n + 1)
                        V.tensor_tensor(hT_lo[:].rearrange("p k t -> p (k t)"), bank[:, 4, :],
                                        hT_hi[:].rearrange("p k t -> p (k t)").bitcast(F32), ALU.subtract).then_inc(s_hlo, 1)

                    def rows_out(n, u, down_used, stored):
                        dve.wait_ge(s_used, down_used)
                        dve.wait_ge(s_yst[u], stored)
                        V.tensor_tensor(y_sb[:, u, :], bank[:, 6:8, :].rearrange("p b c -> p (b c)"), gate2_b[:],
                                        ALU.mult).then_inc(s_y, 1)

                    def step(e, u, stored):
                        if not last_step(e):
                            low(e, u, 0)
                            rows_low(e + 1)
                        hidden(e, 6 * (e + 1) - 2)
                        if not last_step(e):
                            low(e, u, 1)
                            low(e, u, 3)
                        if stored is not None:
                            rows_out(e - 1, 1 - u, 6 * (e + 1), stored)
                        hid_low(e)
                        low(e, u, 5)

                    for p in (0, 1, 3):
                        low(-1, 0, p)
                    rows_low(0)
                    dve.wait_ge(s_g2, 16)
                    step(0, 0, None)
                    with dve.Fori(0, (NE - 4) // 2) as i:
                        for v in range(2):
                            step(2 * i + 1 + v, 1 - v, 16 * i + 16)
                    for e in range(NE - 3, NE):
                        step(e, e % 2, 16 * ((e - 1) // 2) + 16)
                    rows_out(NE - 1, 1, pos_count(LAST, 5), 16 * (LAST // 2) + 16)

                @block.tensor
                def _(pe):
                    def tile_T(t):
                        pe.wait_ge(s_xh, t + 1)
                        if t >= 2:
                            pe.wait_ge(s_hta, t - 1)
                        for k in range(KD):
                            last = pe.transpose(bank[:, 2 * (t % 2) + k // 4, (k % 4) * P:(k % 4 + 1) * P],
                                                xhat[:, t, k * P:(k + 1) * P], ident[:])
                        last.then_inc(s_xt, 1)

                    def logits(t):
                        pe.wait_ge(s_hta, t + 1)
                        for k in range(KD):
                            last = pe.matmul(bank[0:NE, 5, t * P:(t + 1) * P], router_w[:, k, :], hT[:, k, t * P:(t + 1) * P],
                                             start=(k == 0), stop=(k == KD - 1))
                        return last

                    tile_T(0)
                    pe.wait_ge(m_const, 16 * 6)
                    for t in range(NT):
                        if t + 1 < NT:
                            tile_T(t + 1)
                        last = logits(t)
                    last.then_inc(s_lr, 1)
                    pe.wait_ge(s_lrc, 1)
                    for t in range(NT):
                        last = pe.transpose(bank[:, 4, t * NE:(t + 1) * NE], score_rows[0:NE, t * P:(t + 1) * P],
                                            ident[0:NE, 0:NE])
                    last.then_inc(s_lg, 1)
                    pe.wait_ge(s_mask, 1)
                    pe.matmul(bank[:, 5, 0:(NT + 1) * NE], ones[:], e_cum[:].rearrange("p t e -> p (t e)"),
                              start=True, stop=False, skip_group_check=True)
                    pe.matmul(bank[:, 5, 0:NT * NE], before[:], e_mask[:].rearrange("p t e -> p (t e)"),
                              start=False, stop=True, skip_group_check=True).then_inc(s_pos, 1)
                    pe.wait_ge(s_hot, 1)
                    for e in range(3):
                        last = pe.matmul(bank[:, 4, NT * NE + e:NT * NE + e + 1], at_place[:, 0, e, :], ones[:, 0:1],
                                         start=True, stop=True)
                    last.then_inc(s_first, 1)
                    pe.wait_ge(s_cnt, 1)

                    def rows_T(u, gathered):
                        pe.wait_ge(s_xg[u], gathered)
                        for k in range(KD):
                            last = pe.transpose(bank[:, k // 4, (k % 4) * P:(k % 4 + 1) * P],
                                                xg[:, u, k * P:(k + 1) * P], ident[:])
                        last.then_inc(s_gt, 1)

                    def parts(e, p):
                        split_by, n = low_count(e, p)
                        pe.wait_ge(split_by, n)

                    def product(b, e, u, p):
                        parts(e, p)
                        hi = w_hi[:, buf(u, p), :].rearrange("p (k c) -> p k c", c=DE)
                        lo = w_lo[:, buf(u, p), :].rearrange("p (k c) -> p k c", c=DE)
                        n = KD // 2
                        for k in range(n):
                            kk = (p % 2) * n + k
                            for i, (xs, ws) in enumerate(((xT_hi, hi), (xT_hi, lo), (xT_lo, hi))):
                                last = pe.matmul(bank[:, b, :], xs[:, kk, :], ws[:, k, :], start=(kk == 0 and i == 0),
                                                 stop=(kk == KD - 1 and i == 2))
                        last.then_inc(s_used, 3 if isinstance(e, int) and (e, p) == (-1, 3) else 1)

                    def down(e, u, p):
                        parts(e, p)
                        hi = w_hi[:, buf(u, p), :].rearrange("p (k c) -> p k c", c=D)
                        lo = w_lo[:, buf(u, p), :].rearrange("p (k c) -> p k c", c=D)
                        n = KE // 2
                        for hf in range(2):
                            at = slice(hf * HALF, (hf + 1) * HALF)
                            for k in range(n):
                                kk = (p % 2) * n + k
                                for i, (xs, ws) in enumerate(((hT_hi, hi), (hT_hi, lo), (hT_lo, hi))):
                                    last = pe.matmul(bank[:, 6 + hf, :], xs[:, kk, :], ws[:, k, at],
                                                     start=(kk == 0 and i == 0), stop=(kk == KE - 1 and i == 2))
                        last.then_inc(s_used, 1)

                    def step(e, u, gathered):
                        if not last_step(e):
                            pe.wait_ge(s_xlo, e + 2)
                            pe.wait_ge(s_silu, e + 1)
                            product(2, e, u, 0)
                            product(2, e, u, 1)
                        pe.wait_ge(s_hid, e + 1)
                        for k in range(KE):
                            last = pe.transpose(bank[:, 4, k * P:(k + 1) * P], hid[:, k * P:(k + 1) * P], ident[:])
                        last.then_inc(s_ht2, 1)
                        if gathered is not None:
                            rows_T(u, gathered)
                        if not last_step(e):
                            product(3, e, u, 2)
                            product(3, e, u, 3)
                        pe.wait_ge(s_hlo, e + 1)
                        if not (isinstance(e, int) and e == 0):
                            pe.wait_ge(s_y, e)
                        down(e, u, 4)
                        down(e, u, 5)

                    rows_T(0, 16)
                    pe.wait_ge(s_xlo, 1)
                    product(2, -1, 0, 0)
                    product(2, -1, 0, 1)
                    rows_T(1, 16)
                    product(3, -1, 0, 2)
                    product(3, -1, 0, 3)
                    step(0, 0, 32)
                    with pe.Fori(0, (NE - 4) // 2) as i:
                        for v in range(2):
                            step(2 * i + 1 + v, 1 - v, 16 * i + 16 * (2 + v))
                    for e in range(NE - 3, NE):
                        step(e, e % 2, 16 * ((e + 2) // 2 + 1) if e + 2 < NE else None)

            stage_over()

            o_ = lambda s: sem(f"over{l}_{s}")
            v_ld, v_idx, v_xg = o_("weights"), o_("list"), o_("rows")
            v_t, v_tc, v_g, v_u, v_s, v_h = o_("rows_T"), o_("rows_T_copied"), o_("gate"), o_("up"), o_("silu"), o_("hid")
            v_h2, v_h2c, v_d, v_y, v_st = o_("hid_T"), o_("hid_T_copied"), o_("down"), o_("y"), o_("stored")
            v_small = o_("small_op")
            MORE = SEQ // P - 1
            wg, wu, wd = a["moe_w_gate"][l], a["moe_w_up"][l], a["moe_w_down"][l]
            xg, at = carve(0, 1, D)
            xgT, at = carve(at, 1, KD, P)
            act_g, at = carve(at, DE)
            hid, at = carve(at, DE)
            hidT, at = carve(at, KE, P)
            y_sb, at = carve(at, 1, D)
            assert at <= 2 * KD * SEQ + 2 * D
            lists4 = list_dram.rearrange("(b j e) o -> b j (e o)", j=P, e=NE)

            def blocks(eng):
                with eng.Fori(0, MORE) as b:
                    with eng.Fori(0, NE) as e:
                        yield e, b + 1, b * NE + e

            with nc.Block() as block:

                @block.sync
                def _(sp):
                    most = sp.value_load(max_count[0:1, 0:1])
                    with sp.If(most > P):
                        for e, b, n in blocks(sp):
                            sp.wait_ge(v_d, n + 1)
                            put(sp, wg, e, 0, KD).then_inc(v_ld, 16)
                            put(sp, wu, e, 1, KD).then_inc(v_ld, 16)
                            put(sp, wd, e, 2, KE).then_inc(v_ld, 16)

                @block.gpsimd
                def _(pool):
                    most = pool.value_load(max_count[0:1, 0:1])
                    with pool.If(most > P):
                        for e, b, n in blocks(pool):
                            pool.dma_start(idx[:, 0:1].bitcast(I32), lists4[bass.ds(b, 1), :, bass.ds(e, 1)]
                                           .rearrange("b j e -> (b j) e")).then_inc(v_idx, 16)
                            pool.wait_ge(v_idx, 16 * n + 16)
                            nc.gpsimd.tensor_tensor(idx_zero[:], idx_zero[:], idx_zero[:], ALU.add).then_inc(v_small, 1)
                            pool.indirect_dma_start(out=xg[:, 0, :], out_offset=None, in_=xh_dram,
                                                    in_offset=bass.IndirectOffsetOnAxis(ap=idx[:, 0:1], axis=0)
                                                    ).then_inc(v_xg, 16)
                            pool.wait_ge(v_t, n + 1)
                            pool.wait_ge(v_small, n + 1)

                @block.scalar
                def _(act):
                    most = act.value_load(max_count[0:1, 0:1])
                    with act.If(most > P):
                        for e, b, n in blocks(act):
                            act.wait_ge(v_t, n + 1)
                            nc.scalar.copy(xgT[:, 0].rearrange("p k t -> p (k t)"),
                                           bank[:, 0:2, :].rearrange("p b c -> p (b c)")).then_inc(v_tc, 1)
                            act.wait_ge(v_g, n + 1)
                            nc.scalar.activation(act_g, bank[:, 2, :], ACT.Silu).then_inc(v_s, 1)
                            act.wait_ge(v_y, n + 1)
                            act.dma_start(y_dram[bass.ds((b * NE + e) * P, P), :], y_sb[:, 0, :]).then_inc(v_st, 16)
                            act.wait_ge(v_st, 16 * n + 16)

                @block.vector
                def _(dve):
                    most = dve.value_load(max_count[0:1, 0:1])
                    with dve.If(most > P):
                        for e, b, n in blocks(dve):
                            dve.wait_ge(v_u, n + 1)
                            dve.wait_ge(v_s, n + 1)
                            nc.vector.tensor_tensor(hid, act_g, bank[:, 3, :], ALU.mult).then_inc(v_h, 1)
                            dve.wait_ge(v_h2, n + 1)
                            nc.vector.tensor_copy(hidT.rearrange("p k t -> p (k t)"), bank[:, 4, :]).then_inc(v_h2c, 1)
                            dve.wait_ge(v_d, n + 2)
                            nc.vector.tensor_tensor(y_sb[:, 0, :], bank[:, 6:8, :].rearrange("p b c -> p (b c)"),
                                                    gate2_b[:], ALU.mult).then_inc(v_y, 1)
                            dve.wait_ge(v_st, 16 * n + 16)

                @block.tensor
                def _(pe):
                    most = pe.value_load(max_count[0:1, 0:1])
                    with pe.If(most > P):
                        pe.transpose(bank[:, 5, 0:P], ident[:], ident[:]).then_inc(v_d, 1)
                        for e, b, n in blocks(pe):
                            pe.wait_ge(v_xg, 16 * n + 16)
                            for k in range(KD):
                                last = pe.transpose(bank[:, k // 4, (k % 4) * P:(k % 4 + 1) * P],
                                                    xg[:, 0, k * P:(k + 1) * P], ident[:])
                            last.then_inc(v_t, 1)
                            pe.wait_ge(v_tc, n + 1)
                            pe.wait_ge(v_ld, 48 * n + 48)
                            for q, done in ((0, v_g), (1, v_u)):
                                w = slot(q).rearrange("p (k c) -> p k c", k=KD)
                                for k in range(KD):
                                    last = pe.matmul(bank[:, 2 + q, :], xgT[:, 0, k, :], w[:, k, :],
                                                     start=(k == 0), stop=(k == KD - 1))
                                last.then_inc(done, 1)
                            pe.wait_ge(v_h, n + 1)
                            for k in range(KE):
                                last = pe.transpose(bank[:, 4, k * P:(k + 1) * P], hid[:, k * P:(k + 1) * P], ident[:])
                            last.then_inc(v_h2, 1)
                            pe.wait_ge(v_h2c, n + 1)
                            w = slot(2).rearrange("p (k c) -> p k c", k=KE)
                            for hf in range(2):
                                for k in range(KE):
                                    last = pe.matmul(bank[:, 6 + hf, :], hidT[:, k, :], w[:, k, hf * HALF:(hf + 1) * HALF],
                                                     start=(k == 0), stop=(k == KE - 1))
                            last.then_inc(v_d, 1)
                            pe.wait_ge(v_st, 16 * n + 16)

            stage_over()

        class Combine:

            def __init__(self, name, rows):
                self.rows = rows
                self.loaded = [[sem(f"{name}_rows{c}_{t}") for t in range(NT)] for c in range(2)]
                self.chain = sem(f"{name}_first_added")
                self.done = sem(f"{name}_x_ready")

            def fetch(self, pool):
                def tiles(written):
                    for t in range(NT):
                        for c in range(2):
                            pool.indirect_dma_start(
                                out=self.rows[:, c, t, :], out_offset=None, in_=y_dram[0:written, :],
                                in_offset=bass.IndirectOffsetOnAxis(ap=row_of[:, c, t:t + 1], axis=0)
                            ).then_inc(self.loaded[c][t], 16)

                most = pool.value_load(max_count[0:1, 0:1])
                with pool.If(most > P):
                    tiles(LIST_N)
                with pool.Else():
                    tiles(NE * P)

            def add(self, dve, t):
                for c, done in ((0, self.chain), (1, self.done)):
                    dve.wait_ge(self.loaded[c][t], 16)
                    nc.vector.scalar_tensor_tensor(x[:, t, :], self.rows[:, c, t, :], weight[:, c, t:t + 1],
                                                   x[:, t, :], ALU.mult, ALU.add).then_inc(done, 1)
                    dve.wait_ge(done, t + 1)

        def rstd_of(pool, t, squared, chain, ready):
            pool.wait_ge(squared, t + 1)
            nc.gpsimd.tensor_scalar(rstd[:, t:t + 1], stats[:, t:t + 1], 1.0 / D, EPS, ALU.mult, ALU.add).then_inc(chain, 1)
            pool.wait_ge(chain, t + 1)
            nc.gpsimd.tensor_tensor(rstd[:, t:t + 1], rstd[:, t:t + 1], minus_half[:, 0:1], ALU.pow).then_inc(ready, 1)

        moe(0)

        stage_memory(18432 + 2 * NT * D)
        rows, at = carve(0, 2, NT, D)
        combine = Combine("combine0", rows)
        bands, at = carve(at, len(WINDOWS), 5, P)
        pool_w, at = carve(at, len(WINDOWS), 2, 2 * P)
        xhat, at = carve(at, NT, D)
        pooledT, at = carve(at, KD, SEQ)
        scale1_b, at = carve(at, D)
        shift1_b, at = carve(at, D)
        normw1_b, at = carve(at, D)
        upd2, at = carve(at, HALF)
        p_ = lambda s: sem(f"pool_{s}")
        p_ld, p_sq, p_rs, p_xh, p_pl, p_plc = p_("tables"), p_("square_sum"), p_("rstd"), p_("xhat"), p_("pooled"), p_("pooled_copied")
        p_mod, p_ps, p_nw, p_mx, p_xr, p_dc, p_pc = (p_("adaln_rows_loaded"), p_("scale_loaded"), p_("norm_weight_used"),
                                                     p_("mixed"), p_("x_updated"), p_("dve_chain"), p_("pool_chain"))

        p_g1 = p_("g1_loaded")

        with nc.Block() as block:

            @block.sync
            def _(sp):
                for dst, src in ((scale1_b, mod_row(1, SC1)), (normw1_b, a["norm_mix_w"][1].partition_broadcast(P)),
                                 (shift1_b, mod_row(1, SH1))):
                    sp.dma_start(dst, src).then_inc(p_mod, 16)
                sp.wait_ge(combine.done, NT - 1)
                sp.dma_start(bands.rearrange("p g b c -> p (g b c)"), a["k_bands"]).then_inc(p_ld, 16)
                sp.dma_start(pool_w.rearrange("p g k c -> p (g k) c"),
                             a["pool_w"][0].rearrange("g (k p) c -> p (g k) c", p=P)).then_inc(p_ld, 16)
                sp.dma_start(gate1_b[:], mod_row(1, G1)).then_inc(p_g1, 16)
                sp.wait_ge(p_nw, 1)
                sp.dma_start(normw1_b, a["pool_scale"][0].partition_broadcast(P)).then_inc(p_ps, 16)
                sp.wait_ge(combine.done, NT)
                for r in range(6):
                    put_half(sp, 1, 0, r)

            @block.scalar
            def _(act):
                for t in range(NT):
                    act.wait_ge(combine.done, t + 1)
                    nc.scalar.activation(xhat[:, t, :], x[:, t, :], ACT.Square,
                                         accum_out=stats[:, t:t + 1]).then_inc(p_sq, 1)
                for k in range(KD):
                    act.wait_ge(p_pl, k + 1)
                    nc.scalar.copy(pooledT[:, k, :], bank[:, k % 4, :]).then_inc(p_plc, 1)

            @block.gpsimd
            def _(pool):
                combine.fetch(pool)
                for t in range(NT):
                    rstd_of(pool, t, p_sq, p_pc, p_rs)

            @block.vector
            def _(dve):
                link = linker(dve, p_dc)
                combine.add(dve, 0)
                combine.add(dve, 1)
                dve.wait_ge(p_mod, 16 * 3)
                nc.vector.scalar_tensor_tensor(scale1_b, scale1_b, 1.0, normw1_b, ALU.add, ALU.mult).then_inc(p_nw, 1)
                dve.wait_ge(p_nw, 1)
                for t in range(NT):
                    if t + 2 < NT:
                        combine.add(dve, t + 2)
                    dve.wait_ge(p_rs, t + 1)
                    link(nc.vector.scalar_tensor_tensor(xhat[:, t, :], x[:, t, :], rstd[:, t:t + 1], scale1_b,
                                                        ALU.mult, ALU.mult))
                    nc.vector.tensor_tensor(xhat[:, t, :], xhat[:, t, :], shift1_b, ALU.add).then_inc(p_xh, 1)
                dve.wait_ge(p_ps, 16)
                dve.wait_ge(p_g1, 16)
                link(nc.vector.tensor_tensor(gate1_b[:], gate1_b[:], normw1_b, ALU.mult))
                for n in range(2 * NT):
                    hf, t = n // NT, n % NT
                    dve.wait_ge(p_mx, n + 1)
                    if n >= 1:
                        dve.wait_ge(p_xr, n)
                    link(nc.vector.tensor_tensor(upd2, bank[:, 4 + n % 2, :], gate1_b[:, hf * HALF:(hf + 1) * HALF],
                                                 ALU.mult))
                    xs = x[:, t, hf * HALF:(hf + 1) * HALF]
                    nc.vector.tensor_tensor(xs, xs, upd2, ALU.add).then_inc(p_xr, 1)

            @block.tensor
            def _(pe):
                pe.wait_ge(p_ld, 32)
                pe.wait_ge(p_xh, NT)
                for k in range(KD):
                    if k >= 4:
                        pe.wait_ge(p_plc, k - 3)
                    g = k // 2
                    for t in range(NT):
                        near = [(t2, b) for t2, b in ((t - 1, 3), (t, 0 if t == 0 else 2 if t == NT - 1 else 1), (t + 1, 4))
                                if 0 <= t2 < NT]
                        for n, (t2, b) in enumerate(near):
                            last = pe.matmul(bank[:, k % 4, t * P:(t + 1) * P], xhat[:, t2, k * P:(k + 1) * P],
                                             bands[:, g, b, :], start=(n == 0), stop=(n == len(near) - 1))
                    last.then_inc(p_pl, 1)
                pe.wait_ge(p_plc, KD)
                for n in range(2 * NT):
                    hf, t = n // NT, n % NT
                    if n >= 2:
                        pe.wait_ge(p_xr, n - 1)
                    for g in (2 * hf, 2 * hf + 1):
                        c0 = (g % 2) * 2 * P
                        for k in range(2):
                            last = pe.matmul(bank[:, 4 + n % 2, c0:c0 + 2 * P], pooledT[:, 2 * g + k, t * P:(t + 1) * P],
                                             pool_w[:, g, k, :], start=(k == 0), stop=(k == 1))
                    last.then_inc(p_mx, 1)

        stage_over()

        moe(1)

        f_ld, f_sq, f_rs, f_o, f_st, f_pc = (sem(f"fin_{s}") for s in
                                             ("weight", "square_sum", "rstd", "out", "stored", "pool_chain"))
        stage_memory((3 * NT + 1) * D)
        rows, at = carve(0, 2, NT, D)
        combine = Combine("combine1", rows)
        fin_w, at = carve(at, D)
        fin, at = carve(at, NT, D)

        with nc.Block() as block:

            @block.sync
            def _(sp):
                sp.dma_start(fin_w, a["final_norm_w"].partition_broadcast(P)).then_inc(f_ld, 16)
                for t in range(NT):
                    sp.wait_ge(f_o, t + 1)
                    sp.dma_start(out[0, t * P:(t + 1) * P, :], fin[:, t, :]).then_inc(f_st, 16)
                sp.wait_ge(f_st, 16 * NT)

            @block.scalar
            def _(act):
                for t in range(NT):
                    act.wait_ge(combine.done, t + 1)
                    nc.scalar.activation(fin[:, t, :], x[:, t, :], ACT.Square, accum_out=stats[:, t:t + 1]).then_inc(f_sq, 1)

            @block.gpsimd
            def _(pool):
                combine.fetch(pool)
                for t in range(NT):
                    rstd_of(pool, t, f_sq, f_pc, f_rs)

            @block.vector
            def _(dve):
                combine.add(dve, 0)
                combine.add(dve, 1)
                dve.wait_ge(f_ld, 16)
                for t in range(NT):
                    if t + 2 < NT:
                        combine.add(dve, t + 2)
                    dve.wait_ge(f_rs, t + 1)
                    nc.vector.scalar_tensor_tensor(fin[:, t, :], x[:, t, :], rstd[:, t:t + 1], fin_w,
                                                   ALU.mult, ALU.mult).then_inc(f_o, 1)


_INS = ['x', 'c', 'ctx', 'c_ctx', 'ada_w', 'ada_b', 'norm_mix_w', 'norm_ffn_w', 'w_in', 'w_out', 'ret_log_decay',
        'diff_lambda', 'diff_subln_w', 'pool_w', 'pool_scale', 'router_w', 'router_b', 'moe_w_gate', 'moe_w_up',
        'moe_w_down', 'final_norm_w']


def kernel(**inputs):
    import concourse.bacc as bacc
    from concourse.bass_utils import run_bass_kernel_spmd

    nc = bacc.Bacc("TRN2", target_bir_lowering=False, num_devices=1)
    arrays = {f"in_{n}": np.ascontiguousarray(inputs[n]) for n in _INS}
    arrays.update(constants())
    aps = {}
    for name, arr in arrays.items():
        ap = nc.dram_tensor(name, arr.shape, mybir.dt.from_np(arr.dtype), kind="ExternalInput").ap()
        aps[name.removeprefix("in_")] = ap
    out = nc.dram_tensor("out_0", (1, SEQ, D), F32, kind="ExternalOutput").ap()
    build_program(nc, aps, out)
    r = run_bass_kernel_spmd(nc, [arrays], core_ids=[0])
    return r.results[0]["out_0"]
```
